# Optimizing a Trainium2 kernel written in Bass

```python
import jax, jax.numpy as jnp
from jax import lax
import numpy as np

D_MODEL = 1024
BATCH = 1
SEQ = 1024
DEPTH = 1
DEC_BATCH = 1
DEC_SEQ = 64
PAST_LEN = 2048

CHUNK = 64
D_RNN = 1024
N_RNN_HEADS = 16
RNN_BLOCK = D_RNN // N_RNN_HEADS
CONV_W = 4
LRU_C = 8.0
N_HEADS = 16
HEAD_DIM = 64
D_ATTN = N_HEADS * HEAD_DIM
Q_BLOCK = 128
N_GROUPS = 4
EXPERTS_PER_GROUP = 8
N_EXPERTS = N_GROUPS * EXPERTS_PER_GROUP
TOP_K = 2
D_EXPERT = 512
MOE_BLOCK = 128
EPS = 1e-6
NEG_INF = -1e30
D_IN = 2 * D_RNN + 3 * D_ATTN + N_HEADS + 2 * D_MODEL
SPLIT_POINTS = (D_RNN, 2 * D_RNN, 2 * D_RNN + D_ATTN, 2 * D_RNN + 2 * D_ATTN, 2 * D_RNN + 3 * D_ATTN,
                2 * D_RNN + 3 * D_ATTN + N_HEADS, 2 * D_RNN + 3 * D_ATTN + N_HEADS + D_MODEL)

kernel_name = "hawk_fox_hier_moe_stream_step"

def _rmsnorm(x, g):
    xf = x.astype(jnp.float32)
    y = xf * lax.rsqrt(jnp.mean(xf * xf, axis=-1, keepdims=True) + EPS)
    return (y * g.astype(jnp.float32)).astype(x.dtype)

def _lru_combine(left, right):
    a1, b1 = left
    a2, b2 = right
    return a1 * a2, a2 * b1 + b2

def _rg_lru(u, h0, w_a, b_a, w_x, b_x, lru_lambda):
    B, T, _ = u.shape
    ub = u.reshape(B, T, N_RNN_HEADS, RNN_BLOCK)
    r = jax.nn.sigmoid((jnp.einsum('bthi,hij->bthj', ub, w_a).reshape(B, T, D_RNN) + b_a).astype(jnp.float32))
    i = jax.nn.sigmoid((jnp.einsum('bthi,hij->bthj', ub, w_x).reshape(B, T, D_RNN) + b_x).astype(jnp.float32))
    log_a = -LRU_C * r * jax.nn.softplus(-lru_lambda.astype(jnp.float32))
    a = jnp.exp(log_a)
    b = jnp.sqrt(-jnp.expm1(2.0 * log_a)) * (i * u.astype(jnp.float32))
    b = b.at[:, 0].add(a[:, 0] * h0.astype(jnp.float32))
    _, h = lax.associative_scan(_lru_combine, (a, b), axis=1)
    return h, h[:, -1]

def _fox_attention(q, k, v, c_q, c_k, past):
    B, T, H, DH = q.shape
    qb = min(Q_BLOCK, T)
    nb = T // qb
    k_pos = jnp.arange(k.shape[1])
    ckT = c_k.transpose(0, 2, 1)[:, :, None, :]
    scale = HEAD_DIM ** -0.5

    def block(args):
        q_blk, cq_blk, q_pos = args
        s = jnp.einsum('bqhd,bkhd->bhqk', q_blk, k).astype(jnp.float32) * scale
        s = s + cq_blk.astype(jnp.float32).transpose(0, 2, 1)[..., None] - ckT
        s = jnp.where(k_pos[None, :] <= q_pos[:, None], s, NEG_INF)
        p = jax.nn.softmax(s, axis=-1)
        return jnp.einsum('bhqk,bkhd->bqhd', p.astype(v.dtype), v)

    q_r = q.reshape(B, nb, qb, H, DH).transpose(1, 0, 2, 3, 4)
    cq_r = c_q.reshape(B, nb, qb, H).transpose(1, 0, 2, 3)
    pos_r = (past + jnp.arange(T)).reshape(nb, qb)
    out = lax.map(block, (q_r, cq_r, pos_r))
    return out.transpose(1, 0, 2, 3, 4).reshape(B, T, H, DH)

def _grouped_experts(xf, eid, gate, w_gate_e, w_up_e, w_down_e):
    N, D = xf.shape
    A = N * TOP_K
    flat_e = eid.reshape(-1)
    order = jnp.argsort(flat_e)
    se = flat_e[order]
    tok = (order // TOP_K).astype(jnp.int32)
    counts = jnp.bincount(flat_e, length=N_EXPERTS)
    padded = (counts + MOE_BLOCK - 1) // MOE_BLOCK * MOE_BLOCK
    start = jnp.cumsum(counts) - counts
    pend = jnp.cumsum(padded)
    pstart = pend - padded
    dest = pstart[se] + jnp.arange(A) - start[se]
    nblk = (A + MOE_BLOCK - 1) // MOE_BLOCK + N_EXPERTS
    R = nblk * MOE_BLOCK
    row_tok = jnp.full((R,), N, jnp.int32).at[dest].set(tok)
    row_gate = jnp.zeros((R,), xf.dtype).at[dest].set(gate.reshape(-1)[order].astype(xf.dtype))
    blk_e = jnp.minimum(jnp.searchsorted(pend, jnp.arange(nblk) * MOE_BLOCK, side='right'), N_EXPERTS - 1)
    xpad = jnp.concatenate([xf, jnp.zeros((1, D), xf.dtype)], axis=0)
    xb = xpad[row_tok].reshape(nblk, MOE_BLOCK, D)

    def expert_block(args):
        xblk, e = args
        hdn = jax.nn.silu(xblk @ w_gate_e[e]) * (xblk @ w_up_e[e])
        return hdn @ w_down_e[e]

    yb = lax.map(expert_block, (xb, blk_e)).reshape(R, D)
    y = jnp.zeros((N + 1, D), xf.dtype).at[row_tok].add(yb * row_gate[:, None])
    return y[:N]

def _hier_moe(h, w_route_group, b_route_group, w_route_expert, b_route_expert, w_gate_e, w_up_e, w_down_e):
    B, T, D = h.shape
    xf = h.reshape(-1, D)
    N = xf.shape[0]
    g_logits = (xf @ w_route_group).astype(jnp.float32) + b_route_group.astype(jnp.float32)
    g_prob = jax.nn.softmax(g_logits, axis=-1)
    grp = jnp.argmax(g_logits, axis=-1)
    g_w = jnp.take_along_axis(g_prob, grp[:, None], axis=1)
    e_logits = ((xf @ w_route_expert).astype(jnp.float32) + b_route_expert.astype(jnp.float32)).reshape(N, N_GROUPS, EXPERTS_PER_GROUP)
    e_in = jnp.take_along_axis(e_logits, grp[:, None, None], axis=1)[:, 0]
    top_v, top_i = lax.top_k(e_in, TOP_K)
    gate = jax.nn.softmax(top_v, axis=-1) * g_w
    eid = grp[:, None] * EXPERTS_PER_GROUP + top_i
    return _grouped_experts(xf, eid, gate, w_gate_e, w_up_e, w_down_e).reshape(B, T, D)

def _layer(x, conv_hist, h0, k_hist, v_hist, lf_hist,
           norm1_g, w_in, conv_w, conv_b, w_a, b_a, w_x, b_x, lru_lambda, b_f, q_norm_g, k_norm_g,
           w_rnn_out, w_attn_out, w_o, norm2_g, w_route_group, b_route_group, w_route_expert, b_route_expert,
           w_gate_e, w_up_e, w_down_e):
    B, T, _ = x.shape
    P = k_hist.shape[1]
    xn = _rmsnorm(x, norm1_g)
    z = xn @ w_in
    u_x, u_g, q, k, v, f_logit, g_rnn, g_attn = jnp.split(z, SPLIT_POINTS, axis=-1)
    conv_in = jnp.concatenate([conv_hist.astype(u_x.dtype), u_x], axis=1)
    conv_out = lax.conv_general_dilated(conv_in, conv_w.astype(u_x.dtype)[:, None, :], (1,), 'VALID',
                                        dimension_numbers=('NWC', 'WIO', 'NWC'),
                                        feature_group_count=D_RNN) + conv_b
    new_conv = conv_in[:, -(CONV_W - 1):]
    h_seq, h_last = _rg_lru(conv_out, h0, w_a, b_a, w_x, b_x, lru_lambda)
    rnn_y = (jax.nn.gelu(u_g) * h_seq.astype(x.dtype)) @ w_rnn_out
    q = _rmsnorm(q.reshape(B, T, N_HEADS, HEAD_DIM), q_norm_g)
    k = _rmsnorm(k.reshape(B, T, N_HEADS, HEAD_DIM), k_norm_g)
    v = v.reshape(B, T, N_HEADS, HEAD_DIM)
    lf = jax.nn.log_sigmoid(f_logit.astype(jnp.float32) + b_f.astype(jnp.float32))
    k_all = jnp.concatenate([k_hist.astype(k.dtype), k], axis=1)
    v_all = jnp.concatenate([v_hist.astype(v.dtype), v], axis=1)
    c_all = jnp.cumsum(jnp.concatenate([lf_hist.astype(jnp.float32), lf], axis=1), axis=1)
    attn = _fox_attention(q, k_all, v_all, c_all[:, P:], c_all, P)
    attn_y = attn.reshape(B, T, D_ATTN) @ w_attn_out
    x = x + (jax.nn.sigmoid(g_rnn) * rnn_y + jax.nn.sigmoid(g_attn) * attn_y) @ w_o
    x = x + _hier_moe(_rmsnorm(x, norm2_g), w_route_group, b_route_group, w_route_expert, b_route_expert,
                      w_gate_e, w_up_e, w_down_e)
    return x, new_conv, h_last, k, v, lf

def setup_inputs(seed: int = 0) -> dict:
    key = jax.random.key(seed)
    ks = jax.random.split(key, 32)
    n = jax.random.normal
    L = DEPTH
    u = jax.random.uniform(ks[14], (L, D_RNN), minval=0.9, maxval=0.999)
    a0 = u ** (1.0 / LRU_C)
    return {
        "x_prompt": n(ks[0], (BATCH, SEQ, D_MODEL), jnp.float32),
        "x_sample": n(ks[1], (DEC_BATCH, DEC_SEQ, D_MODEL), jnp.float32),
        "cache_k": n(ks[2], (L, DEC_BATCH, PAST_LEN, N_HEADS, HEAD_DIM), jnp.float32),
        "cache_v": n(ks[3], (L, DEC_BATCH, PAST_LEN, N_HEADS, HEAD_DIM), jnp.float32),
        "cache_logf": jax.nn.log_sigmoid(3.0 + n(ks[4], (L, DEC_BATCH, PAST_LEN, N_HEADS), jnp.float32)),
        "state_conv": n(ks[5], (L, DEC_BATCH, CONV_W - 1, D_RNN), jnp.float32),
        "state_rglru": 0.5 * n(ks[6], (L, DEC_BATCH, D_RNN), jnp.float32),
        "norm1_g": 1.0 + 0.05 * n(ks[7], (L, D_MODEL), jnp.float32),
        "w_in": n(ks[8], (L, D_MODEL, D_IN), jnp.float32) * D_MODEL ** -0.5,
        "conv_w": n(ks[9], (L, CONV_W, D_RNN), jnp.float32) * CONV_W ** -0.5,
        "conv_b": 0.01 * n(ks[10], (L, D_RNN), jnp.float32),
        "w_a": n(ks[11], (L, N_RNN_HEADS, RNN_BLOCK, RNN_BLOCK), jnp.float32) * RNN_BLOCK ** -0.5,
        "b_a": 0.01 * n(ks[12], (L, D_RNN), jnp.float32),
        "w_x": n(ks[13], (L, N_RNN_HEADS, RNN_BLOCK, RNN_BLOCK), jnp.float32) * RNN_BLOCK ** -0.5,
        "b_x": 0.01 * n(ks[15], (L, D_RNN), jnp.float32),
        "lru_lambda": jnp.log(a0) - jnp.log1p(-a0),
        "b_f": 3.0 + 0.1 * n(ks[16], (L, N_HEADS), jnp.float32),
        "q_norm_g": 1.0 + 0.05 * n(ks[17], (L, HEAD_DIM), jnp.float32),
        "k_norm_g": 1.0 + 0.05 * n(ks[18], (L, HEAD_DIM), jnp.float32),
        "w_rnn_out": n(ks[19], (L, D_RNN, D_MODEL), jnp.float32) * D_RNN ** -0.5,
        "w_attn_out": n(ks[20], (L, D_ATTN, D_MODEL), jnp.float32) * D_ATTN ** -0.5,
        "w_o": n(ks[21], (L, D_MODEL, D_MODEL), jnp.float32) * D_MODEL ** -0.5,
        "norm2_g": 1.0 + 0.05 * n(ks[22], (L, D_MODEL), jnp.float32),
        "w_route_group": n(ks[23], (L, D_MODEL, N_GROUPS), jnp.float32) * D_MODEL ** -0.5,
        "b_route_group": 0.01 * n(ks[24], (L, N_GROUPS), jnp.float32),
        "w_route_expert": n(ks[25], (L, D_MODEL, N_EXPERTS), jnp.float32) * D_MODEL ** -0.5,
        "b_route_expert": 0.01 * n(ks[26], (L, N_EXPERTS), jnp.float32),
        "w_gate_e": n(ks[27], (L, N_EXPERTS, D_MODEL, D_EXPERT), jnp.float32) * D_MODEL ** -0.5,
        "w_up_e": n(ks[28], (L, N_EXPERTS, D_MODEL, D_EXPERT), jnp.float32) * D_MODEL ** -0.5,
        "w_down_e": n(ks[29], (L, N_EXPERTS, D_EXPERT, D_MODEL), jnp.float32) * D_EXPERT ** -0.5,
    }

def reference(x_prompt, x_sample, cache_k, cache_v, cache_logf, state_conv, state_rglru,
              norm1_g, w_in, conv_w, conv_b, w_a, b_a, w_x, b_x, lru_lambda, b_f, q_norm_g, k_norm_g,
              w_rnn_out, w_attn_out, w_o, norm2_g, w_route_group, b_route_group, w_route_expert, b_route_expert,
              w_gate_e, w_up_e, w_down_e):
    Bp = x_prompt.shape[0]
    yp, ys = x_prompt, x_sample
    kp, vp, lfp, cvp, hp = [], [], [], [], []
    kss, vss, lfs, cvs, hs = [], [], [], [], []
    for l in range(DEPTH):
        lp = (norm1_g[l], w_in[l], conv_w[l], conv_b[l], w_a[l], b_a[l], w_x[l], b_x[l], lru_lambda[l], b_f[l],
              q_norm_g[l], k_norm_g[l], w_rnn_out[l], w_attn_out[l], w_o[l], norm2_g[l],
              w_route_group[l], b_route_group[l], w_route_expert[l], b_route_expert[l],
              w_gate_e[l], w_up_e[l], w_down_e[l])
        yp, c1, h1, k1, v1, f1 = _layer(
            yp, jnp.zeros((Bp, CONV_W - 1, D_RNN), yp.dtype), jnp.zeros((Bp, D_RNN), jnp.float32),
            jnp.zeros((Bp, 0, N_HEADS, HEAD_DIM), yp.dtype), jnp.zeros((Bp, 0, N_HEADS, HEAD_DIM), yp.dtype),
            jnp.zeros((Bp, 0, N_HEADS), jnp.float32), *lp)
        ys, c2, h2, k2, v2, f2 = _layer(
            ys, state_conv[l], state_rglru[l], cache_k[l], cache_v[l], cache_logf[l], *lp)
        kp.append(k1); vp.append(v1); lfp.append(f1); cvp.append(c1); hp.append(h1)
        kss.append(k2); vss.append(v2); lfs.append(f2); cvs.append(c2); hs.append(h2)
    return (yp, ys,
            jnp.stack(kp), jnp.stack(vp), jnp.stack(lfp), jnp.stack(cvp), jnp.stack(hp),
            jnp.stack(kss), jnp.stack(vss), jnp.stack(lfs), jnp.stack(cvs), jnp.stack(hs))


_drawn_inputs = setup_inputs


def setup_inputs(seed=0):
    import zlib

    import numpy as np

    out = dict(_drawn_inputs(seed))
    spreads = {}
    factors = {'cache_logf': 3.377,
     'b_a': 8.0,
     'b_x': 8.0,
     'q_norm_g': 2.942,
     'b_route_expert': 4.407,
     'b_route_group': 7.313}
    for name, (base, spread) in spreads.items():
        noise = np.random.default_rng([zlib.crc32(name.encode()), seed]).standard_normal(out[name].shape)
        drawn = base * np.exp(spread * noise) if base else spread * noise
        out[name] = __import__('jax').numpy.asarray(drawn.astype(out[name].dtype))
    for name, factor in factors.items():
        out[name] = (out[name] * factor).astype(out[name].dtype)
    return out
```

```python
import concourse.bass as bass
from concourse import mybir
from contextlib import ExitStack

F32 = mybir.dt.float32
BF16 = mybir.dt.bfloat16
I32 = mybir.dt.int32
U32 = mybir.dt.uint32
ALU = mybir.AluOpType
ACT = mybir.ActivationFunctionType
X_AXIS = mybir.AxisListType.X

P = 128
D = 1024
KT = D // P
T_PROMPT, T_SAMPLE, PAST = 1024, 64, 2048
T_ALL = T_PROMPT + T_SAMPLE
PT = T_PROMPT // P
NT = PT + 1
T_PAD = NT * P
CHUNKS = ((0, 512), (512, 512), (1024, T_SAMPLE))
BANK = 512
CONV_W = 4
LRU_C = 8.0
HEADS, HD = 16, 64
PAIRS = HEADS // 2
PAST_TILES = PAST // P
KV_SAMPLE = PAST + T_SAMPLE
GROUPS, PER_GROUP = 4, 8
EXPERTS = GROUPS * PER_GROUP
F_EXP = 512
FT = F_EXP // P
TOP_K = 2
CAP = 96
OVER_MAX = TOP_K * T_ALL // CAP
BLOCKS_MAX = (EXPERTS + OVER_MAX + 1) // 2 * 2
SLOTS = BLOCKS_MAX * CAP
EPS = 1e-6
NEG = -1e30

COL_X, COL_G, COL_Q, COL_K, COL_V = 0, D, 2 * D, 3 * D, 4 * D
COL_F = 5 * D
COL_GATE_RNN = COL_F + HEADS
COL_GATE_ATTN = COL_GATE_RNN + D

V_NORM1, V_CONV, V_CONVB, V_BA, V_BX, V_LAM, V_H0, V_HIST = 0, 1, 5, 6, 7, 8, 9, 10
N_VEC = 13


class Chain:

    def __init__(self, eng, sem, base=0):
        self.eng, self.sem, self.base, self.n = eng, sem, base, 0

    def __call__(self, ins, tell=None):
        self.n += 1
        ins.then_inc(self.sem, 1)
        self.eng.wait_ge(self.sem, self.base + self.n)
        if tell is not None:
            self.eng.sem_inc(tell, 1)

    def ended(self, per_pass):
        assert self.n == per_pass, self.n


def alone(eng, g):
    eng.sem_inc(g.apart, 1)


def row(ap, n=1):
    return ap.rearrange("(o n) -> o n", o=n)


def log1p_steps(nc, chain, out, z, s, s2, acc):
    v = nc.vector
    chain(v.tensor_scalar(s, z, 2.0, None, ALU.add))
    chain(v.reciprocal(s2, s))
    chain(v.tensor_tensor(s, z, s2, ALU.mult))
    chain(v.tensor_tensor(s2, s, s, ALU.mult))
    chain(v.tensor_scalar(acc, s2, 1.0 / 17.0, 1.0 / 15.0, ALU.mult, ALU.add))
    for k in (13, 11, 9, 7, 5, 3, 1):
        chain(v.tensor_tensor(acc, acc, s2, ALU.mult))
        chain(v.tensor_scalar(acc, acc, 1.0 / k, None, ALU.add))
    chain(v.scalar_tensor_tensor(out, acc, 2.0, s, ALU.mult, ALU.mult))


LOG1P_STEPS = 5 + 14 + 1


def normalize(nc, g):
    with ExitStack() as ctx:
        sb = lambda name, shape, dt=F32: ctx.enter_context(nc.sbuf_tensor(name, shape, dt))
        vec_rows = sb("vec_rows", [P, P])
        xt = sb("xt", [P, 3, D])
        x_last = sb("x_last", [P, D])
        square = sb("square", [P, D])
        ss = sb("ss", [P, NT])
        rstd = sb("rstd", [P, NT])
        zrows = sb("zrows", [P, D])
        turned = ctx.enter_context(nc.psum_tensor("turned", [P, 2, KT, P], F32))
        vec_ps = ctx.enter_context(nc.psum_tensor("vec_ps", [P, P], F32))
        sem = g.sem
        vec_loaded, const_ready, zrows_ready = sem("vec_loaded"), sem("const_ready"), sem("zrows_ready")
        x_loaded = [sem(f"x_loaded{b}") for b in range(4)]
        sq_ready, mean_ready, rstd_ready, xs_ready = sem("sq_ready"), sem("mean_ready"), sem("rstd_ready"), sem("xs_ready")
        xT_ready, xT_taken, vec_ready, chain_v, chain_p = sem("xT_ready"), sem("xT_taken"), sem("vec_ready"), sem("n_chain_v"), sem("n_chain_p")
        chain_a = sem("n_chain_a")
        tile = lambda t: x_last[:, :] if t == PT else xt[:, t % 3, :]
        load_of = lambda t: (x_loaded[3], 16) if t == PT else (x_loaded[t % 3], 16 * (t // 3 + 1))

        with nc.Block() as block:
            @block.sync
            def _(sp):
                vectors = [g.norm1_g[0], *(g.conv_w[0, j] for j in range(CONV_W)), g.conv_b[0], g.b_a[0], g.b_x[0],
                           g.lru_lambda[0], g.state_rglru[0, 0], *(g.state_conv[0, 0, j] for j in range(CONV_W - 1))]
                sp.dma_start(xt[:, 0, :], g.x_prompt[0, 0:P, :]).then_inc(x_loaded[0], 16)
                for n, vec in enumerate(vectors):
                    sp.dma_start(vec_rows[n * KT:(n + 1) * KT, :], row(vec, KT)).then_inc(vec_loaded, 16)
                for t in range(1, NT):
                    if t == PT:
                        sp.dma_start(x_last[0:T_SAMPLE, :], g.x_sample[0]).then_inc(x_loaded[3], 16)
                        continue
                    if t >= 3:
                        sp.wait_ge(xT_ready, t - 2)
                    sp.dma_start(xt[:, t % 3, :], g.x_prompt[0, t * P:(t + 1) * P, :]).then_inc(x_loaded[t % 3], 16)

            @block.scalar
            def _(act):
                act.wait_ge(zrows_ready, 1)
                for r in range(0, SLOTS, P):
                    n = min(P, SLOTS - r)
                    act.dma_start(g.slot_x[r:r + n, :], zrows[0:n, :]).then_inc(g.slots_cleared, 16)
                for r in range(EXPERTS * CAP, SLOTS, P):
                    n = min(P, SLOTS - r)
                    act.dma_start(g.slot_y[r:r + n, :], zrows[0:n, :]).then_inc(g.slots_cleared, 16)
                for t in range(NT):
                    act.wait_ge(*load_of(t))
                    if t == PT:
                        act.wait_ge(const_ready, 1)
                    if t:
                        act.wait_ge(chain_a, t)
                    nc.scalar.activation(square[:, :], tile(t), ACT.Square, accum_out=ss[:, t:t + 1]).then_inc(chain_a, 1)
                    act.wait_ge(chain_a, t + 1)
                    act.sem_inc(sq_ready, 1)
                    act.wait_ge(mean_ready, t + 1)
                    nc.scalar.activation(rstd[:, t:t + 1], rstd[:, t:t + 1], ACT.Sqrt).then_inc(rstd_ready, 1)
                act.wait_ge(g.slots_cleared, 16 * (-(-SLOTS // P) - (EXPERTS * CAP - SLOTS) // P))

            @block.gpsimd
            def _(pool):
                chain = Chain(pool, chain_p)
                chain(nc.gpsimd.memset(zrows[:, :], 0.0), zrows_ready)
                chain(nc.gpsimd.memset(g.ident[:, :], 0.0))
                chain(nc.gpsimd.affine_select(out=g.ident[:, :], in_=g.ident[:, :], compare_op=ALU.not_equal, fill=1.0,
                                              base=0, pattern=[[-1, P]], channel_multiplier=1))
                chain(nc.gpsimd.memset(x_last[T_SAMPLE:P, :], 0.0), const_ready)
                chain(nc.gpsimd.tensor_copy(g.ident_bf[:, :], g.ident[:, :]))
                chain(nc.gpsimd.memset(g.ones[:, :], 1.0))
                chain(nc.gpsimd.affine_select(out=g.before[:, :], in_=g.ones[:, :], compare_op=ALU.is_gt, fill=0.0,
                                              base=0, pattern=[[1, P]], channel_multiplier=-1))
                chain(nc.gpsimd.memset(g.causal_f[:, :], 0.0))
                chain(nc.gpsimd.affine_select(out=g.causal_f[:, :], in_=g.causal_f[:, :], compare_op=ALU.is_ge, fill=NEG,
                                              base=0, pattern=[[-1, P]], channel_multiplier=1))
                chain(nc.gpsimd.tensor_copy(g.causal[:, :], g.causal_f[:, :]))
                chain(nc.gpsimd.tensor_copy(g.causal_s[0:64, :], g.causal_f[0:64, 0:64]))
                chain(nc.gpsimd.tensor_copy(g.causal_s[64:P, :], g.causal_f[64:P, 64:P]))

            @block.tensor
            def _(pe):
                pe.wait_ge(const_ready, 1)
                pe.wait_ge(vec_loaded, 16 * N_VEC)
                nc.tensor.transpose(vec_ps[:, 0:N_VEC * KT], vec_rows[0:N_VEC * KT, :],
                                    g.ident[0:N_VEC * KT, 0:N_VEC * KT]).then_inc(vec_ready, 1)
                for t in range(NT):
                    pe.wait_ge(xs_ready, t + 1)
                    if t >= 2:
                        pe.wait_ge(xT_taken, t - 1)
                    for k in range(KT):
                        last = nc.tensor.transpose(turned[:, t % 2, k, :], tile(t)[:, k * P:(k + 1) * P], g.ident[:, :])
                    last.then_inc(xT_ready, 1)

            @block.vector
            def _(dve):
                chain = Chain(dve, chain_v)
                dve.wait_ge(vec_ready, 1)
                chain(nc.vector.tensor_copy(g.chan[:, :], vec_ps[:, 0:N_VEC * KT]))

                def take(t):
                    dve.wait_ge(xT_ready, t + 1)
                    gain = g.chan[:, V_NORM1 * KT:(V_NORM1 + 1) * KT].unsqueeze(2).to_broadcast([P, KT, P])
                    chain(nc.vector.tensor_tensor(g.xnT[:, :, t * P:(t + 1) * P], turned[:, t % 2, :, :], gain, ALU.mult),
                          xT_taken)

                for t in range(NT):
                    dve.wait_ge(sq_ready, t + 1)
                    chain(nc.vector.tensor_scalar(rstd[:, t:t + 1], ss[:, t:t + 1], 1.0 / D, EPS, ALU.mult, ALU.add))
                    chain(nc.vector.reciprocal(rstd[:, t:t + 1], rstd[:, t:t + 1]), mean_ready)
                    if t:
                        take(t - 1)
                    dve.wait_ge(rstd_ready, t + 1)
                    chain(nc.vector.tensor_scalar(tile(t), tile(t), rstd[:, t:t + 1], None, ALU.mult), xs_ready)
                take(NT - 1)


def forget_gates(nc, g):
    with ExitStack() as ctx:
        sb = lambda name, shape, dt=F32: ctx.enter_context(nc.sbuf_tensor(name, shape, dt))
        w_f = sb("w_f", [P, KT, HEADS])
        past_lf = sb("past_lf", [P, PAST_TILES, HEADS])
        b_f = sb("b_f_all", [P, HEADS])
        z, e, lf, s, s2, acc = (sb(n, [P, NT * HEADS + KT]) for n in ("fz", "fe", "flf", "fs", "fs2", "facc"))
        ones_row = sb("ones_row", [HEADS, PAST])
        neg_c_p, neg_c_s = sb("neg_c_p", [HEADS, T_PROMPT]), sb("neg_c_s", [HEADS, KV_SAMPLE])
        f_ps = ctx.enter_context(nc.psum_tensor("f_ps", [P, BANK], F32))
        new_ps = ctx.enter_context(nc.psum_tensor("new_ps", [HEADS, 3 * BANK], F32))
        past_ps = ctx.enter_context(nc.psum_tensor("past_ps", [HEADS, PAST], F32))
        sem = g.sem
        f_loaded, f_ready, e_asked, e_ready = sem("f_loaded"), sem("f_ready"), sem("e_asked"), sem("e_ready")
        past_ready, lf_ready, new_ready, chain_v, lf_stored = sem("past_ready"), sem("lf_ready"), sem("new_ready"), sem("f_chain_v"), sem("lf_stored")
        sums_ready = sem("sums_ready")
        F = NT * HEADS

        with nc.Block() as block:
            @block.sync
            def _(sp):
                sp.dma_start(w_f[:, :, :], g.w_in_k[:, :, COL_F:COL_F + HEADS]).then_inc(f_loaded, 16)
                sp.dma_start(past_lf[:, :, :], g.cache_logf[0, 0].rearrange("(t p) h -> p t h", p=P)).then_inc(f_loaded, 16)
                sp.dma_start(b_f[:, :], row(g.b_f[0]).to_broadcast([P, HEADS])).then_inc(f_loaded, 16)
                sp.wait_ge(lf_ready, 1)
                sp.dma_start(g.out_lf_p[0, 0].rearrange("(t p) h -> p t h", p=P),
                             lf[:, 0:PT * HEADS].rearrange("p (t h) -> p t h", h=HEADS)).then_inc(lf_stored, 16)
                sp.dma_start(g.out_lf_s[0, 0], lf[0:T_SAMPLE, PT * HEADS:F]).then_inc(lf_stored, 16)
                sp.wait_ge(sums_ready, 1)
                sp.dma_start(g.neg_c_new[:, 0:T_PROMPT], neg_c_p[:, :]).then_inc(lf_stored, 16)
                sp.dma_start(g.neg_c_new[:, T_PROMPT:T_ALL], neg_c_s[:, PAST:KV_SAMPLE]).then_inc(lf_stored, 16)
                sp.dma_start(g.neg_c_past[:, :], neg_c_s[:, 0:PAST]).then_inc(lf_stored, 16)
                sp.wait_ge(lf_stored, 80)

            @block.tensor
            def _(pe):
                pe.wait_ge(f_loaded, 48)
                for t in range(NT):
                    for k in range(KT):
                        last = nc.tensor.matmul(f_ps[:, t * HEADS:(t + 1) * HEADS], g.xnT[:, k, t * P:(t + 1) * P],
                                                w_f[:, k, :], start=(k == 0), stop=(k == KT - 1))
                last.then_inc(f_ready, 1)
                for t in range(PAST_TILES):
                    last = nc.tensor.transpose(past_ps[:, t * P:(t + 1) * P], past_lf[:, t, :], g.ident[:, :])
                last.then_inc(past_ready, 1)
                pe.wait_ge(lf_ready, 1)
                for t in range(NT):
                    last = nc.tensor.transpose(new_ps[:, t * P:(t + 1) * P], lf[:, t * HEADS:(t + 1) * HEADS], g.ident[:, :])
                last.then_inc(new_ready, 1)

            @block.scalar
            def _(act):
                act.wait_ge(e_asked, 1)
                nc.scalar.activation(e[:, :], e[:, :], ACT.Exp).then_inc(e_ready, 1)

            @block.vector
            def _(dve):
                v, chain = nc.vector, Chain(dve, chain_v)
                dve.wait_ge(f_loaded, 48)
                chain(v.memset(ones_row[:, :], 1.0))
                chain(v.memset(g.qkT[HD:HD + 1, 0:2, :], 1.0))
                dve.wait_ge(f_ready, 1)
                chain(v.tensor_tensor(z[:, 0:F].rearrange("p (t h) -> p t h", h=HEADS),
                                      f_ps[:, 0:F].rearrange("p (t h) -> p t h", h=HEADS),
                                      b_f[:, :].unsqueeze(1).to_broadcast([P, NT, HEADS]), ALU.add))
                chain(v.tensor_copy(z[:, F:F + KT], g.chan[:, V_LAM * KT:(V_LAM + 1) * KT]))
                chain(v.tensor_scalar(e[:, :], z[:, :], -1.0, None, ALU.mult))
                chain(v.tensor_tensor(e[:, :], e[:, :], z[:, :], ALU.min), e_asked)
                dve.wait_ge(e_ready, 1)
                log1p_steps(nc, chain, lf[:, :], e[:, :], s[:, :], s2[:, :], acc[:, :])
                chain(v.tensor_scalar(z[:, :], z[:, :], 0.0, None, ALU.min))
                chain(v.tensor_tensor(lf[:, :], z[:, :], lf[:, :], ALU.subtract), lf_ready)
                chain(v.tensor_scalar(g.decay[:, :], lf[:, F:F + KT], LRU_C, None, ALU.mult))
                dve.wait_ge(past_ready, 1)
                chain(v.tensor_tensor_scan(neg_c_s[:, 0:PAST], ones_row[:, :], past_ps[:, :], 0.0, ALU.mult, ALU.subtract))
                dve.wait_ge(new_ready, 1)
                chain(v.tensor_tensor_scan(neg_c_p[:, :], ones_row[:, 0:T_PROMPT], new_ps[:, 0:T_PROMPT], 0.0,
                                           ALU.mult, ALU.subtract))
                chain(v.tensor_tensor_scan(neg_c_s[:, PAST:KV_SAMPLE], ones_row[:, 0:T_SAMPLE],
                                           new_ps[:, T_PROMPT:T_ALL], neg_c_s[:, PAST - 1:PAST], ALU.mult, ALU.subtract),
                      sums_ready)


def recurrent(nc, g, yT):
    GATE_UNITS = 2 * len(CHUNKS)
    with ExitStack() as ctx:
        sb = lambda name, shape, dt=F32: ctx.enter_context(nc.sbuf_tensor(name, shape, dt))
        w_x = [sb(f"r_wx{u}", [P, KT, P]) for u in range(2)]
        w_g = [sb(f"r_wg{u}", [P, KT, P]) for u in range(2)]
        bd = [sb(f"r_bd{u}", [P, 2, P]) for u in range(2)]
        H = CONV_W - 1
        conv_in = sb("conv_in", [P, H + T_PROMPT + H + T_SAMPLE])
        u_sb, r_sb, i_sb, a_sb, th_sb, v_sb, gel, h_sb = (sb(n, [P, T_ALL]) for n in
                                                         ("u_sb", "r_sb", "i_sb", "a_sb", "th_sb", "v_sb", "gel", "h_sb"))
        tails = sb("tails", [P, 2 * H + 2, KT])
        tails_T = sb("tails_T", [P, P])
        ux_ps = ctx.enter_context(nc.psum_tensor("ux_ps", [P, 3 * BANK], F32))
        ug_ps = ctx.enter_context(nc.psum_tensor("ug_ps", [P, 3 * BANK], F32))
        gate_ps = ctx.enter_context(nc.psum_tensor("gate_ps", [P, 2, BANK], F32))
        sem = g.sem
        w_loaded = [sem(f"rw_loaded{u}") for u in range(2)]
        bd_cleared, w_used = sem("bd_cleared"), sem("rw_used")
        ux_ready, ug_ready, conv_ready = sem("ux_ready"), sem("ug_ready"), sem("conv_in_ready")
        u_ready, gate_ready, gate_taken = sem("u_ready"), sem("gate_ready"), sem("gate_taken")
        ri_ready, at_ready, gel_ready, var_ready, std_ready, step_done = (sem("ri_ready"), sem("at_ready"), sem("gel_ready"),
                                                                          sem("var_ready"), sem("std_ready"), sem("step_done"))
        chain_v, chain_a, chain_e = sem("r_chain_v"), sem("r_chain_a"), sem("r_chain_e")
        tails_ready, tails_turned, tails_kept, tails_stored = sem("tails_ready"), sem("tails_turned"), sem("tails_kept"), sem("tails_stored")
        LOADS = 6 * 16
        V_STEPS, A_STEPS = 19, 13

        with nc.Block() as block:
            @block.sync
            def _(sp):
                sp.wait_ge(bd_cleared, 1)
                with sp.Fori(0, KT // 2) as i:
                    for u in range(2):
                        c = i * 2 + u
                        sp.wait_ge(w_used, c + 1)
                        sp.dma_start(w_x[u][:, :, :], g.w_in_k[:, :, bass.ds(c * P + COL_X, P)]).then_inc(w_loaded[u], 16)
                        for n, w in enumerate((g.w_a, g.w_x)):
                            for h in range(2):
                                sp.dma_start(bd[u][h * 64:(h + 1) * 64, n, h * 64:(h + 1) * 64],
                                             w[0, bass.ds(c * 2 + h, 1)].rearrange("o i j -> (o i) j")).then_inc(w_loaded[u], 16)
                        sp.dma_start(w_g[u][:, :, :], g.w_in_k[:, :, bass.ds(c * P + COL_G, P)]).then_inc(w_loaded[u], 16)
                sp.wait_ge(tails_kept, 1)
                last_rows = lambda out: out[0, 0].rearrange("j (c p) -> (j c) p", p=P)
                one_row = lambda out: out[0, 0:1].rearrange("o (c p) -> (o c) p", p=P)
                sp.dma_start(last_rows(g.out_conv_p), tails_T[0:H * KT, :]).then_inc(tails_stored, 16)
                sp.dma_start(last_rows(g.out_conv_s), tails_T[H * KT:2 * H * KT, :]).then_inc(tails_stored, 16)
                sp.dma_start(one_row(g.out_h_p), tails_T[2 * H * KT:(2 * H + 1) * KT, :]).then_inc(tails_stored, 16)
                sp.dma_start(one_row(g.out_h_s), tails_T[(2 * H + 1) * KT:(2 * H + 2) * KT, :]).then_inc(tails_stored, 16)
                sp.wait_ge(tails_stored, 64)

            @block.tensor
            def _(pe):
                pe.sem_inc(w_used, 2)
                with pe.Fori(0, KT // 2) as i:
                    for u in range(2):
                        c = i * 2 + u
                        pe.wait_ge(w_loaded[u], i * LOADS + LOADS)
                        pe.wait_ge(conv_ready, c)
                        for c0, n in CHUNKS:
                            for k in range(KT):
                                last = nc.tensor.matmul(ux_ps[:, c0:c0 + n], w_x[u][:, k, :], g.xnT[:, k, c0:c0 + n],
                                                        start=(k == 0), stop=(k == KT - 1))
                        last.then_inc(ux_ready, 1)
                        pe.wait_ge(gel_ready, c)
                        for c0, n in CHUNKS:
                            for k in range(KT):
                                last = nc.tensor.matmul(ug_ps[:, c0:c0 + n], w_g[u][:, k, :], g.xnT[:, k, c0:c0 + n],
                                                        start=(k == 0), stop=(k == KT - 1))
                        last.then_inc(ug_ready, 1)
                        pe.wait_ge(u_ready, c + 1)
                        for m in range(GATE_UNITS):
                            c0, n = CHUNKS[m % 3]
                            if m >= 2:
                                pe.wait_ge(gate_taken, c * GATE_UNITS + m - 1)
                            else:
                                pe.wait_ge(gate_taken, c * GATE_UNITS)
                            last = nc.tensor.matmul(gate_ps[:, m % 2, 0:n], bd[u][:, m // 3, :], u_sb[:, c0:c0 + n],
                                                    start=True, stop=True)
                            last.then_inc(gate_ready, 1)
                        pe.wait_ge(gate_ready, c * GATE_UNITS + GATE_UNITS)
                        pe.sem_inc(w_used, 1)
                pe.wait_ge(tails_ready, 1)
                nc.tensor.transpose(ux_ps[0:(2 * H + 2) * KT, 0:P], tails[:, :, :].rearrange("p j c -> p (j c)"),
                                    g.ident[:, :]).then_inc(tails_turned, 1)

            @block.scalar
            def _(act):
                with act.Fori(0, KT // 2) as i:
                    for u in range(2):
                        c = i * 2 + u
                        chain = Chain(act, chain_a, c * A_STEPS)
                        vec = lambda v: g.chan[:, bass.ds(c + v * KT, 1)]
                        act.wait_ge(ux_ready, c + 1)
                        act.wait_ge(u_ready, c)
                        chain(nc.scalar.copy(conv_in[:, H:H + T_PROMPT], ux_ps[:, 0:T_PROMPT]))
                        chain(nc.scalar.copy(conv_in[:, 2 * H + T_PROMPT:], ux_ps[:, T_PROMPT:T_ALL]))
                        for j in range(H):
                            at = H + T_PROMPT + j
                            chain(nc.scalar.copy(conv_in[:, at:at + 1], vec(V_HIST + j)), conv_ready if j == H - 1 else None)
                        for m in range(GATE_UNITS):
                            c0, n = CHUNKS[m % 3]
                            act.wait_ge(gate_ready, c * GATE_UNITS + m + 1)
                            if m == 0:
                                act.wait_ge(step_done, c)
                            dst = (r_sb, i_sb)[m // 3]
                            alone(act, g)
                            chain(nc.scalar.activation(dst[:, c0:c0 + n], gate_ps[:, m % 2, 0:n], ACT.Sigmoid,
                                                       bias=vec(V_BA + m // 3)), gate_taken)
                        act.sem_inc(ri_ready, 1)
                        lam = g.decay[:, bass.ds(c, 1)]
                        alone(act, g)
                        nc.scalar.activation(a_sb[:, :], r_sb[:, :], ACT.Exp, scale=lam).then_inc(at_ready, 1)
                        nc.scalar.activation(th_sb[:, :], r_sb[:, :], ACT.Tanh, scale=lam).then_inc(at_ready, 1)
                        act.wait_ge(at_ready, c * 2 + 2)
                        act.wait_ge(ug_ready, c + 1)
                        chain(nc.scalar.activation(gel[:, :], ug_ps[:, 0:T_ALL], ACT.Gelu_apprx_tanh), gel_ready)
                        act.wait_ge(var_ready, c + 1)
                        chain(nc.scalar.activation(v_sb[:, :], v_sb[:, :], ACT.Sqrt, scale=-1.0), std_ready)
                        chain.ended(A_STEPS)

            @block.vector
            def _(dve):
                v = nc.vector
                edge = Chain(dve, chain_e)
                for u in range(2):
                    edge(v.memset(bd[u][:, :, :], 0.0), bd_cleared if u else None)
                edge(v.memset(conv_in[:, 0:H], 0.0))
                with dve.Fori(0, KT // 2) as i:
                    for u in range(2):
                        c = i * 2 + u
                        chain = Chain(dve, chain_v, c * V_STEPS)
                        vec = lambda k: g.chan[:, bass.ds(c + k * KT, 1)]
                        dve.wait_ge(conv_ready, c + 1)
                        parts = ((0, T_PROMPT, 0), (T_PROMPT, T_SAMPLE, H + T_PROMPT))
                        for dst, n, src in parts:
                            chain(v.tensor_scalar(u_sb[:, dst:dst + n], conv_in[:, src + H:src + H + n], vec(V_CONV + H),
                                                  vec(V_CONVB), ALU.mult, ALU.add))
                        for j in range(H):
                            for dst, n, src in parts:
                                chain(v.scalar_tensor_tensor(u_sb[:, dst:dst + n], conv_in[:, src + j:src + j + n],
                                                             vec(V_CONV + j), u_sb[:, dst:dst + n], ALU.mult, ALU.add))
                        chain(v.tensor_copy(tails[:, 0:H, bass.ds(c, 1)].rearrange("p j o -> p (j o)"), conv_in[:, T_PROMPT:T_PROMPT + H]))
                        end = H + T_PROMPT + T_SAMPLE
                        chain(v.tensor_copy(tails[:, H:2 * H, bass.ds(c, 1)].rearrange("p j o -> p (j o)"), conv_in[:, end:end + H]), u_ready)
                        dve.wait_ge(ri_ready, c + 1)
                        chain(v.tensor_tensor(i_sb[:, :], i_sb[:, :], u_sb[:, :], ALU.mult))
                        dve.wait_ge(at_ready, c * 2 + 2)
                        chain(v.tensor_tensor(v_sb[:, :], a_sb[:, :], a_sb[:, :], ALU.mult))
                        chain(v.scalar_tensor_tensor(v_sb[:, :], v_sb[:, :], 1.0, th_sb[:, :], ALU.add, ALU.mult), var_ready)
                        dve.wait_ge(std_ready, c + 1)
                        chain(v.tensor_tensor(i_sb[:, :], i_sb[:, :], v_sb[:, :], ALU.mult))
                        chain(v.tensor_tensor_scan(h_sb[:, 0:T_PROMPT], a_sb[:, 0:T_PROMPT], i_sb[:, 0:T_PROMPT], 0.0,
                                                   ALU.mult, ALU.add))
                        chain(v.tensor_tensor_scan(h_sb[:, T_PROMPT:T_ALL], a_sb[:, T_PROMPT:T_ALL], i_sb[:, T_PROMPT:T_ALL],
                                                   vec(V_H0), ALU.mult, ALU.add))
                        for n, at in enumerate((T_PROMPT - 1, T_ALL - 1)):
                            chain(v.tensor_copy(tails[:, 2 * H + n, bass.ds(c, 1)], h_sb[:, at:at + 1]))
                        dve.wait_ge(gel_ready, c + 1)
                        chain(v.tensor_tensor(yT[:, bass.ds(c, 1), 0:T_ALL].rearrange("p o t -> p (o t)"), gel[:, :], h_sb[:, :],
                                              ALU.mult), step_done)
                        chain.ended(V_STEPS)
                dve.sem_inc(tails_ready, 1)
                dve.wait_ge(tails_turned, 1)
                edge(v.tensor_copy(tails_T[0:(2 * H + 2) * KT, :], ux_ps[0:(2 * H + 2) * KT, 0:P]), tails_kept)


def project(nc, g, branch, w_out, gate_col, add, tag):
    with ExitStack() as ctx:
        sb = lambda name, shape, dt=F32: ctx.enter_context(nc.sbuf_tensor(tag + name, shape, dt))
        w_p = [sb(f"_wp{u}", [P, KT, P]) for u in range(2)]
        w_g = [sb(f"_wg{u}", [P, KT, P]) for u in range(2)]
        sig = sb("_sig", [P, T_ALL])
        gate_ps = ctx.enter_context(nc.psum_tensor(tag + "_gate_ps", [P, 3 * BANK], F32))
        proj_ps = ctx.enter_context(nc.psum_tensor(tag + "_proj_ps", [P, 3 * BANK], F32))
        sem = lambda name: g.sem(f"{tag}_{name}")
        w_loaded = [sem(f"w_loaded{u}") for u in range(2)]
        w_used, gate_ready, proj_ready, sig_ready, proj_taken, chain_v = (sem("w_used"), sem("gate_ready"), sem("proj_ready"),
                                                                          sem("sig_ready"), sem("proj_taken"), sem("chain_v"))
        V_STEPS = 2 if add else 1
        w_out_k = w_out[0].rearrange("(k p) n -> p k n", p=P)

        with nc.Block() as block:
            @block.sync
            def _(sp):
                with sp.Fori(0, KT // 2) as i:
                    for u in range(2):
                        c = i * 2 + u
                        sp.wait_ge(w_used, c + 1)
                        sp.dma_start(w_g[u][:, :, :], g.w_in_k[:, :, bass.ds(c * P + gate_col, P)]).then_inc(w_loaded[u], 16)
                        sp.dma_start(w_p[u][:, :, :], w_out_k[:, :, bass.ds(c * P, P)]).then_inc(w_loaded[u], 16)

            @block.tensor
            def _(pe):
                pe.sem_inc(w_used, 2)
                with pe.Fori(0, KT // 2) as i:
                    for u in range(2):
                        c = i * 2 + u
                        pe.wait_ge(w_loaded[u], i * 32 + 32)
                        pe.wait_ge(sig_ready, c)
                        for c0, n in CHUNKS:
                            for k in range(KT):
                                last = nc.tensor.matmul(gate_ps[:, c0:c0 + n], w_g[u][:, k, :], g.xnT[:, k, c0:c0 + n],
                                                        start=(k == 0), stop=(k == KT - 1))
                        last.then_inc(gate_ready, 1)
                        pe.wait_ge(proj_taken, c)
                        for c0, n in CHUNKS:
                            for k in range(KT):
                                last = nc.tensor.matmul(proj_ps[:, c0:c0 + n], w_p[u][:, k, :], branch[:, k, c0:c0 + n],
                                                        start=(k == 0), stop=(k == KT - 1))
                        last.then_inc(proj_ready, 1)
                        pe.wait_ge(proj_ready, c + 1)
                        pe.sem_inc(w_used, 1)

            @block.scalar
            def _(act):
                with act.Fori(0, KT) as c:
                    act.wait_ge(gate_ready, c + 1)
                    act.wait_ge(proj_taken, c)
                    nc.scalar.activation(sig[:, :], gate_ps[:, 0:T_ALL], ACT.Sigmoid).then_inc(sig_ready, 1)

            @block.vector
            def _(dve):
                with dve.Fori(0, KT) as c:
                    chain = Chain(dve, chain_v, c * V_STEPS)
                    dve.wait_ge(proj_ready, c + 1)
                    dve.wait_ge(sig_ready, c + 1)
                    m = g.mT[:, bass.ds(c, 1), 0:T_ALL].rearrange("p o t -> p (o t)")
                    if add:
                        chain(nc.vector.tensor_tensor(sig[:, :], sig[:, :], proj_ps[:, 0:T_ALL], ALU.mult))
                        chain(nc.vector.tensor_tensor(m, m, sig[:, :], ALU.add), proj_taken)
                    else:
                        chain(nc.vector.tensor_tensor(m, sig[:, :], proj_ps[:, 0:T_ALL], ALU.mult), proj_taken)
                    chain.ended(V_STEPS)


def attend(nc, g, attnT):
    QKV = 3 * P
    UNITS = [(h, t) for h in range(2) for t in range(PT)] + ["stream"]
    NU = len(UNITS)
    STREAM = NU - 1
    tiles_of = lambda n: PAST_TILES + 1 if n == STREAM else UNITS[n][1] + 1
    groups_of = lambda n: [list(range(j, min(j + 4, tiles_of(n)))) for j in range(0, tiles_of(n), 4)]
    GROUPS_ALL = [(n, js) for n in range(NU) for js in groups_of(n)]
    NG = len(GROUPS_ALL)
    USE_QK, USE_PAST = 0, NT
    USE_P = USE_PAST + 2 * PAST_TILES // 4
    USE_O = USE_P + NG
    USES = USE_O + PT // 4 + 1
    first_group = lambda n: sum(len(groups_of(m)) for m in range(n))

    with ExitStack() as ctx:
        sb = lambda name, shape, dt=F32: ctx.enter_context(nc.sbuf_tensor(name, shape, dt))
        w_qkv = sb("w_qkv", [P, KT, QKV])
        gain = sb("qk_gain", [P, 4, HD])
        qk_sb = sb("qk_sb", [P, NT, 4, HD])
        v_new = sb("v_new", [P, NT, P])
        squares = sb("qk_squares", [P, 4, HD])
        scaled = sb("qk_scaled", [P, 4, HD])
        rstd = sb("qk_rstd", [P, NT, 4])
        k_past, v_past = sb("k_past", [P, PAST_TILES, P]), sb("v_past", [P, PAST_TILES, P])
        qkT, kT_past = g.qkT, sb("kT_past", [HD + 1, 2, PAST])
        probs_s = sb("probs_s", [P, KV_SAMPLE])
        probs = [probs_s[:, b * T_PROMPT:(b + 1) * T_PROMPT] for b in range(2)]
        probsT = [sb(f"probsT{b}", [P, BANK]) for b in range(2)]
        neg_max, total = sb("neg_max", [P, NU + 1]), sb("exp_total", [P, NU + 1])
        tail_sb = sb("tail_sb", [P, T_SAMPLE])
        o_sb, o_s = sb("o_sb", [P, PT, P]), sb("o_s", [P, P])
        scores = ctx.enter_context(nc.psum_tensor("scores", [P, 4 * BANK], F32))
        turn_ps = ctx.enter_context(nc.psum_tensor("turn_ps", [P, 2, BANK], F32))
        out_ps = ctx.enter_context(nc.psum_tensor("out_ps", [P, 2, BANK], F32))
        tail = out_ps[:, 1, 256:256 + T_SAMPLE]
        half = lambda n: scores[:, (n % 2) * 2 * BANK:(n % 2 + 1) * 2 * BANK]

        sem = lambda name: g.sem("a_" + name)
        gain_loaded, w_loaded, past_k_loaded, past_v_loaded, c_loaded = (sem("gain_loaded"), sem("w_loaded"), sem("k_loaded"),
                                                                         sem("v_loaded"), sem("c_loaded"))
        w_used, past_k_used, past_v_used, c_used = sem("w_used"), sem("k_used"), sem("v_used"), sem("c_used")
        kv_ready, kv_stored = sem("kv_ready"), sem("kv_stored")
        qkv_ready, sq_ready, mean_ready, rstd_ready, qk_ready = (sem("qkv_ready"), sem("sq_ready"), sem("mean_ready"),
                                                                 sem("rstd_ready"), sem("qk_ready"))
        turned = sem("turned")
        turn_taken = [sem(f"turn_taken{b}") for b in range(2)]
        scores_ready, max_ready, exp_ready, probs_used = sem("scores_ready"), sem("max_ready"), sem("exp_ready"), sem("probs_used")
        pv_done, out_ready, out_taken, tail_taken = sem("pv_done"), sem("out_ready"), sem("out_taken"), sem("tail_taken")
        chain_v, chain_a, chain_g = sem("chain_v"), sem("chain_a"), sem("chain_g")
        per_bank = [(USES + 1) // 2, USES // 2]

        by_act = lambda m: m < USE_PAST or (m < USE_P and m % 2 == 1)

        with nc.Block() as block:
            @block.sync
            def _(sp):
                for n, vec in enumerate((g.q_norm_g, g.q_norm_g, g.k_norm_g, g.k_norm_g)):
                    sp.dma_start(gain[:, n, :], row(vec[0]).to_broadcast([P, HD])).then_inc(gain_loaded, 16)
                heads = lambda ap, i: ap.rearrange("(t p) h d -> p t (h d)", p=P)[:, :, bass.ds(i * P, P)]
                with sp.Fori(0, PAIRS) as i:
                    sp.wait_ge(w_used, i)
                    for n, col in enumerate((COL_Q, COL_K, COL_V)):
                        sp.dma_start(w_qkv[:, :, n * P:(n + 1) * P], g.w_in_k[:, :, bass.ds(i * P + col, P)]).then_inc(w_loaded, 16)
                    sp.wait_ge(past_k_used, i)
                    alone(sp, g)
                    sp.dma_start(k_past[:, :, :], heads(g.cache_k[0, 0], i)).then_inc(past_k_loaded, 16)
                    sp.wait_ge(kv_ready, i + 1)
                    sp.dma_start(heads(g.out_k_p[0, 0], i), qk_sb[:, 0:PT, 2:4, :].rearrange("p t h d -> p t (h d)")).then_inc(kv_stored, 16)
                    sp.dma_start(heads(g.out_v_p[0, 0], i), v_new[:, 0:PT, :]).then_inc(kv_stored, 16)
                    stream = lambda ap: ap.rearrange("t h d -> t (h d)")[:, bass.ds(i * P, P)]
                    sp.dma_start(stream(g.out_k_s[0, 0]), qk_sb[0:T_SAMPLE, PT, 2:4, :].rearrange("p h d -> p (h d)")).then_inc(kv_stored, 16)
                    sp.dma_start(stream(g.out_v_s[0, 0]), v_new[0:T_SAMPLE, PT, :]).then_inc(kv_stored, 16)
                sp.wait_ge(kv_stored, PAIRS * 64)

            @block.gpsimd
            def _(pool):
                with pool.Fori(0, PAIRS) as i:
                    pool.wait_ge(c_used, i)
                    pool.dma_start(qkT[HD:HD + 1, 2:4, 0:T_ALL], g.neg_c_new[bass.ds(i * 2, 2), :].unsqueeze(0)).then_inc(c_loaded, 16)
                    pool.dma_start(kT_past[HD:HD + 1, :, :], g.neg_c_past[bass.ds(i * 2, 2), :].unsqueeze(0)).then_inc(c_loaded, 16)
                    pool.wait_ge(past_v_used, i)
                    pool.dma_start(v_past[:, :, :], g.cache_v[0, 0].rearrange("(t p) h d -> p t (h d)", p=P)[:, :, bass.ds(i * P, P)])\
                        .then_inc(past_v_loaded, 16)

            @block.tensor
            def _(pe):
                te = nc.tensor
                with pe.Fori(0, PAIRS) as i:
                    def bank_free(m):
                        pe.wait_ge(turn_taken[m % 2], i * per_bank[m % 2] + m // 2)

                    def project_tile(t):
                        if t >= 2:
                            pe.wait_ge(qk_ready, i * NT + (t - 1))
                        for k in range(KT):
                            last = te.matmul(half(t)[:, 0:QKV], g.xnT[:, k, t * P:(t + 1) * P], w_qkv[:, k, :],
                                             start=(k == 0), stop=(k == KT - 1))
                        last.then_inc(qkv_ready, 1)

                    def turn_qk(t):
                        pe.wait_ge(qk_ready, i * NT + (t + 1))
                        bank_free(USE_QK + t)
                        alone(pe, g)
                        for n in range(4):
                            last = te.transpose(turn_ps[0:HD, (USE_QK + t) % 2, n * P:(n + 1) * P], qk_sb[:, t, n, :], g.ident[:, :])
                        last.then_inc(turned, 1)

                    pe.wait_ge(w_loaded, i * 48 + 48)
                    pe.wait_ge(exp_ready, i * NU)
                    for t in range(NT):
                        project_tile(t)
                        if t == NT - 1:
                            pe.wait_ge(qkv_ready, (i + 1) * NT)
                            pe.sem_inc(w_used, 1)
                        if t:
                            turn_qk(t - 1)
                    turn_qk(NT - 1)

                    pe.wait_ge(past_k_loaded, i * 16 + 16)
                    for h in range(2):
                        for c in range(PAST_TILES // 4):
                            m = USE_PAST + h * PAST_TILES // 4 + c
                            bank_free(m)
                            alone(pe, g)
                            for n in range(4):
                                last = te.transpose(turn_ps[0:HD, m % 2, n * P:(n + 1) * P],
                                                    k_past[:, c * 4 + n, h * HD:(h + 1) * HD], g.ident[:, :])
                            last.then_inc(turned, 1)
                    pe.wait_ge(turned, i * USES + USE_P)
                    pe.sem_inc(past_k_used, 1)

                    def score(n):
                        if n == STREAM:
                            pe.wait_ge(exp_ready, i * NU + n)
                            pe.wait_ge(out_taken, i * NU + n - 1)
                            for c in range(PAST // BANK):
                                for h in range(2):
                                    te.matmul(scores[h * 64:(h + 1) * 64, c * BANK:(c + 1) * BANK],
                                              qkT[:, h, T_PROMPT:T_ALL], kT_past[:, h, c * BANK:(c + 1) * BANK],
                                              start=True, stop=True)
                            for h in range(2):
                                te.matmul(tail[h * 64:(h + 1) * 64, :], qkT[:, h, T_PROMPT:T_ALL],
                                          qkT[:, 2 + h, T_PROMPT:T_ALL], start=True, stop=False, skip_group_check=True)
                            te.matmul(tail, g.ident_bf[:, :], g.causal_s[:, :], start=False, stop=True,
                                      skip_group_check=True).then_inc(scores_ready, 1)
                            return
                        h, t = UNITS[n]
                        if n >= 2:
                            pe.wait_ge(exp_ready, i * NU + n - 1)
                        for c0 in range(0, (t + 1) * P, BANK):
                            w = min(BANK, (t + 1) * P - c0)
                            diagonal = c0 + w == (t + 1) * P
                            te.matmul(half(n)[:, c0:c0 + w], qkT[:, h, t * P:(t + 1) * P], qkT[:, 2 + h, c0:c0 + w],
                                      start=True, stop=not diagonal)
                        te.matmul(half(n)[:, t * P:(t + 1) * P], g.ident_bf[:, :], g.causal[:, :],
                                  start=False, stop=True).then_inc(scores_ready, 1)

                    def turn_group(n, q, js):
                        m = USE_P + q
                        bank_free(m)
                        if js[0] == PAST_TILES:
                            alone(pe, g)
                        for s, j in enumerate(js):
                            src = (probs_s if n == STREAM else probs[n % 2])
                            w = T_SAMPLE if j == PAST_TILES else P
                            last = te.transpose(turn_ps[0:w, m % 2, s * P:(s + 1) * P], src[:, j * P:j * P + w], g.ident[:, :])
                        last.then_inc(turned, 1)

                    def weigh_group(n, q, js):
                        m = USE_P + q
                        pe.wait_ge(turn_taken[m % 2], i * per_bank[m % 2] + (m // 2 + 1))
                        for s, j in enumerate(js):
                            flags = dict(start=(j == 0), stop=(j == tiles_of(n) - 1))
                            pt = probsT[q % 2][:, s * P:(s + 1) * P]
                            if n == STREAM and j == PAST_TILES:
                                last = te.matmul(out_ps[:, n % 2, 0:P], pt[0:T_SAMPLE, :], v_new[0:T_SAMPLE, PT, :], **flags)
                            elif n == STREAM:
                                last = te.matmul(out_ps[:, n % 2, 0:P], pt, v_past[:, j, :], **flags)
                            else:
                                h = UNITS[n][0]
                                last = te.matmul(out_ps[:, n % 2, 0:HD], pt, v_new[:, j, h * HD:(h + 1) * HD], **flags)
                        last.then_inc(pv_done, 1)

                    pe.wait_ge(c_loaded, i * 32 + 32)
                    for b in range(2):
                        pe.wait_ge(turn_taken[b], i * per_bank[b] + (USE_P + 1 - b) // 2)
                    score(0)
                    for n in range(NU):
                        if n + 1 < NU:
                            score(n + 1)
                        else:
                            pe.wait_ge(scores_ready, (i + 1) * NU)
                            pe.sem_inc(c_used, 1)
                            pe.wait_ge(past_v_loaded, i * 16 + 16)
                        pe.wait_ge(exp_ready, i * NU + n + 1)
                        if n >= 2:
                            pe.wait_ge(out_taken, i * NU + n - 1)
                        if n + 1 == STREAM:
                            pe.wait_ge(tail_taken, i + 1)
                        q0, groups = first_group(n), groups_of(n)
                        for s, js in enumerate(groups):
                            turn_group(n, q0 + s, js)
                            if s:
                                weigh_group(n, q0 + s - 1, groups[s - 1])
                        weigh_group(n, q0 + len(groups) - 1, groups[-1])
                        pe.wait_ge(pv_done, i * NG + q0 + len(groups))
                        pe.sem_inc(out_ready, 1)
                        pe.sem_inc(probs_used, 1)
                    pe.sem_inc(past_v_used, 1)

                    for s in range(PT // 4):
                        m = USE_O + s
                        pe.wait_ge(out_taken, i * NU + 2 * PT)
                        bank_free(m)
                        for n in range(4):
                            last = te.transpose(turn_ps[:, m % 2, n * P:(n + 1) * P], o_sb[:, s * 4 + n, :], g.ident[:, :])
                        last.then_inc(turned, 1)
                    m = USES - 1
                    pe.wait_ge(out_taken, (i + 1) * NU)
                    bank_free(m)
                    te.transpose(turn_ps[:, m % 2, 0:P], o_s[:, :], g.ident[:, :]).then_inc(turned, 1)

            def take_past(eng, copy, i, m):
                q = m - USE_PAST
                h, c = q // (PAST_TILES // 4), q % (PAST_TILES // 4)
                eng.wait_ge(turned, i * USES + m + 1)
                return copy(kT_past[0:HD, h, c * BANK:(c + 1) * BANK], turn_ps[0:HD, m % 2, :])

            @block.scalar
            def _(act):
                sc = nc.scalar
                A_STEPS = NT * 3 + NT + PAST_TILES // 4 + NU + 1
                with act.Fori(0, PAIRS) as i:
                    chain = Chain(act, chain_a, i * A_STEPS)

                    def take_qk(t):
                        m = USE_QK + t
                        act.wait_ge(turned, i * USES + m + 1)
                        chain(sc.copy(qkT[0:HD, :, t * P:(t + 1) * P],
                                      turn_ps[0:HD, m % 2, :].rearrange("p (n c) -> p n c", n=4)), turn_taken[m % 2])

                    act.wait_ge(kv_stored, i * 64)
                    for t in range(NT):
                        act.wait_ge(qkv_ready, i * NT + t + 1)
                        chain(sc.copy(v_new[:, t, :], half(t)[:, 2 * P:QKV]))
                        act.wait_ge(mean_ready, i * NT + t)
                        chain(sc.activation(squares[:, :, :], half(t)[:, 0:2 * P].rearrange("p (n d) -> p n d", n=4), ACT.Square),
                              sq_ready)
                        act.wait_ge(mean_ready, i * NT + t + 1)
                        chain(sc.activation(rstd[:, t, :], rstd[:, t, :], ACT.Sqrt), rstd_ready)
                        if t:
                            take_qk(t - 1)
                    take_qk(NT - 1)
                    for m in range(USE_PAST, USE_P):
                        if by_act(m):
                            chain(take_past(act, sc.copy, i, m), turn_taken[m % 2])
                    for n in range(NU):
                        act.wait_ge(max_ready, i * NU + n + 1)
                        if n >= 2:
                            act.wait_ge(probs_used, i * NU + (n if n == STREAM else n - 1))
                        if n < STREAM:
                            w = (UNITS[n][1] + 1) * P
                            chain(sc.activation(probs[n % 2][:, 0:w], half(n)[:, 0:w], ACT.Exp, bias=neg_max[:, n:n + 1],
                                                accum_out=total[:, n:n + 1]), exp_ready)
                        else:
                            chain(sc.activation(probs_s[:, 0:PAST], scores[:, :], ACT.Exp, bias=neg_max[:, n:n + 1],
                                                accum_out=total[:, n:n + 1]))
                            chain(sc.activation(probs_s[:, PAST:], tail_sb[:, :], ACT.Exp, bias=neg_max[:, n:n + 1],
                                                accum_out=total[:, n + 1:n + 2]), exp_ready)
                    chain.ended(A_STEPS)

            @block.vector
            def _(dve):
                v = nc.vector
                edge = Chain(dve, chain_g)
                dve.wait_ge(gain_loaded, 64)
                edge(v.tensor_scalar(gain[:, 0:2, :], gain[:, 0:2, :], HD ** -0.5, None, ALU.mult))
                V_STEPS = NT * 5 + (USE_P - USE_PAST) // 2 + (NU + 3) + NG + 2 * NU + 1 + PT // 4 + 2
                with dve.Fori(0, PAIRS) as i:
                    chain = Chain(dve, chain_v, i * V_STEPS)
                    dve.wait_ge(kv_stored, i * 64)
                    for t in range(NT):
                        dve.wait_ge(sq_ready, i * NT + t + 1)
                        chain(v.reduce_sum(rstd[:, t, :], squares[:, :, :], axis=X_AXIS))
                        chain(v.tensor_scalar(rstd[:, t, :], rstd[:, t, :], 1.0 / HD, EPS, ALU.mult, ALU.add))
                        chain(v.reciprocal(rstd[:, t, :], rstd[:, t, :]), mean_ready)
                        dve.wait_ge(rstd_ready, i * NT + t + 1)
                        chain(v.tensor_tensor(scaled[:, :, :], half(t)[:, 0:2 * P].rearrange("p (n d) -> p n d", n=4),
                                              rstd[:, t, :].unsqueeze(2).to_broadcast([P, 4, HD]), ALU.mult))
                        chain(v.tensor_tensor(qk_sb[:, t, :, :], scaled[:, :, :], gain[:, :, :], ALU.mult), qk_ready)
                    dve.sem_inc(kv_ready, 1)
                    for m in range(USE_PAST, USE_P):
                        if not by_act(m):
                            chain(take_past(dve, v.tensor_copy, i, m), turn_taken[m % 2])

                    def maximum(n):
                        dve.wait_ge(scores_ready, i * NU + n + 1)
                        if n < STREAM:
                            chain(v.tensor_reduce(neg_max[:, n:n + 1], half(n)[:, 0:(UNITS[n][1] + 1) * P], X_AXIS, ALU.max,
                                                  negate=True), max_ready)
                        else:
                            chain(v.tensor_copy(tail_sb[:, :], tail), tail_taken)
                            chain(v.tensor_reduce(neg_max[:, n:n + 1], scores[:, :], X_AXIS, ALU.max, negate=True))
                            chain(v.tensor_reduce(neg_max[:, n + 1:n + 2], tail_sb[:, :], X_AXIS, ALU.max, negate=True))
                            chain(v.tensor_tensor(neg_max[:, n:n + 1], neg_max[:, n:n + 1], neg_max[:, n + 1:n + 2], ALU.min),
                                  max_ready)

                    maximum(0)
                    for n in range(NU):
                        if n + 1 < NU:
                            maximum(n + 1)
                        for s, js in enumerate(groups_of(n)):
                            q = first_group(n) + s
                            m = USE_P + q
                            dve.wait_ge(turned, i * USES + m + 1)
                            if q >= 2:
                                dve.wait_ge(pv_done, i * NG + q - 1)
                            rows = T_SAMPLE if js[0] == PAST_TILES else P
                            chain(v.tensor_copy(probsT[q % 2][0:rows, 0:len(js) * P], turn_ps[0:rows, m % 2, 0:len(js) * P]),
                                  turn_taken[m % 2])
                        dve.wait_ge(out_ready, i * NU + n + 1)
                        if n == STREAM:
                            chain(v.tensor_tensor(total[:, n:n + 1], total[:, n:n + 1], total[:, n + 1:n + 2], ALU.add))
                        chain(v.reciprocal(total[:, n:n + 1], total[:, n:n + 1]))
                        if n == STREAM:
                            chain(v.tensor_scalar(o_s[:, :], out_ps[:, n % 2, 0:P], total[:, n:n + 1], None, ALU.mult), out_taken)
                        else:
                            h, t = UNITS[n]
                            chain(v.tensor_scalar(o_sb[:, t, h * HD:(h + 1) * HD], out_ps[:, n % 2, 0:HD], total[:, n:n + 1],
                                                  None, ALU.mult), out_taken)
                    at = lambda rows, c0, n: attnT[rows, bass.ds(i, 1), c0:c0 + n].rearrange("p o t -> p (o t)")
                    for s in range(PT // 4):
                        m = USE_O + s
                        dve.wait_ge(turned, i * USES + m + 1)
                        chain(v.tensor_copy(at(slice(0, P), s * BANK, BANK), turn_ps[:, m % 2, :]), turn_taken[m % 2])
                    m = USES - 1
                    dve.wait_ge(turned, i * USES + m + 1)
                    for h in range(2):
                        rows = slice(h * HD, (h + 1) * HD)
                        chain(v.tensor_copy(at(rows, T_PROMPT, T_SAMPLE), turn_ps[rows, m % 2, rows]),
                              turn_taken[m % 2] if h else None)
                    chain.ended(V_STEPS)


def merge(nc, g, x1, xn2, logits):
    R = GROUPS + EXPERTS
    with ExitStack() as ctx:
        sb = lambda name, shape, dt=F32: ctx.enter_context(nc.sbuf_tensor("m_" + name, shape, dt))
        w_o = sb("w_o", [P, KT, D])
        w_r = sb("w_r", [P, KT, R])
        gain = sb("gain", [P, D])
        squares = sb("squares", [P, D])
        ss = sb("ss", [P, NT])
        turned_sb = [sb(f"turned{b}", [P, KT, P]) for b in range(2)]
        prod = ctx.enter_context(nc.psum_tensor("m_prod", [P, 2, D], F32))
        turn_ps = ctx.enter_context(nc.psum_tensor("m_turn", [P, KT, P], F32))
        logit_ps = ctx.enter_context(nc.psum_tensor("m_logits", [P, NT, R], F32))
        sem = lambda name: g.sem("m_" + name)
        w_loaded, r_loaded, x_loaded, prod_ready, x1_ready, sq_ready, mean_ready, rstd_ready, xn2_ready = (
            sem("w_loaded"), sem("r_loaded"), sem("x_loaded"), sem("prod_ready"), sem("x1_ready"), sem("sq_ready"),
            sem("mean_ready"), sem("rstd_ready"), sem("xn2_ready"))
        turned, turn_taken, logits_ready, chain_v, chain_a, tail_clear = (sem("turned"), sem("turn_taken"), sem("logits_ready"),
                                                                          sem("chain_v"), sem("chain_a"), sem("tail_clear"))
        rows = lambda t: T_SAMPLE if t == PT else P

        with nc.Block() as block:
            @block.sync
            def _(sp):
                sp.dma_start(w_o[:, :, :], g.w_o[0].rearrange("(k p) n -> p k n", p=P)).then_inc(w_loaded, 16)
                sp.dma_start(x1[:, 0:PT, :], g.x_prompt[0].rearrange("(t p) n -> p t n", p=P)).then_inc(x_loaded, 16)
                sp.dma_start(x1[0:T_SAMPLE, PT, :], g.x_sample[0]).then_inc(x_loaded, 16)
                sp.dma_start(gain[:, :], row(g.norm2_g[0]).to_broadcast([P, D])).then_inc(r_loaded, 16)
                sp.dma_start(w_r[:, :, 0:GROUPS], g.w_route_group[0].rearrange("(k p) n -> p k n", p=P)).then_inc(r_loaded, 16)
                sp.dma_start(w_r[:, :, GROUPS:], g.w_route_expert[0].rearrange("(k p) n -> p k n", p=P)).then_inc(r_loaded, 16)

            @block.gpsimd
            def _(pool):
                nc.gpsimd.memset(x1[T_SAMPLE:P, PT, :], 0.0).then_inc(tail_clear, 1)

            @block.tensor
            def _(pe):
                te = nc.tensor
                pe.wait_ge(w_loaded, 16)

                def route_tile(t):
                    pe.wait_ge(xn2_ready, t + 1)
                    if t:
                        pe.wait_ge(turn_taken, t)
                    for k in range(KT):
                        last = te.transpose(turn_ps[:, k, :], xn2[:, t, k * P:(k + 1) * P], g.ident[:, :])
                    last.then_inc(turned, 1)

                def logit_tile(t):
                    pe.wait_ge(turn_taken, t + 1)
                    for k in range(KT):
                        last = te.matmul(logit_ps[:, t, :], turned_sb[t % 2][:, k, :], w_r[:, k, :], start=(k == 0),
                                         stop=(k == KT - 1))
                    last.then_inc(logits_ready, 1)

                pe.wait_ge(r_loaded, 48)
                for t in range(NT + 2):
                    if t < NT:
                        if t >= 2:
                            pe.wait_ge(x1_ready, t - 1)
                        for c in range(D // BANK):
                            for k in range(KT):
                                last = te.matmul(prod[0:rows(t), t % 2, c * BANK:(c + 1) * BANK], g.mT[:, k, t * P:t * P + rows(t)],
                                                 w_o[:, k, c * BANK:(c + 1) * BANK], start=(k == 0), stop=(k == KT - 1))
                        last.then_inc(prod_ready, 1)
                    if t >= 2:
                        logit_tile(t - 2)
                    if 1 <= t <= NT:
                        route_tile(t - 1)

            @block.scalar
            def _(act):
                sc = nc.scalar
                chain = Chain(act, chain_a)

                def take(t):
                    act.wait_ge(turned, t + 1)
                    if t >= 2:
                        act.wait_ge(logits_ready, t - 1)
                    chain(sc.copy(turned_sb[t % 2][:, :, :], turn_ps[:, :, :]), turn_taken)

                for t in range(NT):
                    act.wait_ge(x1_ready, t + 1)
                    if t == PT:
                        act.wait_ge(tail_clear, 1)
                    chain(sc.activation(squares[:, :], x1[:, t, :], ACT.Square, accum_out=ss[:, t:t + 1]), sq_ready)
                    act.wait_ge(mean_ready, t + 1)
                    chain(sc.activation(ss[:, t:t + 1], ss[:, t:t + 1], ACT.Sqrt), rstd_ready)
                    if t:
                        take(t - 1)
                take(NT - 1)

            @block.vector
            def _(dve):
                v, chain = nc.vector, Chain(dve, chain_v)
                dve.wait_ge(x_loaded, 32)
                dve.wait_ge(tail_clear, 1)
                dve.wait_ge(r_loaded, 48)
                for t in range(NT):
                    dve.wait_ge(prod_ready, t + 1)
                    n = rows(t)
                    chain(v.tensor_tensor(x1[0:n, t, :], x1[0:n, t, :], prod[0:n, t % 2, :], ALU.add), x1_ready)
                    dve.wait_ge(sq_ready, t + 1)
                    chain(v.tensor_scalar(ss[:, t:t + 1], ss[:, t:t + 1], 1.0 / D, EPS, ALU.mult, ALU.add))
                    chain(v.reciprocal(ss[:, t:t + 1], ss[:, t:t + 1]), mean_ready)
                    dve.wait_ge(rstd_ready, t + 1)
                    chain(v.scalar_tensor_tensor(xn2[:, t, :], x1[:, t, :], ss[:, t:t + 1], gain[:, :], ALU.mult, ALU.mult),
                          xn2_ready)
                dve.wait_ge(logits_ready, NT)
                chain(v.tensor_copy(logits[:, :, :], logit_ps[:, :, :]))


def route(nc, g, xn2, logits, gates, slots, passes, expert_of):
    OVER = BLOCKS_MAX - EXPERTS
    with ExitStack() as ctx:
        sb = lambda name, shape, dt=F32: ctx.enter_context(nc.sbuf_tensor("q_" + name, shape, dt))
        bias = sb("bias", [P, GROUPS + EXPERTS])
        counting = sb("counting_i", [P, 64], I32)
        ramp = sb("ramp", [P, 64])
        down4, down8 = sb("down4", [P, GROUPS]), sb("down8", [P, PER_GROUP])
        steps = sb("steps", [P, OVER])
        s1, s2, s3, s4 = sb("s1", [P, NT]), sb("s2", [P, NT]), sb("s3", [P, NT]), sb("s4", [P, NT])
        grp, wide4 = sb("grp", [P, NT, GROUPS]), sb("wide4", [P, NT, GROUPS])
        spread = sb("spread", [P, NT, PER_GROUP, GROUPS])
        inner, wide8 = sb("inner", [P, NT, PER_GROUP]), sb("wide8", [P, NT, PER_GROUP])
        pick = [sb(f"pick{n}", [P, NT, PER_GROUP]) for n in range(TOP_K)]
        chosen = [sb(f"chosen{n}", [P, NT, GROUPS, PER_GROUP]) for n in range(TOP_K)]
        both = sb("both", [P, NT, EXPERTS])
        run = sb("run", [P, NT + 1, EXPERTS])
        weighed = sb("weighed", [P, NT, EXPERTS])
        over, over_end, over_start = sb("over", [P, EXPERTS]), sb("over_end", [P, EXPERTS]), sb("over_start", [P, EXPERTS])
        ones_e = sb("ones_e", [P, EXPERTS])
        compared = sb("compared", [P, EXPERTS, OVER])
        rank, expert, start, times, block_of, slot_f = (sb(n, [P, TOP_K, NT]) for n in
                                                        ("rank", "expert", "start", "times", "block_of", "slot_f"))
        ge = sb("ge", [P, TOP_K * NT, OVER])
        pass_cmp, pass_sum = sb("pass_cmp", [1, OVER // 2]), sb("pass_sum", [1, 1])
        table_f = sb("table_f", [1, BLOCKS_MAX])
        counts_ps = ctx.enter_context(nc.psum_tensor("q_counts", [P, 2, BANK], F32))
        sem = lambda name: g.sem("q_" + name)
        bias_loaded, ramps_ready, exp_asked, exp_ready, both_ready, counts_ready, slots_ready, chain_v, chain_p, sent = (
            sem("bias_loaded"), sem("ramps_ready"), sem("exp_asked"), sem("exp_ready"), sem("both_ready"), sem("counts_ready"),
            sem("slots_ready"), sem("chain_v"), sem("chain_p"), sem("sent"))
        W = NT * EXPERTS

        with nc.Block() as block:
            @block.sync
            def _(sp):
                sp.dma_start(bias[:, 0:GROUPS], row(g.b_route_group[0]).to_broadcast([P, GROUPS])).then_inc(bias_loaded, 16)
                sp.dma_start(bias[:, GROUPS:], row(g.b_route_expert[0]).to_broadcast([P, EXPERTS])).then_inc(bias_loaded, 16)

            @block.gpsimd
            def _(pool):
                chain = Chain(pool, chain_p)
                chain(nc.gpsimd.iota(counting[:, :], pattern=[[1, 64]], base=0, channel_multiplier=0))
                chain(nc.gpsimd.tensor_copy(ramp[:, :], counting[:, :]), ramps_ready)
                pool.wait_ge(slots_ready, 1)
                for t in range(NT):
                    n = T_SAMPLE if t == PT else P
                    for s in range(TOP_K):
                        pool.indirect_dma_start(out=g.slot_x[:, :],
                                                out_offset=bass.IndirectOffsetOnAxis(ap=slots[0:n, s, t:t + 1], axis=0),
                                                in_=xn2[0:n, t, :], in_offset=None).then_inc(sent, 16)
                pool.wait_ge(sent, 16 * NT * TOP_K)

            @block.scalar
            def _(act):
                act.wait_ge(exp_asked, 1)
                nc.scalar.activation(wide4[:, :, :], wide4[:, :, :], ACT.Exp).then_inc(exp_ready, 1)
                act.wait_ge(exp_asked, 2)
                nc.scalar.activation(s3[:, :], s3[:, :], ACT.Exp).then_inc(exp_ready, 1)

            @block.tensor
            def _(pe):
                pe.wait_ge(both_ready, 1)
                flat = both[:, :, :].rearrange("p t e -> p (t e)")
                nc.tensor.matmul(counts_ps[:, 0, 0:W], g.before[:, :], flat, start=True, stop=True)
                nc.tensor.matmul(counts_ps[:, 1, 0:W], g.ones[:, :], flat, start=True, stop=True).then_inc(counts_ready, 1)

            @block.vector
            def _(dve):
                v, chain = nc.vector, Chain(dve, chain_v)
                tt, ts = v.tensor_tensor, v.tensor_scalar
                dve.wait_ge(ramps_ready, 1)
                chain(ts(down4[:, :], ramp[:, 0:GROUPS], -1.0, float(GROUPS), ALU.mult, ALU.add))
                chain(ts(down8[:, :], ramp[:, 0:PER_GROUP], -1.0, float(PER_GROUP), ALU.mult, ALU.add))
                chain(ts(steps[:, :], ramp[:, 1:OVER + 1], float(CAP), None, ALU.mult))
                chain(v.memset(ones_e[:, :], 1.0))
                dve.wait_ge(bias_loaded, 32)
                chain(tt(logits[:, :, :], logits[:, :, :], bias[:, :].unsqueeze(1).to_broadcast([P, NT, GROUPS + EXPERTS]), ALU.add))

                def first_of(out, values, top, down, n, scratch):
                    chain(tt(out, values, top.unsqueeze(2).to_broadcast([P, NT, n]), ALU.is_equal))
                    chain(tt(out, out, down.unsqueeze(1).to_broadcast([P, NT, n]), ALU.mult))
                    chain(v.tensor_reduce(scratch, out, X_AXIS, ALU.max))
                    chain(tt(out, out, scratch.unsqueeze(2).to_broadcast([P, NT, n]), ALU.is_equal))

                by_group = logits[:, :, 0:GROUPS]
                chain(v.tensor_reduce(s1[:, :], by_group, X_AXIS, ALU.max))
                chain(tt(wide4[:, :, :], by_group, s1[:, :].unsqueeze(2).to_broadcast([P, NT, GROUPS]), ALU.subtract), exp_asked)
                first_of(grp[:, :, :], by_group, s1[:, :], down4[:, :], GROUPS, s2[:, :])
                dve.wait_ge(exp_ready, 1)
                chain(v.reduce_sum(s4[:, :], wide4[:, :, :], axis=X_AXIS))
                chain(v.reciprocal(s4[:, :], s4[:, :]))

                per_expert = logits[:, :, GROUPS:].rearrange("p t (g e) -> p t e g", g=GROUPS)
                chain(tt(spread[:, :, :, :], per_expert, grp[:, :, :].unsqueeze(2).to_broadcast([P, NT, PER_GROUP, GROUPS]), ALU.mult))
                chain(v.reduce_sum(inner[:, :, :], spread[:, :, :, :], axis=X_AXIS))
                chain(v.tensor_reduce(s1[:, :], inner[:, :, :], X_AXIS, ALU.max))
                first_of(pick[0][:, :, :], inner[:, :, :], s1[:, :], down8[:, :], PER_GROUP, s2[:, :])
                chain(v.scalar_tensor_tensor(wide8[:, :, :], pick[0][:, :, :], NEG, inner[:, :, :], ALU.mult, ALU.add))
                chain(v.tensor_reduce(s3[:, :], wide8[:, :, :], X_AXIS, ALU.max))
                first_of(pick[1][:, :, :], wide8[:, :, :], s3[:, :], down8[:, :], PER_GROUP, s2[:, :])
                chain(tt(s3[:, :], s3[:, :], s1[:, :], ALU.subtract), exp_asked)
                dve.wait_ge(exp_ready, 2)
                chain(ts(s1[:, :], s3[:, :], 1.0, None, ALU.add))
                chain(v.reciprocal(s1[:, :], s1[:, :]))
                chain(tt(gates[:, 0, :], s1[:, :], s4[:, :], ALU.mult))
                chain(tt(gates[:, 1, :], gates[:, 0, :], s3[:, :], ALU.mult))

                for n in range(TOP_K):
                    for k in range(GROUPS):
                        chain(tt(chosen[n][:, :, k, :], pick[n][:, :, :],
                                 grp[:, :, k:k + 1].to_broadcast([P, NT, PER_GROUP]), ALU.mult))
                flat = [c[:, :, :, :].rearrange("p t g e -> p t (g e)") for c in chosen]
                chain(tt(both[:, :, :], flat[0], flat[1], ALU.add))
                chain(v.memset(both[T_SAMPLE:P, PT, :], 0.0), both_ready)

                dve.wait_ge(counts_ready, 1)
                local = counts_ps[:, 0, 0:W].rearrange("p (t e) -> p t e", t=NT)
                whole = counts_ps[:, 1, 0:W].rearrange("p (t e) -> p t e", t=NT)
                chain(v.memset(run[:, 0, :], 0.0))
                for t in range(NT):
                    chain(tt(run[:, t + 1, :], run[:, t, :], whole[:, t, :], ALU.add))
                chain(tt(compared[:, :, :], run[:, NT, :].unsqueeze(2).to_broadcast([P, EXPERTS, OVER]),
                         steps[:, :].unsqueeze(1).to_broadcast([P, EXPERTS, OVER]), ALU.is_gt))
                chain(v.reduce_sum(over[:, :], compared[:, :, :], axis=X_AXIS))
                chain(v.tensor_tensor_scan(over_end[:, :], ones_e[:, :], over[:, :], 0.0, ALU.mult, ALU.add))
                chain(tt(over_start[:, :], over_end[:, :], over[:, :], ALU.subtract))
                chain(tt(both[:, :, :], local, run[:, 0:NT, :], ALU.add))
                wide = lambda ap: ap.unsqueeze(1).to_broadcast([P, NT, EXPERTS])
                for n in range(TOP_K):
                    for out, of in ((rank, both[:, :, :]), (expert, wide(ramp[:, 0:EXPERTS])), (start, wide(over_start[:, :]))):
                        chain(tt(weighed[:, :, :], flat[n], of, ALU.mult))
                        chain(v.reduce_sum(out[:, n, :], weighed[:, :, :], axis=X_AXIS))
                two = lambda a: a[:, :, :].rearrange("p s t -> p (s t)")
                chain(tt(ge[:, :, :], two(rank).unsqueeze(2).to_broadcast([P, TOP_K * NT, OVER]),
                         steps[:, :].unsqueeze(1).to_broadcast([P, TOP_K * NT, OVER]), ALU.is_ge))
                chain(v.reduce_sum(two(times), ge[:, :, :], axis=X_AXIS))
                chain(tt(two(block_of), two(start), two(times), ALU.add))
                chain(tt(two(block_of), two(block_of), two(expert), ALU.subtract))
                chain(ts(two(block_of), two(block_of), float(EXPERTS - 1), None, ALU.add))
                chain(ts(two(slot_f), two(times), 1.0, None, ALU.min))
                chain(tt(two(block_of), two(block_of), two(slot_f), ALU.mult))
                chain(tt(two(block_of), two(block_of), two(expert), ALU.add))
                chain(tt(two(slot_f), two(block_of), two(times), ALU.subtract))
                chain(v.scalar_tensor_tensor(two(slot_f), two(slot_f), float(CAP), two(rank), ALU.mult, ALU.add))
                chain(v.tensor_copy(slots[:, :, :], slot_f[:, :, :]), slots_ready)

                chain(ts(pass_cmp[:, :], ramp[0:1, 0:OVER // 2], 2.0, None, ALU.mult))
                chain(tt(pass_cmp[:, :], over_end[0:1, EXPERTS - 1:EXPERTS].to_broadcast([1, OVER // 2]), pass_cmp[:, :], ALU.is_gt))
                chain(v.reduce_sum(pass_sum[:, :], pass_cmp[:, :], axis=X_AXIS))
                chain(ts(passes[:, :], pass_sum[:, :], float(EXPERTS // 2), None, ALU.add))
                chain(v.tensor_copy(table_f[:, 0:EXPERTS], ramp[0:1, 0:EXPERTS]))
                by_block = compared[0:1, :, :].rearrange("p e o -> p (e o)").rearrange("p (o e) -> p o e", e=EXPERTS)
                chain(tt(by_block, over_end[0:1, :].unsqueeze(1).to_broadcast([1, OVER, EXPERTS]),
                         ramp[0:1, 0:OVER].unsqueeze(2).to_broadcast([1, OVER, EXPERTS]), ALU.is_le))
                chain(v.reduce_sum(table_f[:, EXPERTS:], by_block, axis=X_AXIS))
                chain(ts(table_f[:, :], table_f[:, :], float(EXPERTS - 1), None, ALU.min))
                chain(v.tensor_copy(expert_of[:, :], table_f[:, :]))


def experts(nc, g, passes, expert_of):
    with ExitStack() as ctx:
        sb = lambda name, shape, dt=F32: ctx.enter_context(nc.sbuf_tensor("e_" + name, shape, dt))
        w_gate = [sb(f"gate{u}", [P, KT, F_EXP]) for u in range(2)]
        w_up = [sb(f"up{u}", [P, KT, F_EXP]) for u in range(2)]
        w_down = [sb(f"down{u}", [P, FT, D]) for u in range(2)]
        xb = [sb(f"x{u}", [CAP, D]) for u in range(2)]
        xT = sb("xT", [P, KT, CAP])
        act_sb = sb("act", [P, FT * CAP])
        hT = sb("hT", [P, FT * CAP])
        y_sb = [sb(f"y{u}", [CAP, D]) for u in range(2)]
        xT_ps = ctx.enter_context(nc.psum_tensor("e_xT_ps", [P, 2, BANK], F32))
        gate_ps = ctx.enter_context(nc.psum_tensor("e_gate_ps", [P, BANK], F32))
        up_ps = ctx.enter_context(nc.psum_tensor("e_up_ps", [P, BANK], F32))
        y_ps = ctx.enter_context(nc.psum_tensor("e_y_ps", [CAP, D], F32))
        sem = lambda name: g.sem("e_" + name)
        x_loaded, gate_loaded, up_loaded, down_loaded = ([sem(f"{n}_loaded{u}") for u in range(2)] for n in ("x", "gate", "up", "down"))
        x_used, in_used, down_used = sem("x_used"), sem("in_used"), sem("down_used")
        x_turned, xT_ready, gate_ready, up_ready, act_ready, h_ready, y_ready, y_kept = (
            sem("x_turned"), sem("xT_ready"), sem("gate_ready"), sem("up_ready"), sem("act_ready"), sem("h_ready"),
            sem("y_ready"), sem("y_kept"))
        y_stored = [sem(f"y_stored{u}") for u in range(2)]
        limits = dict(min_val=EXPERTS // 2, max_val=BLOCKS_MAX // 2)

        with nc.Block() as block:
            @block.sync
            def _(sp):
                n = sp.value_load(passes[0:1, 0:1], **limits)
                with sp.Fori(0, n) as i:
                    for u in range(2):
                        b = i * 2 + u
                        e = sp.value_load(expert_of[0:1, bass.ds(b, 1)], min_val=0, max_val=EXPERTS - 1)
                        sp.wait_ge(x_used, b + 1)
                        sp.dma_start(xb[u][:, :], g.slot_x[bass.ds(b * CAP, CAP), :]).then_inc(x_loaded[u], 16)
                        sp.wait_ge(in_used, b + 1)
                        into = lambda w, p: w[0, bass.ds(e, 1)].rearrange("o (k p) n -> p (o k) n", p=p)
                        sp.dma_start(w_gate[u][:, :, :], into(g.w_gate_e, P)).then_inc(gate_loaded[u], 16)
                        sp.dma_start(w_up[u][:, :, :], into(g.w_up_e, P)).then_inc(up_loaded[u], 16)
                        sp.wait_ge(down_used, b + 1)
                        sp.dma_start(w_down[u][:, :, :], into(g.w_down_e, P)).then_inc(down_loaded[u], 16)

            @block.tensor
            def _(pe):
                te = nc.tensor
                n = pe.value_load(passes[0:1, 0:1], **limits)
                pe.sem_inc(x_used, 2)
                pe.sem_inc(in_used, 2)
                pe.sem_inc(down_used, 2)
                with pe.Fori(0, n) as i:
                    for u in range(2):
                        b = i * 2 + u
                        pe.wait_ge(x_loaded[u], i * 16 + 16)
                        pe.wait_ge(xT_ready, b)
                        for k in range(KT):
                            last = te.transpose(xT_ps[:, k // 4, (k % 4) * CAP:(k % 4 + 1) * CAP], xb[u][:, k * P:(k + 1) * P],
                                                g.ident[0:CAP, 0:CAP])
                        last.then_inc(x_turned, 1)
                        pe.wait_ge(x_turned, b + 1)
                        pe.sem_inc(x_used, 1)
                        pe.wait_ge(xT_ready, b + 1)
                        pe.wait_ge(h_ready, b)
                        for w, loaded, out, ready in ((w_gate, gate_loaded, gate_ps, gate_ready), (w_up, up_loaded, up_ps, up_ready)):
                            pe.wait_ge(loaded[u], i * 16 + 16)
                            for f in range(FT):
                                for k in range(KT):
                                    last = te.matmul(out[:, f * CAP:(f + 1) * CAP], w[u][:, k, f * P:(f + 1) * P], xT[:, k, :],
                                                     start=(k == 0), stop=(k == KT - 1))
                            last.then_inc(ready, 1)
                        pe.wait_ge(up_ready, b + 1)
                        pe.sem_inc(in_used, 1)
                        pe.wait_ge(h_ready, b + 1)
                        pe.wait_ge(down_loaded[u], i * 16 + 16)
                        pe.wait_ge(y_kept, b)
                        for c in range(D // BANK):
                            for f in range(FT):
                                last = te.matmul(y_ps[:, c * BANK:(c + 1) * BANK], hT[:, f * CAP:(f + 1) * CAP],
                                                 w_down[u][:, f, c * BANK:(c + 1) * BANK], start=(f == 0), stop=(f == FT - 1))
                        last.then_inc(y_ready, 1)
                        pe.wait_ge(y_ready, b + 1)
                        pe.sem_inc(down_used, 1)

            @block.scalar
            def _(act):
                n = act.value_load(passes[0:1, 0:1], **limits)
                with act.Fori(0, n) as i:
                    for u in range(2):
                        b = i * 2 + u
                        act.wait_ge(gate_ready, b + 1)
                        act.wait_ge(h_ready, b)
                        nc.scalar.activation(act_sb[:, :], gate_ps[:, 0:FT * CAP], ACT.Silu).then_inc(act_ready, 1)
                        act.wait_ge(y_ready, b + 1)
                        act.wait_ge(y_stored[u], i * 16)
                        nc.scalar.copy(y_sb[u][:, :], y_ps[:, :]).then_inc(y_kept, 1)
                        act.wait_ge(y_kept, b + 1)
                        act.dma_start(g.slot_y[bass.ds(b * CAP, CAP), :], y_sb[u][:, :]).then_inc(y_stored[u], 16)
                for u in range(2):
                    act.wait_ge(y_stored[u], n * 16)
                alone(act, g)

            @block.vector
            def _(dve):
                n = dve.value_load(passes[0:1, 0:1], **limits)
                with dve.Fori(0, n) as i:
                    for u in range(2):
                        b = i * 2 + u
                        dve.wait_ge(x_turned, b + 1)
                        dve.wait_ge(up_ready, b)
                        nc.vector.tensor_copy(xT[:, :, :].rearrange("p (a k) c -> p a (k c)", a=2), xT_ps[:, :, 0:4 * CAP])\
                            .then_inc(xT_ready, 1)
                        dve.wait_ge(up_ready, b + 1)
                        dve.wait_ge(act_ready, b + 1)
                        dve.wait_ge(y_ready, b)
                        nc.vector.tensor_tensor(hT[:, :], act_sb[:, :], up_ps[:, 0:FT * CAP], ALU.mult).then_inc(h_ready, 1)


def combine(nc, g, x1, gates, slots):
    BUFS = 3
    with ExitStack() as ctx:
        got = [[ctx.enter_context(nc.sbuf_tensor(f"c_got{s}_{b}", [P, D], F32)) for b in range(BUFS)] for s in range(TOP_K)]
        sem = lambda name: g.sem("c_" + name)
        gathered = [[sem(f"gathered{s}_{b}") for b in range(BUFS)] for s in range(TOP_K)]
        summed, chain_v, y_stored = sem("summed"), sem("chain_v"), sem("y_stored")
        rows = lambda t: T_SAMPLE if t == PT else P

        with nc.Block() as block:
            @block.gpsimd
            def _(pool):
                for t in range(NT):
                    if t >= BUFS:
                        pool.wait_ge(summed, t - BUFS + 1)
                    for s in range(TOP_K):
                        pool.indirect_dma_start(out=got[s][t % BUFS][0:rows(t), :], out_offset=None, in_=g.slot_y[:, :],
                                                in_offset=bass.IndirectOffsetOnAxis(ap=slots[0:rows(t), s, t:t + 1], axis=0))\
                            .then_inc(gathered[s][t % BUFS], 16)

            @block.vector
            def _(dve):
                chain = Chain(dve, chain_v)
                for t in range(NT):
                    n = rows(t)
                    for s in range(TOP_K):
                        dve.wait_ge(gathered[s][t % BUFS], 16 * (t // BUFS + 1))
                        chain(nc.vector.scalar_tensor_tensor(x1[0:n, t, :], got[s][t % BUFS][0:n, :], gates[0:n, s, t:t + 1],
                                                             x1[0:n, t, :], ALU.mult, ALU.add), summed if s else None)

            @block.sync
            def _(sp):
                for t in range(NT):
                    sp.wait_ge(summed, t + 1)
                    out = g.out_y_s[0] if t == PT else g.out_y_p[0, t * P:(t + 1) * P, :]
                    sp.dma_start(out, x1[0:rows(t), t, :]).then_inc(y_stored, 16)
                sp.wait_ge(y_stored, 16 * NT)


def back(nc, g):
    with ExitStack() as ctx:
        sb = lambda name, shape, dt=F32: ctx.enter_context(nc.sbuf_tensor(name, shape, dt))
        x1 = sb("x1", [P, NT, D])
        gates, slots = sb("gates", [P, TOP_K, NT]), sb("slots", [P, TOP_K, NT], U32)
        passes, expert_of = sb("passes", [1, 1], I32), sb("expert_of", [1, BLOCKS_MAX], I32)
        with nc.sbuf_tensor("xn2", [P, NT, D], F32) as xn2, nc.sbuf_tensor("logits", [P, NT, GROUPS + EXPERTS], F32) as logits:
            merge(nc, g, x1, xn2, logits)
            route(nc, g, xn2, logits, gates, slots, passes, expert_of)
        experts(nc, g, passes, expert_of)
        combine(nc, g, x1, gates, slots)


_INS = ["x_prompt", "x_sample", "cache_k", "cache_v", "cache_logf", "state_conv", "state_rglru", "norm1_g", "w_in",
        "conv_w", "conv_b", "w_a", "b_a", "w_x", "b_x", "lru_lambda", "b_f", "q_norm_g", "k_norm_g", "w_rnn_out",
        "w_attn_out", "w_o", "norm2_g", "w_route_group", "b_route_group", "w_route_expert", "b_route_expert",
        "w_gate_e", "w_up_e", "w_down_e"]
_OUTS = [("out_y_p", (1, T_PROMPT, D)), ("out_y_s", (1, T_SAMPLE, D)),
         ("out_k_p", (1, 1, T_PROMPT, HEADS, HD)), ("out_v_p", (1, 1, T_PROMPT, HEADS, HD)),
         ("out_lf_p", (1, 1, T_PROMPT, HEADS)), ("out_conv_p", (1, 1, CONV_W - 1, D)), ("out_h_p", (1, 1, D)),
         ("out_k_s", (1, 1, T_SAMPLE, HEADS, HD)), ("out_v_s", (1, 1, T_SAMPLE, HEADS, HD)),
         ("out_lf_s", (1, 1, T_SAMPLE, HEADS)), ("out_conv_s", (1, 1, CONV_W - 1, D)), ("out_h_s", (1, 1, D))]


class Shared:
    pass


def layer(nc, ctx, a):
    g = Shared()
    (g.x_prompt, g.x_sample, g.cache_k, g.cache_v, g.cache_logf, g.state_conv, g.state_rglru, g.norm1_g, g.w_in,
     g.conv_w, g.conv_b, g.w_a, g.b_a, g.w_x, g.b_x, g.lru_lambda, g.b_f, g.q_norm_g, g.k_norm_g, g.w_rnn_out,
     g.w_attn_out, g.w_o, g.norm2_g, g.w_route_group, g.b_route_group, g.w_route_expert, g.b_route_expert,
     g.w_gate_e, g.w_up_e, g.w_down_e) = (a[name] for name in _INS)
    (g.out_y_p, g.out_y_s, g.out_k_p, g.out_v_p, g.out_lf_p, g.out_conv_p, g.out_h_p, g.out_k_s, g.out_v_s,
     g.out_lf_s, g.out_conv_s, g.out_h_s) = (a[name] for name, _ in _OUTS)
    sb = lambda name, shape, dt=F32: ctx.enter_context(nc.sbuf_tensor(name, shape, dt))
    g.sem = lambda name: ctx.enter_context(nc.semaphore(name))
    g.slots_cleared = g.sem("slots_cleared")
    g.apart = g.sem("apart")
    g.w_in_k = g.w_in[0].rearrange("(k p) n -> p k n", p=P)
    g.slot_x = nc.dram_tensor("slot_x", [SLOTS, D], F32, kind="Internal").ap()
    g.slot_y = nc.dram_tensor("slot_y", [SLOTS, D], F32, kind="Internal").ap()
    g.neg_c_new = nc.dram_tensor("neg_c_new", [HEADS, T_ALL], F32, kind="Internal").ap()
    g.neg_c_past = nc.dram_tensor("neg_c_past", [HEADS, PAST], F32, kind="Internal").ap()
    g.ident, g.ones, g.before = sb("ident", [P, P]), sb("ones", [P, P]), sb("before", [P, P])
    g.ident_bf, g.causal = sb("ident_bf", [P, P], BF16), sb("causal", [P, P], BF16)
    g.causal_s = sb("causal_s", [P, T_SAMPLE], BF16)
    g.causal_f = sb("causal_f", [P, P])
    g.chan = sb("chan", [P, N_VEC * KT])
    g.decay = sb("decay", [P, KT])
    g.mT = sb("mT", [P, KT, T_PAD])
    with ExitStack() as front:
        sbf = lambda name, shape, dt=F32: front.enter_context(nc.sbuf_tensor(name, shape, dt))
        g.xnT = sbf("xnT", [P, KT, T_PAD])
        normalize(nc, g)
        g.qkT = sbf("qkT", [HD + 1, 4, T_PAD])
        forget_gates(nc, g)
        with nc.sbuf_tensor("yT", [P, KT, T_PAD], F32) as yT:
            recurrent(nc, g, yT)
            project(nc, g, yT, g.w_rnn_out, COL_GATE_RNN, False, "pr")
        with nc.sbuf_tensor("attnT", [P, KT, T_PAD], F32) as attnT:
            attend(nc, g, attnT)
            project(nc, g, attnT, g.w_attn_out, COL_GATE_ATTN, True, "pa")
    back(nc, g)


def kernel(**inputs):
    import numpy as np
    import concourse.bacc as bacc
    from concourse.bass_utils import run_bass_kernel_spmd

    nc = bacc.Bacc("TRN2", target_bir_lowering=False, num_devices=1)
    arrays, aps = {}, {}
    for name in _INS:
        arrays[name] = np.ascontiguousarray(inputs[name])
        aps[name] = nc.dram_tensor(name, arrays[name].shape, F32, kind="ExternalInput").ap()
    for name, shape in _OUTS:
        aps[name] = nc.dram_tensor(name, shape, F32, kind="ExternalOutput").ap()
    with ExitStack() as ctx:
        layer(nc, ctx, aps)
    r = run_bass_kernel_spmd(nc, [arrays], core_ids=[0])
    return tuple(r.results[0][name] for name, _ in _OUTS)
```

```python
import concourse.bass as bass
from concourse import mybir
from contextlib import ExitStack

F32 = mybir.dt.float32
BF16 = mybir.dt.bfloat16
I32 = mybir.dt.int32
U32 = mybir.dt.uint32
ALU = mybir.AluOpType
ACT = mybir.ActivationFunctionType
X_AXIS = mybir.AxisListType.X

P = 128
D = 1024
KT = D // P
T_PROMPT, T_SAMPLE, PAST = 1024, 64, 2048
T_ALL = T_PROMPT + T_SAMPLE
PT = T_PROMPT // P
NT = PT + 1
T_PAD = NT * P
CHUNKS = ((0, 512), (512, 512), (1024, T_SAMPLE))
BANK = 512
CONV_W = 4
LRU_C = 8.0
HEADS, HD = 16, 64
PAIRS = HEADS // 2
PAST_TILES = PAST // P
KV_SAMPLE = PAST + T_SAMPLE
GROUPS, PER_GROUP = 4, 8
EXPERTS = GROUPS * PER_GROUP
F_EXP = 512
FT = F_EXP // P
TOP_K = 2
CAP = 96
OVER_MAX = TOP_K * T_ALL // CAP
BLOCKS_MAX = (EXPERTS + OVER_MAX + 1) // 2 * 2
SLOTS = BLOCKS_MAX * CAP
EPS = 1e-6
NEG = -1e30

COL_X, COL_G, COL_Q, COL_K, COL_V = 0, D, 2 * D, 3 * D, 4 * D
COL_F = 5 * D
COL_GATE_RNN = COL_F + HEADS
COL_GATE_ATTN = COL_GATE_RNN + D

V_NORM1, V_CONV, V_CONVB, V_BA, V_BX, V_LAM, V_H0, V_HIST = 0, 1, 5, 6, 7, 8, 9, 10
N_VEC = 13


class Chain:

    def __init__(self, eng, sem, base=0):
        self.eng, self.sem, self.base, self.n = eng, sem, base, 0

    def __call__(self, ins, tell=None):
        self.n += 1
        ins.then_inc(self.sem, 1)
        self.eng.wait_ge(self.sem, self.base + self.n)
        if tell is not None:
            self.eng.sem_inc(tell, 1)

    def ended(self, per_pass):
        assert self.n == per_pass, self.n


def alone(eng, g):
    eng.sem_inc(g.apart, 1)


def row(ap, n=1):
    return ap.rearrange("(o n) -> o n", o=n)


def log1p_steps(nc, chain, out, z, s, s2, acc):
    v = nc.vector
    chain(v.tensor_scalar(s, z, 2.0, None, ALU.add))
    chain(v.reciprocal(s2, s))
    chain(v.tensor_tensor(s, z, s2, ALU.mult))
    chain(v.tensor_tensor(s2, s, s, ALU.mult))
    chain(v.tensor_scalar(acc, s2, 1.0 / 17.0, 1.0 / 15.0, ALU.mult, ALU.add))
    for k in (13, 11, 9, 7, 5, 3, 1):
        chain(v.tensor_tensor(acc, acc, s2, ALU.mult))
        chain(v.tensor_scalar(acc, acc, 1.0 / k, None, ALU.add))
    chain(v.scalar_tensor_tensor(out, acc, 2.0, s, ALU.mult, ALU.mult))


LOG1P_STEPS = 5 + 14 + 1


def normalize(nc, g):
    with ExitStack() as ctx:
        sb = lambda name, shape, dt=F32: ctx.enter_context(nc.sbuf_tensor(name, shape, dt))
        vec_rows = sb("vec_rows", [P, P])
        xt = sb("xt", [P, 3, D])
        x_last = sb("x_last", [P, D])
        square = sb("square", [P, D])
        ss = sb("ss", [P, NT])
        rstd = sb("rstd", [P, NT])
        zrows = sb("zrows", [P, D])
        turned = ctx.enter_context(nc.psum_tensor("turned", [P, 2, KT, P], F32))
        vec_ps = ctx.enter_context(nc.psum_tensor("vec_ps", [P, P], F32))
        sem = g.sem
        vec_loaded, const_ready, zrows_ready = sem("vec_loaded"), sem("const_ready"), sem("zrows_ready")
        x_loaded = [sem(f"x_loaded{b}") for b in range(4)]
        sq_ready, mean_ready, rstd_ready, xs_ready = sem("sq_ready"), sem("mean_ready"), sem("rstd_ready"), sem("xs_ready")
        xT_ready, xT_taken, vec_ready, chain_v, chain_p = sem("xT_ready"), sem("xT_taken"), sem("vec_ready"), sem("n_chain_v"), sem("n_chain_p")
        chain_a = sem("n_chain_a")
        tile = lambda t: x_last[:, :] if t == PT else xt[:, t % 3, :]
        load_of = lambda t: (x_loaded[3], 16) if t == PT else (x_loaded[t % 3], 16 * (t // 3 + 1))

        with nc.Block() as block:
            @block.sync
            def _(sp):
                vectors = [g.norm1_g[0], *(g.conv_w[0, j] for j in range(CONV_W)), g.conv_b[0], g.b_a[0], g.b_x[0],
                           g.lru_lambda[0], g.state_rglru[0, 0], *(g.state_conv[0, 0, j] for j in range(CONV_W - 1))]
                sp.dma_start(xt[:, 0, :], g.x_prompt[0, 0:P, :]).then_inc(x_loaded[0], 16)
                for n, vec in enumerate(vectors):
                    sp.dma_start(vec_rows[n * KT:(n + 1) * KT, :], row(vec, KT)).then_inc(vec_loaded, 16)
                for t in range(1, NT):
                    if t == PT:
                        sp.dma_start(x_last[0:T_SAMPLE, :], g.x_sample[0]).then_inc(x_loaded[3], 16)
                        continue
                    if t >= 3:
                        sp.wait_ge(xT_ready, t - 2)
                    sp.dma_start(xt[:, t % 3, :], g.x_prompt[0, t * P:(t + 1) * P, :]).then_inc(x_loaded[t % 3], 16)

            @block.scalar
            def _(act):
                act.wait_ge(zrows_ready, 1)
                for r in range(0, SLOTS + CAP, P):
                    n = min(P, SLOTS + CAP - r)
                    act.dma_start(g.slot_x[r:r + n, :], zrows[0:n, :]).then_inc(g.slots_cleared, 16)
                for r in range(EXPERTS * CAP, SLOTS, P):
                    n = min(P, SLOTS - r)
                    act.dma_start(g.slot_y[r:r + n, :], zrows[0:n, :]).then_inc(g.slots_cleared, 16)
                for t in range(NT):
                    act.wait_ge(*load_of(t))
                    if t == PT:
                        act.wait_ge(const_ready, 1)
                    if t:
                        act.wait_ge(chain_a, t)
                    nc.scalar.activation(square[:, :], tile(t), ACT.Square, accum_out=ss[:, t:t + 1]).then_inc(chain_a, 1)
                    act.wait_ge(chain_a, t + 1)
                    act.sem_inc(sq_ready, 1)
                    act.wait_ge(mean_ready, t + 1)
                    nc.scalar.activation(rstd[:, t:t + 1], rstd[:, t:t + 1], ACT.Sqrt).then_inc(rstd_ready, 1)
                act.wait_ge(g.slots_cleared, 16 * (-(-(SLOTS + CAP) // P) - (EXPERTS * CAP - SLOTS) // P))

            @block.gpsimd
            def _(pool):
                chain = Chain(pool, chain_p)
                chain(nc.gpsimd.memset(zrows[:, :], 0.0), zrows_ready)
                chain(nc.gpsimd.memset(g.ident[:, :], 0.0))
                chain(nc.gpsimd.affine_select(out=g.ident[:, :], in_=g.ident[:, :], compare_op=ALU.not_equal, fill=1.0,
                                              base=0, pattern=[[-1, P]], channel_multiplier=1))
                chain(nc.gpsimd.memset(x_last[T_SAMPLE:P, :], 0.0), const_ready)
                chain(nc.gpsimd.tensor_copy(g.ident_bf[:, :], g.ident[:, :]))
                chain(nc.gpsimd.memset(g.ones[:, :], 1.0))
                chain(nc.gpsimd.affine_select(out=g.before[:, :], in_=g.ones[:, :], compare_op=ALU.is_gt, fill=0.0,
                                              base=0, pattern=[[1, P]], channel_multiplier=-1))
                chain(nc.gpsimd.memset(g.causal_f[:, :], 0.0))
                chain(nc.gpsimd.affine_select(out=g.causal_f[:, :], in_=g.causal_f[:, :], compare_op=ALU.is_ge, fill=NEG,
                                              base=0, pattern=[[-1, P]], channel_multiplier=1))
                chain(nc.gpsimd.tensor_copy(g.causal[:, :], g.causal_f[:, :]))
                chain(nc.gpsimd.tensor_copy(g.causal_s[0:64, :], g.causal_f[0:64, 0:64]))
                chain(nc.gpsimd.tensor_copy(g.causal_s[64:P, :], g.causal_f[64:P, 64:P]))

            @block.tensor
            def _(pe):
                pe.wait_ge(const_ready, 1)
                pe.wait_ge(vec_loaded, 16 * N_VEC)
                nc.tensor.transpose(vec_ps[:, 0:N_VEC * KT], vec_rows[0:N_VEC * KT, :],
                                    g.ident[0:N_VEC * KT, 0:N_VEC * KT]).then_inc(vec_ready, 1)
                for t in range(NT):
                    pe.wait_ge(xs_ready, t + 1)
                    if t >= 2:
                        pe.wait_ge(xT_taken, t - 1)
                    for k in range(KT):
                        last = nc.tensor.transpose(turned[:, t % 2, k, :], tile(t)[:, k * P:(k + 1) * P], g.ident[:, :])
                    last.then_inc(xT_ready, 1)

            @block.vector
            def _(dve):
                chain = Chain(dve, chain_v)
                dve.wait_ge(vec_ready, 1)
                chain(nc.vector.tensor_copy(g.chan[:, :], vec_ps[:, 0:N_VEC * KT]))

                def take(t):
                    dve.wait_ge(xT_ready, t + 1)
                    gain = g.chan[:, V_NORM1 * KT:(V_NORM1 + 1) * KT].unsqueeze(2).to_broadcast([P, KT, P])
                    chain(nc.vector.tensor_tensor(g.xnT[:, :, t * P:(t + 1) * P], turned[:, t % 2, :, :], gain, ALU.mult),
                          xT_taken)

                for t in range(NT):
                    dve.wait_ge(sq_ready, t + 1)
                    chain(nc.vector.tensor_scalar(rstd[:, t:t + 1], ss[:, t:t + 1], 1.0 / D, EPS, ALU.mult, ALU.add))
                    chain(nc.vector.reciprocal(rstd[:, t:t + 1], rstd[:, t:t + 1]), mean_ready)
                    if t:
                        take(t - 1)
                    dve.wait_ge(rstd_ready, t + 1)
                    chain(nc.vector.tensor_scalar(tile(t), tile(t), rstd[:, t:t + 1], None, ALU.mult), xs_ready)
                take(NT - 1)


def forget_gates(nc, g):
    with ExitStack() as ctx:
        sb = lambda name, shape, dt=F32: ctx.enter_context(nc.sbuf_tensor(name, shape, dt))
        w_f = sb("w_f", [P, KT, HEADS])
        past_lf = sb("past_lf", [P, PAST_TILES, HEADS])
        b_f = sb("b_f_all", [P, HEADS])
        z, e, lf, s, s2, acc = (sb(n, [P, NT * HEADS + KT]) for n in ("fz", "fe", "flf", "fs", "fs2", "facc"))
        ones_row = sb("ones_row", [HEADS, PAST])
        neg_c_p, neg_c_s = sb("neg_c_p", [HEADS, T_PROMPT]), sb("neg_c_s", [HEADS, KV_SAMPLE])
        f_ps = ctx.enter_context(nc.psum_tensor("f_ps", [P, BANK], F32))
        new_ps = ctx.enter_context(nc.psum_tensor("new_ps", [HEADS, 3 * BANK], F32))
        past_ps = ctx.enter_context(nc.psum_tensor("past_ps", [HEADS, PAST], F32))
        sem = g.sem
        f_loaded, f_ready, e_asked, e_ready = sem("f_loaded"), sem("f_ready"), sem("e_asked"), sem("e_ready")
        past_ready, lf_ready, new_ready, chain_v, lf_stored = sem("past_ready"), sem("lf_ready"), sem("new_ready"), sem("f_chain_v"), sem("lf_stored")
        sums_ready = sem("sums_ready")
        F = NT * HEADS

        with nc.Block() as block:
            @block.sync
            def _(sp):
                sp.dma_start(w_f[:, :, :], g.w_in_k[:, :, COL_F:COL_F + HEADS]).then_inc(f_loaded, 16)
                sp.dma_start(past_lf[:, :, :], g.cache_logf[0, 0].rearrange("(t p) h -> p t h", p=P)).then_inc(f_loaded, 16)
                sp.dma_start(b_f[:, :], row(g.b_f[0]).to_broadcast([P, HEADS])).then_inc(f_loaded, 16)
                sp.wait_ge(lf_ready, 1)
                sp.dma_start(g.out_lf_p[0, 0].rearrange("(t p) h -> p t h", p=P),
                             lf[:, 0:PT * HEADS].rearrange("p (t h) -> p t h", h=HEADS)).then_inc(lf_stored, 16)
                sp.dma_start(g.out_lf_s[0, 0], lf[0:T_SAMPLE, PT * HEADS:F]).then_inc(lf_stored, 16)
                sp.wait_ge(sums_ready, 1)
                sp.dma_start(g.neg_c_new[:, 0:T_PROMPT], neg_c_p[:, :]).then_inc(lf_stored, 16)
                sp.dma_start(g.neg_c_new[:, T_PROMPT:T_ALL], neg_c_s[:, PAST:KV_SAMPLE]).then_inc(lf_stored, 16)
                sp.dma_start(g.neg_c_past[:, :], neg_c_s[:, 0:PAST]).then_inc(lf_stored, 16)
                sp.wait_ge(lf_stored, 80)

            @block.tensor
            def _(pe):
                pe.wait_ge(f_loaded, 48)
                for t in range(NT):
                    for k in range(KT):
                        last = nc.tensor.matmul(f_ps[:, t * HEADS:(t + 1) * HEADS], g.xnT[:, k, t * P:(t + 1) * P],
                                                w_f[:, k, :], start=(k == 0), stop=(k == KT - 1))
                last.then_inc(f_ready, 1)
                for t in range(PAST_TILES):
                    last = nc.tensor.transpose(past_ps[:, t * P:(t + 1) * P], past_lf[:, t, :], g.ident[:, :])
                last.then_inc(past_ready, 1)
                pe.wait_ge(lf_ready, 1)
                for t in range(NT):
                    last = nc.tensor.transpose(new_ps[:, t * P:(t + 1) * P], lf[:, t * HEADS:(t + 1) * HEADS], g.ident[:, :])
                last.then_inc(new_ready, 1)

            @block.scalar
            def _(act):
                act.wait_ge(e_asked, 1)
                nc.scalar.activation(e[:, :], e[:, :], ACT.Exp).then_inc(e_ready, 1)

            @block.vector
            def _(dve):
                v, chain = nc.vector, Chain(dve, chain_v)
                dve.wait_ge(f_loaded, 48)
                chain(v.memset(ones_row[:, :], 1.0))
                chain(v.memset(g.qkT[HD:HD + 1, 0:2, :], 1.0))
                dve.wait_ge(f_ready, 1)
                chain(v.tensor_tensor(z[:, 0:F].rearrange("p (t h) -> p t h", h=HEADS),
                                      f_ps[:, 0:F].rearrange("p (t h) -> p t h", h=HEADS),
                                      b_f[:, :].unsqueeze(1).to_broadcast([P, NT, HEADS]), ALU.add))
                chain(v.tensor_copy(z[:, F:F + KT], g.chan[:, V_LAM * KT:(V_LAM + 1) * KT]))
                chain(v.tensor_scalar(e[:, :], z[:, :], -1.0, None, ALU.mult))
                chain(v.tensor_tensor(e[:, :], e[:, :], z[:, :], ALU.min), e_asked)
                dve.wait_ge(e_ready, 1)
                log1p_steps(nc, chain, lf[:, :], e[:, :], s[:, :], s2[:, :], acc[:, :])
                chain(v.tensor_scalar(z[:, :], z[:, :], 0.0, None, ALU.min))
                chain(v.tensor_tensor(lf[:, :], z[:, :], lf[:, :], ALU.subtract), lf_ready)
                chain(v.tensor_scalar(g.decay[:, :], lf[:, F:F + KT], LRU_C, None, ALU.mult))
                dve.wait_ge(past_ready, 1)
                chain(v.tensor_tensor_scan(neg_c_s[:, 0:PAST], ones_row[:, :], past_ps[:, :], 0.0, ALU.mult, ALU.subtract))
                dve.wait_ge(new_ready, 1)
                chain(v.tensor_tensor_scan(neg_c_p[:, :], ones_row[:, 0:T_PROMPT], new_ps[:, 0:T_PROMPT], 0.0,
                                           ALU.mult, ALU.subtract))
                chain(v.tensor_tensor_scan(neg_c_s[:, PAST:KV_SAMPLE], ones_row[:, 0:T_SAMPLE],
                                           new_ps[:, T_PROMPT:T_ALL], neg_c_s[:, PAST - 1:PAST], ALU.mult, ALU.subtract),
                      sums_ready)


def recurrent(nc, g, yT):
    GATE_UNITS = 2 * len(CHUNKS)
    with ExitStack() as ctx:
        sb = lambda name, shape, dt=F32: ctx.enter_context(nc.sbuf_tensor(name, shape, dt))
        w_x = [sb(f"r_wx{u}", [P, KT, P]) for u in range(2)]
        w_g = [sb(f"r_wg{u}", [P, KT, P]) for u in range(2)]
        bd = [sb(f"r_bd{u}", [P, 2, P]) for u in range(2)]
        H = CONV_W - 1
        conv_in = sb("conv_in", [P, H + T_PROMPT + H + T_SAMPLE])
        u_sb, r_sb, i_sb, a_sb, th_sb, v_sb, gel, h_sb = (sb(n, [P, T_ALL]) for n in
                                                         ("u_sb", "r_sb", "i_sb", "a_sb", "th_sb", "v_sb", "gel", "h_sb"))
        tails = sb("tails", [P, 2 * H + 2, KT])
        tails_T = sb("tails_T", [P, P])
        ux_ps = ctx.enter_context(nc.psum_tensor("ux_ps", [P, 3 * BANK], F32))
        ug_ps = ctx.enter_context(nc.psum_tensor("ug_ps", [P, 3 * BANK], F32))
        gate_ps = ctx.enter_context(nc.psum_tensor("gate_ps", [P, 2, BANK], F32))
        sem = g.sem
        w_loaded = [sem(f"rw_loaded{u}") for u in range(2)]
        bd_cleared, w_used = sem("bd_cleared"), sem("rw_used")
        ux_ready, ug_ready, conv_ready = sem("ux_ready"), sem("ug_ready"), sem("conv_in_ready")
        u_ready, gate_ready, gate_taken = sem("u_ready"), sem("gate_ready"), sem("gate_taken")
        ri_ready, at_ready, gel_ready, var_ready, std_ready, step_done = (sem("ri_ready"), sem("at_ready"), sem("gel_ready"),
                                                                          sem("var_ready"), sem("std_ready"), sem("step_done"))
        chain_v, chain_a, chain_e = sem("r_chain_v"), sem("r_chain_a"), sem("r_chain_e")
        tails_ready, tails_turned, tails_kept, tails_stored = sem("tails_ready"), sem("tails_turned"), sem("tails_kept"), sem("tails_stored")
        LOADS = 6 * 16
        V_STEPS, A_STEPS = 19, 13

        with nc.Block() as block:
            @block.sync
            def _(sp):
                sp.wait_ge(bd_cleared, 1)
                with sp.Fori(0, KT // 2) as i:
                    for u in range(2):
                        c = i * 2 + u
                        sp.wait_ge(w_used, c + 1)
                        sp.dma_start(w_x[u][:, :, :], g.w_in_k[:, :, bass.ds(c * P + COL_X, P)]).then_inc(w_loaded[u], 16)
                        for n, w in enumerate((g.w_a, g.w_x)):
                            for h in range(2):
                                sp.dma_start(bd[u][h * 64:(h + 1) * 64, n, h * 64:(h + 1) * 64],
                                             w[0, bass.ds(c * 2 + h, 1)].rearrange("o i j -> (o i) j")).then_inc(w_loaded[u], 16)
                        sp.dma_start(w_g[u][:, :, :], g.w_in_k[:, :, bass.ds(c * P + COL_G, P)]).then_inc(w_loaded[u], 16)
                sp.wait_ge(tails_kept, 1)
                last_rows = lambda out: out[0, 0].rearrange("j (c p) -> (j c) p", p=P)
                one_row = lambda out: out[0, 0:1].rearrange("o (c p) -> (o c) p", p=P)
                sp.dma_start(last_rows(g.out_conv_p), tails_T[0:H * KT, :]).then_inc(tails_stored, 16)
                sp.dma_start(last_rows(g.out_conv_s), tails_T[H * KT:2 * H * KT, :]).then_inc(tails_stored, 16)
                sp.dma_start(one_row(g.out_h_p), tails_T[2 * H * KT:(2 * H + 1) * KT, :]).then_inc(tails_stored, 16)
                sp.dma_start(one_row(g.out_h_s), tails_T[(2 * H + 1) * KT:(2 * H + 2) * KT, :]).then_inc(tails_stored, 16)
                sp.wait_ge(tails_stored, 64)

            @block.tensor
            def _(pe):
                pe.sem_inc(w_used, 2)
                with pe.Fori(0, KT // 2) as i:
                    for u in range(2):
                        c = i * 2 + u
                        pe.wait_ge(w_loaded[u], i * LOADS + LOADS)
                        pe.wait_ge(conv_ready, c)
                        for c0, n in CHUNKS:
                            for k in range(KT):
                                last = nc.tensor.matmul(ux_ps[:, c0:c0 + n], w_x[u][:, k, :], g.xnT[:, k, c0:c0 + n],
                                                        start=(k == 0), stop=(k == KT - 1))
                        last.then_inc(ux_ready, 1)
                        pe.wait_ge(gel_ready, c)
                        for c0, n in CHUNKS:
                            for k in range(KT):
                                last = nc.tensor.matmul(ug_ps[:, c0:c0 + n], w_g[u][:, k, :], g.xnT[:, k, c0:c0 + n],
                                                        start=(k == 0), stop=(k == KT - 1))
                        last.then_inc(ug_ready, 1)
                        pe.wait_ge(u_ready, c + 1)
                        for m in range(GATE_UNITS):
                            c0, n = CHUNKS[m % 3]
                            if m >= 2:
                                pe.wait_ge(gate_taken, c * GATE_UNITS + m - 1)
                            else:
                                pe.wait_ge(gate_taken, c * GATE_UNITS)
                            last = nc.tensor.matmul(gate_ps[:, m % 2, 0:n], bd[u][:, m // 3, :], u_sb[:, c0:c0 + n],
                                                    start=True, stop=True)
                            last.then_inc(gate_ready, 1)
                        pe.wait_ge(gate_ready, c * GATE_UNITS + GATE_UNITS)
                        pe.sem_inc(w_used, 1)
                pe.wait_ge(tails_ready, 1)
                nc.tensor.transpose(ux_ps[0:(2 * H + 2) * KT, 0:P], tails[:, :, :].rearrange("p j c -> p (j c)"),
                                    g.ident[:, :]).then_inc(tails_turned, 1)

            @block.scalar
            def _(act):
                with act.Fori(0, KT // 2) as i:
                    for u in range(2):
                        c = i * 2 + u
                        chain = Chain(act, chain_a, c * A_STEPS)
                        vec = lambda v: g.chan[:, bass.ds(c + v * KT, 1)]
                        act.wait_ge(ux_ready, c + 1)
                        act.wait_ge(u_ready, c)
                        chain(nc.scalar.copy(conv_in[:, H:H + T_PROMPT], ux_ps[:, 0:T_PROMPT]))
                        chain(nc.scalar.copy(conv_in[:, 2 * H + T_PROMPT:], ux_ps[:, T_PROMPT:T_ALL]))
                        for j in range(H):
                            at = H + T_PROMPT + j
                            chain(nc.scalar.copy(conv_in[:, at:at + 1], vec(V_HIST + j)), conv_ready if j == H - 1 else None)
                        for m in range(GATE_UNITS):
                            c0, n = CHUNKS[m % 3]
                            act.wait_ge(gate_ready, c * GATE_UNITS + m + 1)
                            if m == 0:
                                act.wait_ge(step_done, c)
                            dst = (r_sb, i_sb)[m // 3]
                            alone(act, g)
                            chain(nc.scalar.activation(dst[:, c0:c0 + n], gate_ps[:, m % 2, 0:n], ACT.Sigmoid,
                                                       bias=vec(V_BA + m // 3)), gate_taken)
                        act.sem_inc(ri_ready, 1)
                        lam = g.decay[:, bass.ds(c, 1)]
                        alone(act, g)
                        nc.scalar.activation(a_sb[:, :], r_sb[:, :], ACT.Exp, scale=lam).then_inc(at_ready, 1)
                        nc.scalar.activation(th_sb[:, :], r_sb[:, :], ACT.Tanh, scale=lam).then_inc(at_ready, 1)
                        act.wait_ge(at_ready, c * 2 + 2)
                        act.wait_ge(ug_ready, c + 1)
                        chain(nc.scalar.activation(gel[:, :], ug_ps[:, 0:T_ALL], ACT.Gelu_apprx_tanh), gel_ready)
                        act.wait_ge(var_ready, c + 1)
                        chain(nc.scalar.activation(v_sb[:, :], v_sb[:, :], ACT.Sqrt, scale=-1.0), std_ready)
                        chain.ended(A_STEPS)

            @block.vector
            def _(dve):
                v = nc.vector
                edge = Chain(dve, chain_e)
                for u in range(2):
                    edge(v.memset(bd[u][:, :, :], 0.0), bd_cleared if u else None)
                edge(v.memset(conv_in[:, 0:H], 0.0))
                with dve.Fori(0, KT // 2) as i:
                    for u in range(2):
                        c = i * 2 + u
                        chain = Chain(dve, chain_v, c * V_STEPS)
                        vec = lambda k: g.chan[:, bass.ds(c + k * KT, 1)]
                        dve.wait_ge(conv_ready, c + 1)
                        parts = ((0, T_PROMPT, 0), (T_PROMPT, T_SAMPLE, H + T_PROMPT))
                        for dst, n, src in parts:
                            chain(v.tensor_scalar(u_sb[:, dst:dst + n], conv_in[:, src + H:src + H + n], vec(V_CONV + H),
                                                  vec(V_CONVB), ALU.mult, ALU.add))
                        for j in range(H):
                            for dst, n, src in parts:
                                chain(v.scalar_tensor_tensor(u_sb[:, dst:dst + n], conv_in[:, src + j:src + j + n],
                                                             vec(V_CONV + j), u_sb[:, dst:dst + n], ALU.mult, ALU.add))
                        chain(v.tensor_copy(tails[:, 0:H, bass.ds(c, 1)].rearrange("p j o -> p (j o)"), conv_in[:, T_PROMPT:T_PROMPT + H]))
                        end = H + T_PROMPT + T_SAMPLE
                        chain(v.tensor_copy(tails[:, H:2 * H, bass.ds(c, 1)].rearrange("p j o -> p (j o)"), conv_in[:, end:end + H]), u_ready)
                        dve.wait_ge(ri_ready, c + 1)
                        chain(v.tensor_tensor(i_sb[:, :], i_sb[:, :], u_sb[:, :], ALU.mult))
                        dve.wait_ge(at_ready, c * 2 + 2)
                        chain(v.tensor_tensor(v_sb[:, :], a_sb[:, :], a_sb[:, :], ALU.mult))
                        chain(v.scalar_tensor_tensor(v_sb[:, :], v_sb[:, :], 1.0, th_sb[:, :], ALU.add, ALU.mult), var_ready)
                        dve.wait_ge(std_ready, c + 1)
                        chain(v.tensor_tensor(i_sb[:, :], i_sb[:, :], v_sb[:, :], ALU.mult))
                        chain(v.tensor_tensor_scan(h_sb[:, 0:T_PROMPT], a_sb[:, 0:T_PROMPT], i_sb[:, 0:T_PROMPT], 0.0,
                                                   ALU.mult, ALU.add))
                        chain(v.tensor_tensor_scan(h_sb[:, T_PROMPT:T_ALL], a_sb[:, T_PROMPT:T_ALL], i_sb[:, T_PROMPT:T_ALL],
                                                   vec(V_H0), ALU.mult, ALU.add))
                        for n, at in enumerate((T_PROMPT - 1, T_ALL - 1)):
                            chain(v.tensor_copy(tails[:, 2 * H + n, bass.ds(c, 1)], h_sb[:, at:at + 1]))
                        dve.wait_ge(gel_ready, c + 1)
                        chain(v.tensor_tensor(yT[:, bass.ds(c, 1), 0:T_ALL].rearrange("p o t -> p (o t)"), gel[:, :], h_sb[:, :],
                                              ALU.mult), step_done)
                        chain.ended(V_STEPS)
                dve.sem_inc(tails_ready, 1)
                dve.wait_ge(tails_turned, 1)
                edge(v.tensor_copy(tails_T[0:(2 * H + 2) * KT, :], ux_ps[0:(2 * H + 2) * KT, 0:P]), tails_kept)


def project(nc, g, branch, w_out, gate_col, add, tag):
    with ExitStack() as ctx:
        sb = lambda name, shape, dt=F32: ctx.enter_context(nc.sbuf_tensor(tag + name, shape, dt))
        w_p = [sb(f"_wp{u}", [P, KT, P]) for u in range(2)]
        w_g = [sb(f"_wg{u}", [P, KT, P]) for u in range(2)]
        sig = sb("_sig", [P, T_ALL])
        gate_ps = ctx.enter_context(nc.psum_tensor(tag + "_gate_ps", [P, 3 * BANK], F32))
        proj_ps = ctx.enter_context(nc.psum_tensor(tag + "_proj_ps", [P, 3 * BANK], F32))
        sem = lambda name: g.sem(f"{tag}_{name}")
        w_loaded = [sem(f"w_loaded{u}") for u in range(2)]
        w_used, gate_ready, proj_ready, sig_ready, proj_taken, chain_v = (sem("w_used"), sem("gate_ready"), sem("proj_ready"),
                                                                          sem("sig_ready"), sem("proj_taken"), sem("chain_v"))
        V_STEPS = 2 if add else 1
        w_out_k = w_out[0].rearrange("(k p) n -> p k n", p=P)

        with nc.Block() as block:
            @block.sync
            def _(sp):
                with sp.Fori(0, KT // 2) as i:
                    for u in range(2):
                        c = i * 2 + u
                        sp.wait_ge(w_used, c + 1)
                        sp.dma_start(w_g[u][:, :, :], g.w_in_k[:, :, bass.ds(c * P + gate_col, P)]).then_inc(w_loaded[u], 16)
                        sp.dma_start(w_p[u][:, :, :], w_out_k[:, :, bass.ds(c * P, P)]).then_inc(w_loaded[u], 16)

            @block.tensor
            def _(pe):
                pe.sem_inc(w_used, 2)
                with pe.Fori(0, KT // 2) as i:
                    for u in range(2):
                        c = i * 2 + u
                        pe.wait_ge(w_loaded[u], i * 32 + 32)
                        pe.wait_ge(sig_ready, c)
                        for c0, n in CHUNKS:
                            for k in range(KT):
                                last = nc.tensor.matmul(gate_ps[:, c0:c0 + n], w_g[u][:, k, :], g.xnT[:, k, c0:c0 + n],
                                                        start=(k == 0), stop=(k == KT - 1))
                        last.then_inc(gate_ready, 1)
                        pe.wait_ge(proj_taken, c)
                        for c0, n in CHUNKS:
                            for k in range(KT):
                                last = nc.tensor.matmul(proj_ps[:, c0:c0 + n], w_p[u][:, k, :], branch[:, k, c0:c0 + n],
                                                        start=(k == 0), stop=(k == KT - 1))
                        last.then_inc(proj_ready, 1)
                        pe.wait_ge(proj_ready, c + 1)
                        pe.sem_inc(w_used, 1)

            @block.scalar
            def _(act):
                with act.Fori(0, KT) as c:
                    act.wait_ge(gate_ready, c + 1)
                    act.wait_ge(proj_taken, c)
                    nc.scalar.activation(sig[:, :], gate_ps[:, 0:T_ALL], ACT.Sigmoid).then_inc(sig_ready, 1)

            @block.vector
            def _(dve):
                with dve.Fori(0, KT) as c:
                    chain = Chain(dve, chain_v, c * V_STEPS)
                    dve.wait_ge(proj_ready, c + 1)
                    dve.wait_ge(sig_ready, c + 1)
                    m = g.mT[:, bass.ds(c, 1), 0:T_ALL].rearrange("p o t -> p (o t)")
                    if add:
                        chain(nc.vector.tensor_tensor(sig[:, :], sig[:, :], proj_ps[:, 0:T_ALL], ALU.mult))
                        chain(nc.vector.tensor_tensor(m, m, sig[:, :], ALU.add), proj_taken)
                    else:
                        chain(nc.vector.tensor_tensor(m, sig[:, :], proj_ps[:, 0:T_ALL], ALU.mult), proj_taken)
                    chain.ended(V_STEPS)


def attend(nc, g, attnT):
    QKV = 3 * P
    UNITS = [(n % 2, n // 2) for n in range(2 * PT)] + ["stream"]
    NU = len(UNITS)
    STREAM = NU - 1
    tiles_of = lambda n: PAST_TILES + 1 if n == STREAM else UNITS[n][1] + 1
    groups_of = lambda n: [list(range(j, min(j + 4, tiles_of(n)))) for j in range(0, tiles_of(n), 4)]
    NG = sum(len(groups_of(n)) for n in range(NU))
    first_group = lambda n: sum(len(groups_of(m)) for m in range(n))
    end_group = lambda n: first_group(n) + len(groups_of(n))
    owner = [(n, js) for n in range(NU) for js in groups_of(n)]
    PAST_TURNS = 2 * PAST_TILES // 4
    HALVES_AT = (0, 0, 1, 1, 2, 2, 3, 4, 5, 6, 7, 8, 9, 10, 11, 12, 13, 14)
    PROJECTED_AT = HALVES_AT[1::2]
    PAST_AT = (5, 7, 8, 9, 11, 12, 13, 14)
    assert len(HALVES_AT) == 2 * NT and len(PAST_AT) == PAST_TURNS
    O_TURNS = PT // 4 + 1
    NORM_PARTS = 3
    FIRST_O = 2 * PT // 2 + 2
    TAKE_QK_ACT = 4

    def turns_of(ahead):
        order = []
        for n in range(STREAM):
            if n in PAST_AT:
                order.append(("past", PAST_AT.index(n)))
            if n == FIRST_O:
                order.append(("o", 0))
            order += [("p", q) for q in range(first_group(n), end_group(n))]
        if ahead:
            order += [("qk", t) for t in range(NT)]
        order += [("p", first_group(STREAM)), ("o", 1)]
        order += [("p", q) for q in range(first_group(STREAM) + 1, NG)] + [("o", 2)]
        return {use: m for m, use in enumerate(order)}

    TURNS, TURNS_LAST = turns_of(True), turns_of(False)
    USES = len(TURNS)
    in_bank = lambda m, b: (m + 1 - b) // 2

    with ExitStack() as ctx:
        sb = lambda name, shape, dt=F32: ctx.enter_context(nc.sbuf_tensor(name, shape, dt))
        w_qkv = sb("w_qkv", [P, KT, QKV])
        gain = sb("qk_gain", [P, 4, HD])
        qk_sb = sb("qk_sb", [P, NT, 4, HD])
        v_next, v_new = sb("v_next", [P, NT, P]), sb("v_new", [P, NT, P])
        squares = sb("qk_squares", [P, 2, 4, HD])
        rstd = sb("qk_rstd", [P, NT, 4])
        qkT, spare = g.qkT, g.mT[:, :, :].rearrange("p k t -> p (k t)")
        kT_past = spare[0:HD + 1, 0:2 * PAST].rearrange("p (h t) -> p h t", h=2)
        k_past, v_past = (spare[:, 2 * PAST + n * PAST:3 * PAST + n * PAST].rearrange("p (t d) -> p t d", d=P) for n in range(2))
        o_sb = spare[:, 4 * PAST:4 * PAST + PT * P].rearrange("p (t d) -> p t d", d=P)
        probs_s = sb("probs_s", [P, KV_SAMPLE])
        probs = [probs_s[:, b * T_PROMPT:(b + 1) * T_PROMPT] for b in range(2)]
        probsT = [sb(f"probsT{b}", [P, BANK]) for b in range(2)]
        neg_max, total = sb("neg_max", [P, NU + 1]), sb("exp_total", [P, NU + 1])
        o_s = sb("o_s", [P, P])
        scores = ctx.enter_context(nc.psum_tensor("scores", [P, 4 * BANK], F32))
        turn_ps = ctx.enter_context(nc.psum_tensor("turn_ps", [P, 2, BANK], F32))
        out_ps = ctx.enter_context(nc.psum_tensor("out_ps", [P, BANK], F32))
        proj_ps = ctx.enter_context(nc.psum_tensor("proj_ps", [P, BANK], F32))
        tail = proj_ps[:, 0:T_SAMPLE]
        half = lambda n: scores[:, (n % 2) * 2 * BANK:(n % 2 + 1) * 2 * BANK]

        sem = lambda name: g.sem("a_" + name)
        gain_loaded, w_loaded, past_k_loaded, past_v_loaded, c_loaded = (sem("gain_loaded"), sem("w_loaded"), sem("k_loaded"),
                                                                         sem("v_loaded"), sem("c_loaded"))
        kv_ready, kv_stored, v_copied = sem("kv_ready"), sem("kv_stored"), sem("v_copied")
        qkv_ready, tile_taken, sq_summed = sem("qkv_ready"), sem("tile_taken"), sem("sq_summed")
        mean_ready, rstd_ready = sem("mean_ready"), sem("rstd_ready")
        turned = sem("turned")
        turn_taken = [sem(f"turn_taken{b}") for b in range(2)]
        scores_ready, max_ready, exp_ready = sem("scores_ready"), sem("max_ready"), sem("exp_ready")
        pv_done, out_taken = sem("pv_done"), sem("out_taken")
        chain_v, chain_a, chain_g = sem("chain_v"), sem("chain_a"), sem("chain_g")
        turned_count = lambda i, m: NT + i * USES + m + 1
        taken_before = lambda i, m: in_bank(NT, m % 2) + i * in_bank(USES, m % 2) + m // 2

        with nc.Block() as block:
            @block.sync
            def _(sp):
                for n, vec in enumerate((g.q_norm_g, g.q_norm_g, g.k_norm_g, g.k_norm_g)):
                    sp.dma_start(gain[:, n, :], row(vec[0]).to_broadcast([P, HD])).then_inc(gain_loaded, 16)
                heads = lambda ap, p: ap.rearrange("(t p) h d -> p t (h d)", p=P)[:, :, bass.ds(p * P, P)]

                def load_w(p):
                    for n, col in enumerate((COL_Q, COL_K, COL_V)):
                        sp.dma_start(w_qkv[:, :, n * P:(n + 1) * P], g.w_in_k[:, :, bass.ds(p * P + col, P)]).then_inc(w_loaded, 16)

                def load_past_k(p):
                    sp.dma_start(k_past[:, :, :], heads(g.cache_k[0, 0], p)).then_inc(past_k_loaded, 16)

                def store_kv(p):
                    sp.wait_ge(kv_ready, p + 1)
                    sp.dma_start(heads(g.out_k_p[0, 0], p), qk_sb[:, 0:PT, 2:4, :].rearrange("p t h d -> p t (h d)")).then_inc(kv_stored, 16)
                    sp.dma_start(heads(g.out_v_p[0, 0], p), v_next[:, 0:PT, :]).then_inc(kv_stored, 16)
                    stream = lambda ap: ap.rearrange("t h d -> t (h d)")[:, bass.ds(p * P, P)]
                    sp.dma_start(stream(g.out_k_s[0, 0]), qk_sb[0:T_SAMPLE, PT, 2:4, :].rearrange("p h d -> p (h d)")).then_inc(kv_stored, 16)
                    sp.dma_start(stream(g.out_v_s[0, 0]), v_next[0:T_SAMPLE, PT, :]).then_inc(kv_stored, 16)

                def past_turned(i):
                    sp.wait_ge(turned, turned_count(i, TURNS["past", PAST_TURNS - 1]))

                load_w(0)
                load_past_k(0)
                store_kv(0)
                load_w(1)
                with sp.Fori(0, PAIRS - 2) as i:
                    store_kv(i + 1)
                    load_w(i + 2)
                    past_turned(i)
                    load_past_k(i + 1)
                store_kv(PAIRS - 1)
                past_turned(PAIRS - 2)
                load_past_k(PAIRS - 1)
                sp.wait_ge(kv_stored, PAIRS * 64)

            @block.gpsimd
            def _(pool):
                def load_c(p):
                    pool.dma_start(qkT[HD:HD + 1, 2:4, 0:T_ALL], g.neg_c_new[bass.ds(p * 2, 2), :].unsqueeze(0)).then_inc(c_loaded, 16)
                    pool.dma_start(kT_past[HD:HD + 1, :, :], g.neg_c_past[bass.ds(p * 2, 2), :].unsqueeze(0)).then_inc(c_loaded, 16)

                def take_v(p):
                    pool.wait_ge(kv_ready, p + 1)
                    alone(pool, g)
                    nc.gpsimd.tensor_copy(v_new[:, :, :], v_next[:, :, :]).then_inc(v_copied, 1)

                def load_past_v(p):
                    pool.dma_start(v_past[:, :, :], g.cache_v[0, 0].rearrange("(t p) h d -> p t (h d)", p=P)[:, :, bass.ds(p * P, P)])\
                        .then_inc(past_v_loaded, 16)

                load_c(0)
                load_past_v(0)
                take_v(0)
                with pool.Fori(0, PAIRS - 1) as i:
                    pool.wait_ge(scores_ready, (i + 1) * NU)
                    load_c(i + 1)
                    pool.wait_ge(pv_done, (i + 1) * NG)
                    take_v(i + 1)
                    load_past_v(i + 1)

            @block.tensor
            def _(pe):
                te = nc.tensor

                def project_half(t, part, acc):
                    for k in range(part * KT // 2, (part + 1) * KT // 2):
                        last = te.matmul(acc[:, 0:QKV], g.xnT[:, k, t * P:(t + 1) * P], w_qkv[:, k, :],
                                         start=(k == 0), stop=(k == KT - 1))
                    if part:
                        last.then_inc(qkv_ready, 1)

                def turn_qk(t, bank):
                    for n in range(4):
                        last = te.transpose(turn_ps[0:HD, bank, n * P:(n + 1) * P], qk_sb[:, t, n, :], g.ident[:, :])
                    last.then_inc(turned, 1)

                pe.wait_ge(w_loaded, 48)
                for t in range(NT):
                    if t >= 2:
                        pe.wait_ge(tile_taken, 3 * (t - 1))
                    for part in range(2):
                        project_half(t, part, (proj_ps, out_ps)[t % 2])
                pe.wait_ge(kv_ready, 1)
                for t in range(NT):
                    if t >= 2:
                        pe.wait_ge(turn_taken[t % 2], t // 2)
                    turn_qk(t, t % 2)

                def step(i, ahead):
                    use = TURNS if ahead else TURNS_LAST

                    def bank_of(*which):
                        m = use[which]
                        pe.wait_ge(turn_taken[m % 2], taken_before(i, m))
                        return m % 2

                    def score(n):
                        if n == STREAM:
                            pe.wait_ge(exp_ready, i * NU + n)
                            b = use["past", PAST_TURNS - 1]
                            for m in (b - 1, b):
                                pe.wait_ge(turn_taken[m % 2], taken_before(i, m) + 1)
                            for c in range(PAST // BANK):
                                for h in range(2):
                                    te.matmul(scores[h * 64:(h + 1) * 64, c * BANK:(c + 1) * BANK],
                                              qkT[:, h, T_PROMPT:T_ALL], kT_past[:, h, c * BANK:(c + 1) * BANK],
                                              start=True, stop=True)
                            for h in range(2):
                                te.matmul(tail[h * 64:(h + 1) * 64, :], qkT[:, h, T_PROMPT:T_ALL],
                                          qkT[:, 2 + h, T_PROMPT:T_ALL], start=True, stop=False, skip_group_check=True)
                            te.matmul(tail, g.ident_bf[:, :], g.causal_s[:, :], start=False, stop=True,
                                      skip_group_check=True).then_inc(scores_ready, 1)
                            return
                        h, t = UNITS[n]
                        if n >= 2:
                            pe.wait_ge(exp_ready, i * NU + n - 1)
                        for c0 in range(0, (t + 1) * P, BANK):
                            w = min(BANK, (t + 1) * P - c0)
                            diagonal = c0 + w == (t + 1) * P
                            te.matmul(half(n)[:, c0:c0 + w], qkT[:, h, t * P:(t + 1) * P], qkT[:, 2 + h, c0:c0 + w],
                                      start=True, stop=not diagonal)
                        te.matmul(half(n)[:, t * P:(t + 1) * P], g.ident_bf[:, :], g.causal[:, :],
                                  start=False, stop=True).then_inc(scores_ready, 1)

                    def turn_past(s):
                        h, c = s // (PAST_TILES // 4), s % (PAST_TILES // 4)
                        if s == 0:
                            pe.wait_ge(past_k_loaded, i * 16 + 16)
                        bank = bank_of("past", s)
                        alone(pe, g)
                        for n in range(4):
                            last = te.transpose(turn_ps[0:HD, bank, n * P:(n + 1) * P],
                                                k_past[:, c * 4 + n, h * HD:(h + 1) * HD], g.ident[:, :])
                        last.then_inc(turned, 1)

                    def turn_group(q):
                        n, js = owner[q]
                        bank = bank_of("p", q)
                        if js[0] == PAST_TILES:
                            alone(pe, g)
                        src = probs_s if n == STREAM else probs[n % 2]
                        for s, j in enumerate(js):
                            w = T_SAMPLE if j == PAST_TILES else P
                            last = te.transpose(turn_ps[0:w, bank, s * P:(s + 1) * P], src[:, j * P:j * P + w], g.ident[:, :])
                        last.then_inc(turned, 1)

                    def weigh_group(q):
                        n, js = owner[q]
                        m = use["p", q]
                        pe.wait_ge(turn_taken[m % 2], taken_before(i, m) + 1)
                        if q == 0:
                            pe.wait_ge(v_copied, i + 1)
                        elif js[0] == 0:
                            pe.wait_ge(out_taken, i * NU + n)
                        for s, j in enumerate(js):
                            flags = dict(start=(j == 0), stop=(j == tiles_of(n) - 1))
                            pt = probsT[q % 2][:, s * P:(s + 1) * P]
                            if n == STREAM and j == PAST_TILES:
                                last = te.matmul(out_ps[:, 0:P], pt[0:T_SAMPLE, :], v_new[0:T_SAMPLE, PT, :], **flags)
                            elif n == STREAM:
                                last = te.matmul(out_ps[:, 0:P], pt, v_past[:, j, :], **flags)
                            else:
                                h = UNITS[n][0]
                                last = te.matmul(out_ps[:, 0:HD], pt, v_new[:, j, h * HD:(h + 1) * HD], **flags)
                        last.then_inc(pv_done, 1)

                    def turn_out(s):
                        pe.wait_ge(out_taken, i * NU + (s + 1) * 8)
                        bank = bank_of("o", s)
                        for n in range(4):
                            last = te.transpose(turn_ps[:, bank, n * P:(n + 1) * P], o_sb[:, s * 4 + n, :], g.ident[:, :])
                        last.then_inc(turned, 1)

                    pe.wait_ge(c_loaded, i * 32 + 32)
                    for b in range(2):
                        pe.wait_ge(turn_taken[b], taken_before(i, b))
                    score(0)
                    for n in range(STREAM):
                        if n + 1 < STREAM:
                            score(n + 1)
                        if n:
                            weigh_group(first_group(n) - 1)
                        for x, at in enumerate(HALVES_AT):
                            if not ahead or at != n:
                                continue
                            if x == 0:
                                pe.wait_ge(w_loaded, i * 48 + 96)
                            elif x % 2 == 0:
                                pe.wait_ge(tile_taken, 3 * ((i + 1) * NT + x // 2))
                            project_half(x // 2, x % 2, proj_ps)
                        if n in PAST_AT:
                            turn_past(PAST_AT.index(n))
                        if n == FIRST_O:
                            turn_out(0)
                        pe.wait_ge(exp_ready, i * NU + n + 1)
                        for q in range(first_group(n), end_group(n)):
                            turn_group(q)
                            if q > first_group(n):
                                weigh_group(q - 1)
                    score(STREAM)
                    weigh_group(first_group(STREAM) - 1)
                    if ahead:
                        pe.wait_ge(kv_ready, i + 2)
                        for t in range(NT):
                            bank = bank_of("qk", t)
                            alone(pe, g)
                            turn_qk(t, bank)
                    pe.wait_ge(exp_ready, (i + 1) * NU)
                    pe.wait_ge(past_v_loaded, i * 16 + 16)
                    for q in range(first_group(STREAM), NG):
                        turn_group(q)
                        if q > first_group(STREAM):
                            weigh_group(q - 1)
                        else:
                            turn_out(1)
                    weigh_group(NG - 1)
                    pe.wait_ge(out_taken, (i + 1) * NU)
                    te.transpose(turn_ps[:, bank_of("o", 2), 0:P], o_s[:, :], g.ident[:, :]).then_inc(turned, 1)

                with pe.Fori(0, PAIRS - 1) as i:
                    step(i, True)
                step(PAIRS - 1, False)

            @block.scalar
            def _(act):
                sc = nc.scalar

                def take_tile(p, t, acc, first=False):
                    act.wait_ge(qkv_ready, p * NT + t + 1)
                    sc.copy(v_next[:, t, :], acc[:, 2 * P:QKV]).then_inc(tile_taken, 1)
                    q_and_k = acc[:, 0:2 * P].rearrange("p (n d) -> p n d", n=4)
                    sc.copy(qk_sb[:, t, :, :], q_and_k).then_inc(tile_taken, 1)
                    if not first or t >= 2:
                        act.wait_ge(sq_summed, p * NT + max(t - 1, 0))
                    sc.activation(squares[:, t % 2, :, :], q_and_k, ACT.Square).then_inc(tile_taken, 1)

                def root(p):
                    act.wait_ge(mean_ready, p + 1)
                    sc.activation(rstd[:, :, :], rstd[:, :, :], ACT.Sqrt).then_inc(rstd_ready, 1)

                def take_qk(chain, t, bank):
                    chain(sc.copy(qkT[0:HD, :, t * P:(t + 1) * P],
                                  turn_ps[0:HD, bank, :].rearrange("p (n c) -> p n c", n=4)), turn_taken[bank])

                A_FIRST = NT
                A_STEPS = TAKE_QK_ACT + PAST_TURNS + NU + 1
                chain = Chain(act, chain_a)
                for t in range(NT):
                    take_tile(0, t, (proj_ps, out_ps)[t % 2], first=True)
                root(0)
                for t in range(NT):
                    act.wait_ge(turned, t + 1)
                    take_qk(chain, t, t % 2)
                chain.ended(A_FIRST)

                def step(i, ahead):
                    use = TURNS if ahead else TURNS_LAST
                    chain = Chain(act, chain_a, i * A_STEPS + A_FIRST)

                    def exp(n):
                        act.wait_ge(max_ready, i * NU + n + 1)
                        if n >= 2:
                            act.wait_ge(turned, turned_count(i, use["p", end_group(n - 1 if n == STREAM else n - 2) - 1]))
                        if n < STREAM:
                            w = (UNITS[n][1] + 1) * P
                            chain(sc.activation(probs[n % 2][:, 0:w], half(n)[:, 0:w], ACT.Exp, bias=neg_max[:, n:n + 1],
                                                accum_out=total[:, n:n + 1]), exp_ready)
                        else:
                            chain(sc.activation(probs_s[:, 0:PAST], scores[:, :], ACT.Exp, bias=neg_max[:, n:n + 1],
                                                accum_out=total[:, n:n + 1]))
                            chain(sc.activation(probs_s[:, PAST:], tail, ACT.Exp, bias=neg_max[:, n:n + 1],
                                                accum_out=total[:, n + 1:n + 2]), exp_ready)

                    if ahead:
                        act.wait_ge(kv_stored, i * 64 + 64)
                        act.wait_ge(v_copied, i + 1)
                    exp(0)
                    for n in range(STREAM):
                        if n + 1 < STREAM:
                            exp(n + 1)
                        if ahead and n in PROJECTED_AT:
                            take_tile(i + 1, PROJECTED_AT.index(n), proj_ps)
                        if n in PAST_AT:
                            s = PAST_AT.index(n)
                            m = use["past", s]
                            h, c = s // (PAST_TILES // 4), s % (PAST_TILES // 4)
                            act.wait_ge(turned, turned_count(i, m))
                            chain(sc.copy(kT_past[0:HD, h, c * BANK:(c + 1) * BANK], turn_ps[0:HD, m % 2, :]), turn_taken[m % 2])
                    if ahead:
                        root(i + 1)
                        for t in range(TAKE_QK_ACT):
                            m = use["qk", t]
                            act.wait_ge(turned, turned_count(i, m))
                            take_qk(chain, t, m % 2)
                    exp(STREAM)
                    if ahead:
                        chain.ended(A_STEPS)

                with act.Fori(0, PAIRS - 1) as i:
                    step(i, True)
                step(PAIRS - 1, False)

            @block.vector
            def _(dve):
                v = nc.vector
                edge = Chain(dve, chain_g)
                dve.wait_ge(gain_loaded, 64)
                edge(v.tensor_scalar(gain[:, 0:2, :], gain[:, 0:2, :], HD ** -0.5, None, ALU.mult))

                def sum_squares(chain, p, t):
                    dve.wait_ge(tile_taken, 3 * (p * NT + t + 1))
                    chain(v.reduce_sum(rstd[:, t, :], squares[:, t % 2, :, :], axis=X_AXIS), sq_summed)

                def mean(chain):
                    chain(v.tensor_scalar(rstd[:, :, :], rstd[:, :, :], 1.0 / HD, EPS, ALU.mult, ALU.add))
                    chain(v.reciprocal(rstd[:, :, :], rstd[:, :, :]), mean_ready)

                def norm_part(chain, p, s):
                    if s == 0:
                        dve.wait_ge(rstd_ready, p + 1)
                    n = NT // NORM_PARTS
                    part = qk_sb[:, s * n:(s + 1) * n, :, :]
                    chain(v.tensor_tensor(part, part, rstd[:, s * n:(s + 1) * n, :].unsqueeze(3).to_broadcast([P, n, 4, HD]), ALU.mult))
                    chain(v.tensor_tensor(part, part, gain[:, :, :].unsqueeze(1).to_broadcast([P, n, 4, HD]), ALU.mult),
                          kv_ready if s == NORM_PARTS - 1 else None)

                V_FIRST = NT + 2 + 2 * NORM_PARTS
                V_STEPS = V_FIRST + NT - TAKE_QK_ACT + (NU + 2) + NG + 2 * NU + 1 + PT // 4 + 2
                chain = Chain(dve, chain_v)
                for t in range(NT):
                    sum_squares(chain, 0, t)
                mean(chain)
                for s in range(NORM_PARTS):
                    norm_part(chain, 0, s)
                chain.ended(V_FIRST)

                def step(i, ahead):
                    use = TURNS if ahead else TURNS_LAST
                    chain = Chain(dve, chain_v, i * V_STEPS + V_FIRST)

                    def maximum(n):
                        dve.wait_ge(scores_ready, i * NU + n + 1)
                        if n < STREAM:
                            chain(v.tensor_reduce(neg_max[:, n:n + 1], half(n)[:, 0:(UNITS[n][1] + 1) * P], X_AXIS, ALU.max,
                                                  negate=True), max_ready)
                        else:
                            chain(v.tensor_reduce(neg_max[:, n:n + 1], scores[:, :], X_AXIS, ALU.max, negate=True))
                            chain(v.tensor_reduce(neg_max[:, n + 1:n + 2], tail, X_AXIS, ALU.max, negate=True))
                            chain(v.tensor_tensor(neg_max[:, n:n + 1], neg_max[:, n:n + 1], neg_max[:, n + 1:n + 2], ALU.min),
                                  max_ready)

                    def take_group(q):
                        n, js = owner[q]
                        m = use["p", q]
                        dve.wait_ge(turned, turned_count(i, m))
                        if q >= 2:
                            dve.wait_ge(pv_done, i * NG + q - 1)
                        rows = T_SAMPLE if js[0] == PAST_TILES else P
                        chain(v.tensor_copy(probsT[q % 2][0:rows, 0:len(js) * P], turn_ps[0:rows, m % 2, 0:len(js) * P]),
                              turn_taken[m % 2])

                    def take_out(n):
                        if n == STREAM:
                            chain(v.tensor_tensor(total[:, n:n + 1], total[:, n:n + 1], total[:, n + 1:n + 2], ALU.add))
                        chain(v.reciprocal(total[:, n:n + 1], total[:, n:n + 1]))
                        dve.wait_ge(pv_done, i * NG + end_group(n))
                        if n == STREAM:
                            chain(v.tensor_scalar(o_s[:, :], out_ps[:, 0:P], total[:, n:n + 1], None, ALU.mult), out_taken)
                        else:
                            h, t = UNITS[n]
                            chain(v.tensor_scalar(o_sb[:, t, h * HD:(h + 1) * HD], out_ps[:, 0:HD], total[:, n:n + 1],
                                                  None, ALU.mult), out_taken)

                    at = lambda rows, c0, n: attnT[rows, bass.ds(i, 1), c0:c0 + n].rearrange("p o t -> p (o t)")

                    def take_turned_out(s):
                        m = use["o", s]
                        dve.wait_ge(turned, turned_count(i, m))
                        chain(v.tensor_copy(at(slice(0, P), s * BANK, BANK), turn_ps[:, m % 2, :]), turn_taken[m % 2])

                    maximum(0)
                    for n in range(STREAM):
                        if n + 1 < STREAM:
                            maximum(n + 1)
                        if n:
                            take_out(n - 1)
                        if n == FIRST_O:
                            take_turned_out(0)
                        take_group(first_group(n))
                        if ahead and n in PROJECTED_AT:
                            sum_squares(chain, i + 1, PROJECTED_AT.index(n))
                            if n == PROJECTED_AT[-1]:
                                mean(chain)
                        for q in range(first_group(n) + 1, end_group(n)):
                            take_group(q)
                    if ahead:
                        for s in range(NORM_PARTS):
                            norm_part(chain, i + 1, s)
                    maximum(STREAM)
                    take_out(STREAM - 1)
                    if ahead:
                        for t in range(TAKE_QK_ACT, NT):
                            m = use["qk", t]
                            dve.wait_ge(turned, turned_count(i, m))
                            chain(v.tensor_copy(qkT[0:HD, :, t * P:(t + 1) * P],
                                                turn_ps[0:HD, m % 2, :].rearrange("p (n c) -> p n c", n=4)), turn_taken[m % 2])
                    for q in range(first_group(STREAM), NG):
                        take_group(q)
                        if q == first_group(STREAM):
                            take_turned_out(1)
                    take_out(STREAM)
                    m = use["o", 2]
                    dve.wait_ge(turned, turned_count(i, m))
                    for h in range(2):
                        rows = slice(h * HD, (h + 1) * HD)
                        chain(v.tensor_copy(at(rows, T_PROMPT, T_SAMPLE), turn_ps[rows, m % 2, rows]),
                              turn_taken[m % 2] if h else None)
                    if ahead:
                        chain.ended(V_STEPS)

                with dve.Fori(0, PAIRS - 1) as i:
                    step(i, True)
                step(PAIRS - 1, False)


def merge(nc, g, w, x1, xn2, logits):
    R = GROUPS + EXPERTS
    with ExitStack() as ctx:
        sb = lambda name, shape, dt=F32: ctx.enter_context(nc.sbuf_tensor("m_" + name, shape, dt))
        w_o = sb("w_o", [P, KT, D])
        w_r = sb("w_r", [P, KT, R])
        gain = sb("gain", [P, D])
        ss = sb("ss", [P, NT])
        turned_sb = [sb(f"turned{b}", [P, KT, P]) for b in range(2)]
        prod = ctx.enter_context(nc.psum_tensor("m_prod", [P, 2, D], F32))
        turn_ps = ctx.enter_context(nc.psum_tensor("m_turn", [P, KT, P], F32))
        logit_ps = ctx.enter_context(nc.psum_tensor("m_logits", [P, NT, R], F32))
        sem = lambda name: g.sem("m_" + name)
        w_loaded, r_loaded, x_loaded, prod_ready, x1_ready, sq_ready, mean_ready, rstd_ready, xn2_ready = (
            sem("w_loaded"), sem("r_loaded"), sem("x_loaded"), sem("prod_ready"), sem("x1_ready"), sem("sq_ready"),
            sem("mean_ready"), sem("rstd_ready"), sem("xn2_ready"))
        turned, turn_taken, logits_ready, chain_v, chain_a, tail_clear = (sem("turned"), sem("turn_taken"), sem("logits_ready"),
                                                                          sem("chain_v"), sem("chain_a"), sem("tail_clear"))
        rows = lambda t: T_SAMPLE if t == PT else P

        with nc.Block() as block:
            @block.sync
            def _(sp):
                sp.dma_start(w_o[:, :, :], g.w_o[0].rearrange("(k p) n -> p k n", p=P)).then_inc(w_loaded, 16)
                sp.dma_start(x1[:, 0:PT, :], g.x_prompt[0].rearrange("(t p) n -> p t n", p=P)).then_inc(x_loaded, 16)
                sp.dma_start(x1[0:T_SAMPLE, PT, :], g.x_sample[0]).then_inc(x_loaded, 16)
                sp.dma_start(gain[:, :], row(g.norm2_g[0]).to_broadcast([P, D])).then_inc(r_loaded, 16)
                sp.dma_start(w_r[:, :, 0:GROUPS], g.w_route_group[0].rearrange("(k p) n -> p k n", p=P)).then_inc(r_loaded, 16)
                sp.dma_start(w_r[:, :, GROUPS:], g.w_route_expert[0].rearrange("(k p) n -> p k n", p=P)).then_inc(r_loaded, 16)
                w.load_in(sp, g, 0, 0)
                w.load_down(sp, g, 0, 0)

            @block.gpsimd
            def _(pool):
                nc.gpsimd.memset(x1[T_SAMPLE:P, PT, :], 0.0).then_inc(tail_clear, 1)

            @block.tensor
            def _(pe):
                te = nc.tensor
                pe.wait_ge(w_loaded, 16)

                def route_tile(t):
                    pe.wait_ge(xn2_ready, t + 1)
                    if t:
                        pe.wait_ge(turn_taken, t)
                    for k in range(KT):
                        last = te.transpose(turn_ps[:, k, :], xn2[:, t, k * P:(k + 1) * P], g.ident[:, :])
                    last.then_inc(turned, 1)

                def logit_tile(t):
                    pe.wait_ge(turn_taken, t + 1)
                    for k in range(KT):
                        last = te.matmul(logit_ps[:, t, :], turned_sb[t % 2][:, k, :], w_r[:, k, :], start=(k == 0),
                                         stop=(k == KT - 1))
                    last.then_inc(logits_ready, 1)

                pe.wait_ge(r_loaded, 48)
                for t in range(NT + 2):
                    if t < NT:
                        if t >= 2:
                            pe.wait_ge(x1_ready, t - 1)
                        for c in range(D // BANK):
                            for k in range(KT):
                                last = te.matmul(prod[0:rows(t), t % 2, c * BANK:(c + 1) * BANK], g.mT[:, k, t * P:t * P + rows(t)],
                                                 w_o[:, k, c * BANK:(c + 1) * BANK], start=(k == 0), stop=(k == KT - 1))
                        last.then_inc(prod_ready, 1)
                    if t >= 2:
                        logit_tile(t - 2)
                    if 1 <= t <= NT:
                        route_tile(t - 1)

            @block.scalar
            def _(act):
                sc = nc.scalar
                chain = Chain(act, chain_a)

                def take(t):
                    act.wait_ge(turned, t + 1)
                    if t >= 2:
                        act.wait_ge(logits_ready, t - 1)
                    chain(sc.copy(turned_sb[t % 2][:, :, :], turn_ps[:, :, :]), turn_taken)

                for t in range(NT):
                    act.wait_ge(x1_ready, t + 1)
                    if t == PT:
                        act.wait_ge(tail_clear, 1)
                    chain(sc.activation(xn2[:, t, :], x1[:, t, :], ACT.Square, accum_out=ss[:, t:t + 1]), sq_ready)
                    act.wait_ge(mean_ready, t + 1)
                    chain(sc.activation(ss[:, t:t + 1], ss[:, t:t + 1], ACT.Sqrt), rstd_ready)
                    if t:
                        take(t - 1)
                take(NT - 1)

            @block.vector
            def _(dve):
                v, chain = nc.vector, Chain(dve, chain_v)
                dve.wait_ge(x_loaded, 32)
                dve.wait_ge(tail_clear, 1)
                dve.wait_ge(r_loaded, 48)
                for t in range(NT):
                    dve.wait_ge(prod_ready, t + 1)
                    n = rows(t)
                    chain(v.tensor_tensor(x1[0:n, t, :], x1[0:n, t, :], prod[0:n, t % 2, :], ALU.add), x1_ready)
                    dve.wait_ge(sq_ready, t + 1)
                    chain(v.tensor_scalar(ss[:, t:t + 1], ss[:, t:t + 1], 1.0 / D, EPS, ALU.mult, ALU.add))
                    chain(v.reciprocal(ss[:, t:t + 1], ss[:, t:t + 1]), mean_ready)
                    dve.wait_ge(rstd_ready, t + 1)
                    chain(v.scalar_tensor_tensor(xn2[:, t, :], x1[:, t, :], ss[:, t:t + 1], gain[:, :], ALU.mult, ALU.mult),
                          xn2_ready)
                dve.wait_ge(logits_ready, NT)
                chain(v.tensor_copy(logits[:, :, :], logit_ps[:, :, :]))


def route(nc, g, w, xn2, logits, gates, slots, passes, expert_of):
    OVER = BLOCKS_MAX - EXPERTS
    with ExitStack() as ctx:
        sb = lambda name, shape, dt=F32: ctx.enter_context(nc.sbuf_tensor("q_" + name, shape, dt))
        bias = sb("bias", [P, GROUPS + EXPERTS])
        counting = sb("counting_i", [P, 64], I32)
        ramp = sb("ramp", [P, 64])
        down4, down8 = sb("down4", [P, GROUPS]), sb("down8", [P, PER_GROUP])
        steps = sb("steps", [P, OVER])
        s1, s2, s3, s4 = sb("s1", [P, NT]), sb("s2", [P, NT]), sb("s3", [P, NT]), sb("s4", [P, NT])
        grp, wide4 = sb("grp", [P, NT, GROUPS]), sb("wide4", [P, NT, GROUPS])
        spread = sb("spread", [P, NT, PER_GROUP, GROUPS])
        inner, wide8 = sb("inner", [P, NT, PER_GROUP]), sb("wide8", [P, NT, PER_GROUP])
        pick = [sb(f"pick{n}", [P, NT, PER_GROUP]) for n in range(TOP_K)]
        chosen = [sb(f"chosen{n}", [P, NT, GROUPS, PER_GROUP]) for n in range(TOP_K)]
        both = sb("both", [P, NT, EXPERTS])
        run = sb("run", [P, NT + 1, EXPERTS])
        weighed = sb("weighed", [P, NT, EXPERTS])
        over, over_end, over_start = sb("over", [P, EXPERTS]), sb("over_end", [P, EXPERTS]), sb("over_start", [P, EXPERTS])
        ones_e = sb("ones_e", [P, EXPERTS])
        compared = sb("compared", [P, EXPERTS, OVER])
        rank, expert, start, times, block_of, slot_f = (sb(n, [P, TOP_K, NT]) for n in
                                                        ("rank", "expert", "start", "times", "block_of", "slot_f"))
        ge = sb("ge", [P, TOP_K * NT, OVER])
        pass_cmp, pass_sum = sb("pass_cmp", [1, OVER // 2]), sb("pass_sum", [1, 1])
        table_f = sb("table_f", [1, BLOCKS_MAX])
        counts_ps = ctx.enter_context(nc.psum_tensor("q_counts", [P, 2, BANK], F32))
        sem = lambda name: g.sem("q_" + name)
        bias_loaded, ramps_ready, exp_asked, exp_ready, both_ready, counts_ready, slots_ready, chain_v, chain_p, sent = (
            sem("bias_loaded"), sem("ramps_ready"), sem("exp_asked"), sem("exp_ready"), sem("both_ready"), sem("counts_ready"),
            sem("slots_ready"), sem("chain_v"), sem("chain_p"), sem("sent"))
        W = NT * EXPERTS

        with nc.Block() as block:
            @block.sync
            def _(sp):
                sp.dma_start(bias[:, 0:GROUPS], row(g.b_route_group[0]).to_broadcast([P, GROUPS])).then_inc(bias_loaded, 16)
                sp.dma_start(bias[:, GROUPS:], row(g.b_route_expert[0]).to_broadcast([P, EXPERTS])).then_inc(bias_loaded, 16)
                w.load_in(sp, g, 1, 1)
                w.load_down(sp, g, 1, 1)

            @block.gpsimd
            def _(pool):
                chain = Chain(pool, chain_p)
                chain(nc.gpsimd.iota(counting[:, :], pattern=[[1, 64]], base=0, channel_multiplier=0))
                chain(nc.gpsimd.tensor_copy(ramp[:, :], counting[:, :]), ramps_ready)
                pool.wait_ge(slots_ready, 1)
                for t in range(NT):
                    n = T_SAMPLE if t == PT else P
                    for s in range(TOP_K):
                        pool.indirect_dma_start(out=g.slot_x[:, :],
                                                out_offset=bass.IndirectOffsetOnAxis(ap=slots[0:n, s, t:t + 1], axis=0),
                                                in_=xn2[0:n, t, :], in_offset=None).then_inc(sent, 16)
                pool.wait_ge(sent, 16 * NT * TOP_K)

            @block.scalar
            def _(act):
                act.wait_ge(exp_asked, 1)
                nc.scalar.activation(wide4[:, :, :], wide4[:, :, :], ACT.Exp).then_inc(exp_ready, 1)
                act.wait_ge(exp_asked, 2)
                nc.scalar.activation(s3[:, :], s3[:, :], ACT.Exp).then_inc(exp_ready, 1)

            @block.tensor
            def _(pe):
                pe.wait_ge(both_ready, 1)
                flat = both[:, :, :].rearrange("p t e -> p (t e)")
                nc.tensor.matmul(counts_ps[:, 0, 0:W], g.before[:, :], flat, start=True, stop=True)
                nc.tensor.matmul(counts_ps[:, 1, 0:W], g.ones[:, :], flat, start=True, stop=True).then_inc(counts_ready, 1)

            @block.vector
            def _(dve):
                v, chain = nc.vector, Chain(dve, chain_v)
                tt, ts = v.tensor_tensor, v.tensor_scalar
                dve.wait_ge(ramps_ready, 1)
                chain(ts(down4[:, :], ramp[:, 0:GROUPS], -1.0, float(GROUPS), ALU.mult, ALU.add))
                chain(ts(down8[:, :], ramp[:, 0:PER_GROUP], -1.0, float(PER_GROUP), ALU.mult, ALU.add))
                chain(ts(steps[:, :], ramp[:, 1:OVER + 1], float(CAP), None, ALU.mult))
                chain(v.memset(ones_e[:, :], 1.0))
                dve.wait_ge(bias_loaded, 32)
                chain(tt(logits[:, :, :], logits[:, :, :], bias[:, :].unsqueeze(1).to_broadcast([P, NT, GROUPS + EXPERTS]), ALU.add))

                def first_of(out, values, top, down, n, scratch):
                    chain(tt(out, values, top.unsqueeze(2).to_broadcast([P, NT, n]), ALU.is_equal))
                    chain(tt(out, out, down.unsqueeze(1).to_broadcast([P, NT, n]), ALU.mult))
                    chain(v.tensor_reduce(scratch, out, X_AXIS, ALU.max))
                    chain(tt(out, out, scratch.unsqueeze(2).to_broadcast([P, NT, n]), ALU.is_equal))

                by_group = logits[:, :, 0:GROUPS]
                chain(v.tensor_reduce(s1[:, :], by_group, X_AXIS, ALU.max))
                chain(tt(wide4[:, :, :], by_group, s1[:, :].unsqueeze(2).to_broadcast([P, NT, GROUPS]), ALU.subtract), exp_asked)
                first_of(grp[:, :, :], by_group, s1[:, :], down4[:, :], GROUPS, s2[:, :])
                dve.wait_ge(exp_ready, 1)
                chain(v.reduce_sum(s4[:, :], wide4[:, :, :], axis=X_AXIS))
                chain(v.reciprocal(s4[:, :], s4[:, :]))

                per_expert = logits[:, :, GROUPS:].rearrange("p t (g e) -> p t e g", g=GROUPS)
                chain(tt(spread[:, :, :, :], per_expert, grp[:, :, :].unsqueeze(2).to_broadcast([P, NT, PER_GROUP, GROUPS]), ALU.mult))
                chain(v.reduce_sum(inner[:, :, :], spread[:, :, :, :], axis=X_AXIS))
                chain(v.tensor_reduce(s1[:, :], inner[:, :, :], X_AXIS, ALU.max))
                first_of(pick[0][:, :, :], inner[:, :, :], s1[:, :], down8[:, :], PER_GROUP, s2[:, :])
                chain(v.scalar_tensor_tensor(wide8[:, :, :], pick[0][:, :, :], NEG, inner[:, :, :], ALU.mult, ALU.add))
                chain(v.tensor_reduce(s3[:, :], wide8[:, :, :], X_AXIS, ALU.max))
                first_of(pick[1][:, :, :], wide8[:, :, :], s3[:, :], down8[:, :], PER_GROUP, s2[:, :])
                chain(tt(s3[:, :], s3[:, :], s1[:, :], ALU.subtract), exp_asked)
                dve.wait_ge(exp_ready, 2)
                chain(ts(s1[:, :], s3[:, :], 1.0, None, ALU.add))
                chain(v.reciprocal(s1[:, :], s1[:, :]))
                chain(tt(gates[:, 0, :], s1[:, :], s4[:, :], ALU.mult))
                chain(tt(gates[:, 1, :], gates[:, 0, :], s3[:, :], ALU.mult))

                for n in range(TOP_K):
                    for k in range(GROUPS):
                        chain(tt(chosen[n][:, :, k, :], pick[n][:, :, :],
                                 grp[:, :, k:k + 1].to_broadcast([P, NT, PER_GROUP]), ALU.mult))
                flat = [c[:, :, :, :].rearrange("p t g e -> p t (g e)") for c in chosen]
                chain(tt(both[:, :, :], flat[0], flat[1], ALU.add))
                chain(v.memset(both[T_SAMPLE:P, PT, :], 0.0), both_ready)

                dve.wait_ge(counts_ready, 1)
                local = counts_ps[:, 0, 0:W].rearrange("p (t e) -> p t e", t=NT)
                whole = counts_ps[:, 1, 0:W].rearrange("p (t e) -> p t e", t=NT)
                chain(v.memset(run[:, 0, :], 0.0))
                for t in range(NT):
                    chain(tt(run[:, t + 1, :], run[:, t, :], whole[:, t, :], ALU.add))
                chain(tt(compared[:, :, :], run[:, NT, :].unsqueeze(2).to_broadcast([P, EXPERTS, OVER]),
                         steps[:, :].unsqueeze(1).to_broadcast([P, EXPERTS, OVER]), ALU.is_gt))
                chain(v.reduce_sum(over[:, :], compared[:, :, :], axis=X_AXIS))
                chain(v.tensor_tensor_scan(over_end[:, :], ones_e[:, :], over[:, :], 0.0, ALU.mult, ALU.add))
                chain(tt(over_start[:, :], over_end[:, :], over[:, :], ALU.subtract))
                chain(tt(both[:, :, :], local, run[:, 0:NT, :], ALU.add))
                wide = lambda ap: ap.unsqueeze(1).to_broadcast([P, NT, EXPERTS])
                for n in range(TOP_K):
                    for out, of in ((rank, both[:, :, :]), (expert, wide(ramp[:, 0:EXPERTS])), (start, wide(over_start[:, :]))):
                        chain(tt(weighed[:, :, :], flat[n], of, ALU.mult))
                        chain(v.reduce_sum(out[:, n, :], weighed[:, :, :], axis=X_AXIS))
                two = lambda a: a[:, :, :].rearrange("p s t -> p (s t)")
                chain(tt(ge[:, :, :], two(rank).unsqueeze(2).to_broadcast([P, TOP_K * NT, OVER]),
                         steps[:, :].unsqueeze(1).to_broadcast([P, TOP_K * NT, OVER]), ALU.is_ge))
                chain(v.reduce_sum(two(times), ge[:, :, :], axis=X_AXIS))
                chain(tt(two(block_of), two(start), two(times), ALU.add))
                chain(tt(two(block_of), two(block_of), two(expert), ALU.subtract))
                chain(ts(two(block_of), two(block_of), float(EXPERTS - 1), None, ALU.add))
                chain(ts(two(slot_f), two(times), 1.0, None, ALU.min))
                chain(tt(two(block_of), two(block_of), two(slot_f), ALU.mult))
                chain(tt(two(block_of), two(block_of), two(expert), ALU.add))
                chain(tt(two(slot_f), two(block_of), two(times), ALU.subtract))
                chain(v.scalar_tensor_tensor(two(slot_f), two(slot_f), float(CAP), two(rank), ALU.mult, ALU.add))
                chain(v.tensor_copy(slots[:, :, :], slot_f[:, :, :]), slots_ready)

                chain(ts(pass_cmp[:, :], ramp[0:1, 0:OVER // 2], 2.0, None, ALU.mult))
                chain(tt(pass_cmp[:, :], over_end[0:1, EXPERTS - 1:EXPERTS].to_broadcast([1, OVER // 2]), pass_cmp[:, :], ALU.is_gt))
                chain(v.reduce_sum(pass_sum[:, :], pass_cmp[:, :], axis=X_AXIS))
                chain(ts(passes[:, :], pass_sum[:, :], float(EXPERTS // 2), None, ALU.add))
                chain(v.tensor_copy(table_f[:, 0:EXPERTS], ramp[0:1, 0:EXPERTS]))
                by_block = compared[0:1, :, :].rearrange("p e o -> p (e o)").rearrange("p (o e) -> p o e", e=EXPERTS)
                chain(tt(by_block, over_end[0:1, :].unsqueeze(1).to_broadcast([1, OVER, EXPERTS]),
                         ramp[0:1, 0:OVER].unsqueeze(2).to_broadcast([1, OVER, EXPERTS]), ALU.is_le))
                chain(v.reduce_sum(table_f[:, EXPERTS:], by_block, axis=X_AXIS))
                chain(ts(table_f[:, :], table_f[:, :], float(EXPERTS - 1), None, ALU.min))
                chain(v.tensor_copy(expert_of[:, :], table_f[:, :]))


class ExpertWeights:

    def __init__(self, nc, g, ctx):
        sb = lambda name, shape: ctx.enter_context(nc.sbuf_tensor("e_" + name, shape, F32))
        self.gate = [sb("gate0", [P, KT, F_EXP])]
        self.up = [sb("up0", [P, KT, F_EXP])]
        self.down = [sb("down0", [P, FT, D])]
        self.gate_loaded, self.up_loaded, self.down_loaded = ([g.sem(f"e_{n}_loaded{u}") for u in range(2)]
                                                              for n in ("gate", "up", "down"))

    def second(self, nc, ctx):
        sb = lambda name, shape: ctx.enter_context(nc.sbuf_tensor("e_" + name, shape, F32, side="right"))
        self.gate.append(sb("gate1", [P, KT, F_EXP]))
        self.up.append(sb("up1", [P, KT, F_EXP]))
        self.down.append(sb("down1", [P, FT, D]))

    def load_in(self, sp, g, u, e):
        into = lambda w: w[0, bass.ds(e, 1)].rearrange("o (k p) n -> p (o k) n", p=P)
        sp.dma_start(self.gate[u][:, :, :], into(g.w_gate_e)).then_inc(self.gate_loaded[u], 16)
        sp.dma_start(self.up[u][:, :, :], into(g.w_up_e)).then_inc(self.up_loaded[u], 16)

    def load_down(self, sp, g, u, e):
        sp.dma_start(self.down[u][:, :, :], g.w_down_e[0, bass.ds(e, 1)].rearrange("o (k p) n -> p (o k) n", p=P))\
            .then_inc(self.down_loaded[u], 16)


def experts(nc, g, w, passes, expert_of):
    with ExitStack() as ctx:
        sb = lambda name, shape, dt=F32: ctx.enter_context(nc.sbuf_tensor("e_" + name, shape, dt))
        xb = [sb(f"x{u}", [CAP, D]) for u in range(2)]
        xT = sb("xT", [P, KT, CAP])
        act_sb = sb("act", [P, FT * CAP])
        hT = sb("hT", [P, FT * CAP])
        y_sb = [sb(f"y{u}", [CAP, D]) for u in range(2)]
        xT_ps = ctx.enter_context(nc.psum_tensor("e_xT_ps", [P, 2, BANK], F32))
        gate_ps = ctx.enter_context(nc.psum_tensor("e_gate_ps", [P, BANK], F32))
        up_ps = ctx.enter_context(nc.psum_tensor("e_up_ps", [P, BANK], F32))
        y_ps = ctx.enter_context(nc.psum_tensor("e_y_ps", [CAP, D], F32))
        sem = lambda name: g.sem("e_" + name)
        x_loaded = [sem(f"x_loaded{u}") for u in range(2)]
        x_turned, xT_ready, gate_ready, up_ready, act_ready, h_ready, y_ready, y_kept = (
            sem("x_turned"), sem("xT_ready"), sem("gate_ready"), sem("up_ready"), sem("act_ready"), sem("h_ready"),
            sem("y_ready"), sem("y_kept"))
        y_stored = [sem(f"y_stored{u}") for u in range(2)]
        limits = dict(min_val=EXPERTS // 2, max_val=BLOCKS_MAX // 2)

        with nc.Block() as block:
            @block.sync
            def _(sp):
                n = sp.value_load(passes[0:1, 0:1], **limits)

                def load_x(b, u):
                    sp.dma_start(xb[u][:, :], g.slot_x[bass.ds(b * CAP, CAP), :]).then_inc(x_loaded[u], 16)

                load_x(0, 0)
                load_x(1, 1)
                with sp.Fori(0, n - 1) as i:
                    for u in range(2):
                        b = i * 2 + u
                        e = sp.value_load(expert_of[0:1, bass.ds(b + 2, 1)], min_val=0, max_val=EXPERTS - 1)
                        sp.wait_ge(x_turned, b + 2)
                        load_x(b + 2, u)
                        sp.wait_ge(up_ready, b + 1)
                        w.load_in(sp, g, u, e)
                        sp.wait_ge(y_ready, b + 1)
                        w.load_down(sp, g, u, e)
                sp.wait_ge(x_turned, n * 2)
                load_x(n * 2, 0)

            @block.tensor
            def _(pe):
                te = nc.tensor

                def turn_x(u):
                    for k in range(KT):
                        last = te.transpose(xT_ps[:, k // 4, (k % 4) * CAP:(k % 4 + 1) * CAP], xb[u][:, k * P:(k + 1) * P],
                                            g.ident[0:CAP, 0:CAP])
                    last.then_inc(x_turned, 1)

                n = pe.value_load(passes[0:1, 0:1], **limits)
                pe.sem_inc(y_kept, 1)
                pe.sem_inc(x_turned, 1)
                pe.wait_ge(x_loaded[0], 16)
                turn_x(0)
                with pe.Fori(0, n) as i:
                    for u in range(2):
                        b = i * 2 + u
                        pe.wait_ge(xT_ready, b + 1)
                        for weights, loaded, out, ready in ((w.gate, w.gate_loaded, gate_ps, gate_ready),
                                                            (w.up, w.up_loaded, up_ps, up_ready)):
                            pe.wait_ge(loaded[u], i * 16 + 16)
                            for f in range(FT):
                                for k in range(KT):
                                    last = te.matmul(out[:, f * CAP:(f + 1) * CAP], weights[u][:, k, f * P:(f + 1) * P], xT[:, k, :],
                                                     start=(k == 0), stop=(k == KT - 1))
                            last.then_inc(ready, 1)
                        pe.wait_ge(x_loaded[1 - u], i * 16 + 16 + 16 * u)
                        alone(pe, g)
                        turn_x(1 - u)
                        pe.wait_ge(h_ready, b + 1)
                        pe.wait_ge(w.down_loaded[u], i * 16 + 16)
                        pe.wait_ge(y_kept, b + 1)
                        for c in range(D // BANK):
                            for f in range(FT):
                                last = te.matmul(y_ps[:, c * BANK:(c + 1) * BANK], hT[:, f * CAP:(f + 1) * CAP],
                                                 w.down[u][:, f, c * BANK:(c + 1) * BANK], start=(f == 0), stop=(f == FT - 1))
                        last.then_inc(y_ready, 1)

            @block.scalar
            def _(act):
                n = act.value_load(passes[0:1, 0:1], **limits)
                for u in range(2):
                    act.sem_inc(y_stored[u], 16)
                with act.Fori(0, n) as i:
                    for u in range(2):
                        b = i * 2 + u
                        act.wait_ge(gate_ready, b + 1)
                        nc.scalar.activation(act_sb[:, :], gate_ps[:, 0:FT * CAP], ACT.Silu).then_inc(act_ready, 1)
                        act.wait_ge(y_ready, b + 1)
                        act.wait_ge(y_stored[u], i * 16 + 16)
                        nc.scalar.copy(y_sb[u][:, :], y_ps[:, :]).then_inc(y_kept, 1)
                        act.wait_ge(y_kept, b + 2)
                        act.dma_start(g.slot_y[bass.ds(b * CAP, CAP), :], y_sb[u][:, :]).then_inc(y_stored[u], 16)
                for u in range(2):
                    act.wait_ge(y_stored[u], n * 16 + 16)
                alone(act, g)

            @block.vector
            def _(dve):
                def take_x():
                    nc.vector.tensor_copy(xT[:, :, :].rearrange("p (a k) c -> p a (k c)", a=2), xT_ps[:, :, 0:4 * CAP])\
                        .then_inc(xT_ready, 1)

                n = dve.value_load(passes[0:1, 0:1], **limits)
                dve.wait_ge(x_turned, 2)
                take_x()
                with dve.Fori(0, n) as i:
                    for u in range(2):
                        b = i * 2 + u
                        dve.wait_ge(up_ready, b + 1)
                        dve.wait_ge(act_ready, b + 1)
                        nc.vector.tensor_tensor(hT[:, :], act_sb[:, :], up_ps[:, 0:FT * CAP], ALU.mult).then_inc(h_ready, 1)
                        dve.wait_ge(x_turned, b + 3)
                        take_x()


def combine(nc, g, x1, gates, slots):
    BUFS = 3
    with ExitStack() as ctx:
        got = [[ctx.enter_context(nc.sbuf_tensor(f"c_got{s}_{b}", [P, D], F32)) for b in range(BUFS)] for s in range(TOP_K)]
        sem = lambda name: g.sem("c_" + name)
        gathered = [[sem(f"gathered{s}_{b}") for b in range(BUFS)] for s in range(TOP_K)]
        summed, chain_v, y_stored = sem("summed"), sem("chain_v"), sem("y_stored")
        rows = lambda t: T_SAMPLE if t == PT else P

        with nc.Block() as block:
            @block.gpsimd
            def _(pool):
                for t in range(NT):
                    if t >= BUFS:
                        pool.wait_ge(summed, t - BUFS + 1)
                    for s in range(TOP_K):
                        pool.indirect_dma_start(out=got[s][t % BUFS][0:rows(t), :], out_offset=None, in_=g.slot_y[:, :],
                                                in_offset=bass.IndirectOffsetOnAxis(ap=slots[0:rows(t), s, t:t + 1], axis=0))\
                            .then_inc(gathered[s][t % BUFS], 16)

            @block.vector
            def _(dve):
                chain = Chain(dve, chain_v)
                for t in range(NT):
                    n = rows(t)
                    for s in range(TOP_K):
                        dve.wait_ge(gathered[s][t % BUFS], 16 * (t // BUFS + 1))
                        chain(nc.vector.scalar_tensor_tensor(x1[0:n, t, :], got[s][t % BUFS][0:n, :], gates[0:n, s, t:t + 1],
                                                             x1[0:n, t, :], ALU.mult, ALU.add), summed if s else None)

            @block.sync
            def _(sp):
                for t in range(NT):
                    sp.wait_ge(summed, t + 1)
                    out = g.out_y_s[0] if t == PT else g.out_y_p[0, t * P:(t + 1) * P, :]
                    sp.dma_start(out, x1[0:rows(t), t, :]).then_inc(y_stored, 16)
                sp.wait_ge(y_stored, 16 * NT)


def back(nc, g, mixed):
    with ExitStack() as ctx:
        sb = lambda name, shape, dt=F32: ctx.enter_context(nc.sbuf_tensor(name, shape, dt))
        x1 = sb("x1", [P, NT, D])
        gates, slots = sb("gates", [P, TOP_K, NT]), sb("slots", [P, TOP_K, NT], U32)
        passes, expert_of = sb("passes", [1, 1], I32), sb("expert_of", [1, BLOCKS_MAX], I32)
        with ExitStack() as weights:
            w = ExpertWeights(nc, g, weights)
            with nc.sbuf_tensor("xn2", [P, NT, D], F32) as xn2, nc.sbuf_tensor("logits", [P, NT, GROUPS + EXPERTS], F32) as logits:
                merge(nc, g, w, x1, xn2, logits)
                mixed.close()
                w.second(nc, g.right)
                route(nc, g, w, xn2, logits, gates, slots, passes, expert_of)
            experts(nc, g, w, passes, expert_of)
        combine(nc, g, x1, gates, slots)


_INS = ["x_prompt", "x_sample", "cache_k", "cache_v", "cache_logf", "state_conv", "state_rglru", "norm1_g", "w_in",
        "conv_w", "conv_b", "w_a", "b_a", "w_x", "b_x", "lru_lambda", "b_f", "q_norm_g", "k_norm_g", "w_rnn_out",
        "w_attn_out", "w_o", "norm2_g", "w_route_group", "b_route_group", "w_route_expert", "b_route_expert",
        "w_gate_e", "w_up_e", "w_down_e"]
_OUTS = [("out_y_p", (1, T_PROMPT, D)), ("out_y_s", (1, T_SAMPLE, D)),
         ("out_k_p", (1, 1, T_PROMPT, HEADS, HD)), ("out_v_p", (1, 1, T_PROMPT, HEADS, HD)),
         ("out_lf_p", (1, 1, T_PROMPT, HEADS)), ("out_conv_p", (1, 1, CONV_W - 1, D)), ("out_h_p", (1, 1, D)),
         ("out_k_s", (1, 1, T_SAMPLE, HEADS, HD)), ("out_v_s", (1, 1, T_SAMPLE, HEADS, HD)),
         ("out_lf_s", (1, 1, T_SAMPLE, HEADS)), ("out_conv_s", (1, 1, CONV_W - 1, D)), ("out_h_s", (1, 1, D))]


class Shared:
    pass


def layer(nc, ctx, a):
    g = Shared()
    (g.x_prompt, g.x_sample, g.cache_k, g.cache_v, g.cache_logf, g.state_conv, g.state_rglru, g.norm1_g, g.w_in,
     g.conv_w, g.conv_b, g.w_a, g.b_a, g.w_x, g.b_x, g.lru_lambda, g.b_f, g.q_norm_g, g.k_norm_g, g.w_rnn_out,
     g.w_attn_out, g.w_o, g.norm2_g, g.w_route_group, g.b_route_group, g.w_route_expert, g.b_route_expert,
     g.w_gate_e, g.w_up_e, g.w_down_e) = (a[name] for name in _INS)
    (g.out_y_p, g.out_y_s, g.out_k_p, g.out_v_p, g.out_lf_p, g.out_conv_p, g.out_h_p, g.out_k_s, g.out_v_s,
     g.out_lf_s, g.out_conv_s, g.out_h_s) = (a[name] for name, _ in _OUTS)
    sb = lambda name, shape, dt=F32: ctx.enter_context(nc.sbuf_tensor(name, shape, dt))
    g.sem = lambda name: ctx.enter_context(nc.semaphore(name))
    g.slots_cleared = g.sem("slots_cleared")
    g.apart = g.sem("apart")
    g.w_in_k = g.w_in[0].rearrange("(k p) n -> p k n", p=P)
    g.slot_x = nc.dram_tensor("slot_x", [SLOTS + CAP, D], F32, kind="Internal").ap()
    g.slot_y = nc.dram_tensor("slot_y", [SLOTS, D], F32, kind="Internal").ap()
    g.neg_c_new = nc.dram_tensor("neg_c_new", [HEADS, T_ALL], F32, kind="Internal").ap()
    g.neg_c_past = nc.dram_tensor("neg_c_past", [HEADS, PAST], F32, kind="Internal").ap()
    g.ident, g.ones, g.before = sb("ident", [P, P]), sb("ones", [P, P]), sb("before", [P, P])
    g.ident_bf, g.causal = sb("ident_bf", [P, P], BF16), sb("causal", [P, P], BF16)
    g.causal_s = sb("causal_s", [P, T_SAMPLE], BF16)
    g.causal_f = sb("causal_f", [P, P])
    g.chan = sb("chan", [P, N_VEC * KT])
    g.decay = sb("decay", [P, KT])
    g.right, mixed = ExitStack(), ExitStack()
    g.mT = mixed.enter_context(nc.sbuf_tensor("mT", [P, KT, T_PAD], F32, side="right"))
    with ExitStack() as front:
        sbf = lambda name, shape, dt=F32: front.enter_context(nc.sbuf_tensor(name, shape, dt))
        g.xnT = sbf("xnT", [P, KT, T_PAD])
        normalize(nc, g)
        g.qkT = sbf("qkT", [HD + 1, 4, T_PAD])
        forget_gates(nc, g)
        with nc.sbuf_tensor("attnT", [P, KT, T_PAD], F32) as attnT:
            attend(nc, g, attnT)
            project(nc, g, attnT, g.w_attn_out, COL_GATE_ATTN, False, "pa")
        with nc.sbuf_tensor("yT", [P, KT, T_PAD], F32) as yT:
            recurrent(nc, g, yT)
            project(nc, g, yT, g.w_rnn_out, COL_GATE_RNN, True, "pr")
    with g.right:
        back(nc, g, mixed)


def kernel(**inputs):
    import numpy as np
    import concourse.bacc as bacc
    from concourse.bass_utils import run_bass_kernel_spmd

    nc = bacc.Bacc("TRN2", target_bir_lowering=False, num_devices=1)
    arrays, aps = {}, {}
    for name in _INS:
        arrays[name] = np.ascontiguousarray(inputs[name])
        aps[name] = nc.dram_tensor(name, arrays[name].shape, F32, kind="ExternalInput").ap()
    for name, shape in _OUTS:
        aps[name] = nc.dram_tensor(name, shape, F32, kind="ExternalOutput").ap()
    with ExitStack() as ctx:
        layer(nc, ctx, aps)
    r = run_bass_kernel_spmd(nc, [arrays], core_ids=[0])
    return tuple(r.results[0][name] for name, _ in _OUTS)
```

```python
import concourse.bass as bass
from concourse import mybir
from contextlib import ExitStack

F32 = mybir.dt.float32
F32R = mybir.dt.float32r
BF16 = mybir.dt.bfloat16
I32 = mybir.dt.int32
U32 = mybir.dt.uint32
ALU = mybir.AluOpType
ACT = mybir.ActivationFunctionType
X_AXIS = mybir.AxisListType.X

P = 128
D = 1024
KT = D // P
T_PROMPT, T_SAMPLE, PAST = 1024, 64, 2048
T_ALL = T_PROMPT + T_SAMPLE
PT = T_PROMPT // P
NT = PT + 1
T_PAD = NT * P
CHUNKS = ((0, 512), (512, 512), (1024, T_SAMPLE))
BANK = 512
N_THIRDS, THIRD = 3, 364
T_WIDE = N_THIRDS * THIRD
CONV_W = 4
LRU_C = 8.0
HEADS, HD = 16, 64
PAIRS = HEADS // 2
PAST_TILES = PAST // P
KV_SAMPLE = PAST + T_SAMPLE
GROUPS, PER_GROUP = 4, 8
EXPERTS = GROUPS * PER_GROUP
F_EXP = 512
FT = F_EXP // P
TOP_K = 2
CAP = 96
OVER_MAX = TOP_K * T_ALL // CAP
BLOCKS_MAX = (EXPERTS + OVER_MAX + 1) // 2 * 2
SLOTS = BLOCKS_MAX * CAP
EPS = 1e-6
NEG = -1e30

QKV = 3 * P

COL_X, COL_G, COL_Q, COL_K, COL_V = 0, D, 2 * D, 3 * D, 4 * D
COL_F = 5 * D
COL_GATE_RNN = COL_F + HEADS
COL_GATE_ATTN = COL_GATE_RNN + D

V_NORM1, V_CONV, V_CONVB, V_BA, V_BX, V_LAM, V_H0, V_HIST = 0, 1, 5, 6, 7, 8, 9, 10
N_VEC = 13


class Chain:

    def __init__(self, eng, sem, base=0):
        self.eng, self.sem, self.base, self.n = eng, sem, base, 0

    def __call__(self, ins, tell=None):
        self.n += 1
        ins.then_inc(self.sem, 1)
        self.eng.wait_ge(self.sem, self.base + self.n)
        if tell is not None:
            self.eng.sem_inc(tell, 1)

    def ended(self, per_pass):
        assert self.n == per_pass, self.n


def alone(eng, g):
    eng.sem_inc(g.apart, 1)


def product(nc, out, a, b, start, stop):
    (a_hi, a_lo), (b_hi, b_lo) = a, b
    nc.tensor.matmul(out, a_hi, b_hi, start=start, stop=False)
    nc.tensor.matmul(out, a_hi, b_lo, start=False, stop=False)
    return nc.tensor.matmul(out, a_lo, b_hi, start=False, stop=stop)


def row(ap, n=1):
    return ap.rearrange("(o n) -> o n", o=n)


def log1p_steps(nc, chain, out, z, s, s2, acc):
    v = nc.vector
    chain(v.tensor_scalar(s, z, 2.0, None, ALU.add))
    chain(v.reciprocal(s2, s))
    chain(v.tensor_tensor(s, z, s2, ALU.mult))
    chain(v.tensor_tensor(s2, s, s, ALU.mult))
    chain(v.tensor_scalar(acc, s2, 1.0 / 17.0, 1.0 / 15.0, ALU.mult, ALU.add))
    for k in (13, 11, 9, 7, 5, 3, 1):
        chain(v.tensor_tensor(acc, acc, s2, ALU.mult))
        chain(v.tensor_scalar(acc, acc, 1.0 / k, None, ALU.add))
    chain(v.scalar_tensor_tensor(out, acc, 2.0, s, ALU.mult, ALU.mult))


LOG1P_STEPS = 5 + 14 + 1


def normalize(nc, g):
    with ExitStack() as ctx:
        sb = lambda name, shape, dt=F32: ctx.enter_context(nc.sbuf_tensor(name, shape, dt))
        vec_rows = sb("vec_rows", [P, P])
        xt = sb("xt", [P, 3, D])
        x_last = sb("x_last", [P, D])
        square = sb("square", [P, D])
        ss = sb("ss", [P, NT])
        rstd = sb("rstd", [P, NT])
        scaled = sb("scaled", [P, 2, KT, P])
        causal_f = sb("causal_f", [P, P])
        turned = ctx.enter_context(nc.psum_tensor("turned", [P, 2, KT, P], F32))
        vec_ps = ctx.enter_context(nc.psum_tensor("vec_ps", [P, P], F32))
        sem = g.sem
        vec_loaded, const_ready = sem("vec_loaded"), sem("const_ready")
        x_loaded = [sem(f"x_loaded{b}") for b in range(4)]
        sq_ready, mean_ready, rstd_ready, xs_ready = sem("sq_ready"), sem("mean_ready"), sem("rstd_ready"), sem("xs_ready")
        xT_ready, xT_taken, vec_ready, chain_v, chain_p = sem("xT_ready"), sem("xT_taken"), sem("vec_ready"), sem("n_chain_v"), sem("n_chain_p")
        chain_a, xh_ready = sem("n_chain_a"), sem("xh_ready")
        tile = lambda t: x_last[:, :] if t == PT else xt[:, t % 3, :]
        load_of = lambda t: (x_loaded[3], 16) if t == PT else (x_loaded[t % 3], 16 * (t // 3 + 1))

        with nc.Block() as block:
            @block.sync
            def _(sp):
                vectors = [g.norm1_g[0], *(g.conv_w[0, j] for j in range(CONV_W)), g.conv_b[0], g.b_a[0], g.b_x[0],
                           g.lru_lambda[0], g.state_rglru[0, 0], *(g.state_conv[0, 0, j] for j in range(CONV_W - 1))]
                sp.dma_start(xt[:, 0, :], g.x_prompt[0, 0:P, :]).then_inc(x_loaded[0], 16)
                for n, vec in enumerate(vectors):
                    sp.dma_start(vec_rows[n * KT:(n + 1) * KT, :], row(vec, KT)).then_inc(vec_loaded, 16)
                for t in range(1, NT):
                    if t == PT:
                        sp.dma_start(x_last[0:T_SAMPLE, :], g.x_sample[0]).then_inc(x_loaded[3], 16)
                        continue
                    if t >= 3:
                        sp.wait_ge(xT_ready, t - 2)
                    sp.dma_start(xt[:, t % 3, :], g.x_prompt[0, t * P:(t + 1) * P, :]).then_inc(x_loaded[t % 3], 16)

            @block.scalar
            def _(act):
                def round_tile(t):
                    act.wait_ge(xT_taken, t + 1)
                    nc.scalar.copy(g.xh[:, :, t * P:(t + 1) * P], scaled[:, t % 2, :, :]).then_inc(xh_ready, 1)

                for t in range(NT):
                    act.wait_ge(*load_of(t))
                    if t == PT:
                        act.wait_ge(const_ready, 1)
                    if t:
                        act.wait_ge(chain_a, t)
                    nc.scalar.activation(square[:, :], tile(t), ACT.Square, accum_out=ss[:, t:t + 1]).then_inc(chain_a, 1)
                    act.wait_ge(chain_a, t + 1)
                    act.sem_inc(sq_ready, 1)
                    act.wait_ge(mean_ready, t + 1)
                    nc.scalar.activation(rstd[:, t:t + 1], rstd[:, t:t + 1], ACT.Sqrt).then_inc(rstd_ready, 1)
                    if t:
                        round_tile(t - 1)
                round_tile(NT - 1)

            @block.gpsimd
            def _(pool):
                chain = Chain(pool, chain_p)
                chain(nc.gpsimd.memset(g.ident[:, :], 0.0))
                chain(nc.gpsimd.affine_select(out=g.ident[:, :], in_=g.ident[:, :], compare_op=ALU.not_equal, fill=1.0,
                                              base=0, pattern=[[-1, P]], channel_multiplier=1))
                chain(nc.gpsimd.memset(x_last[T_SAMPLE:P, :], 0.0), const_ready)
                chain(nc.gpsimd.tensor_copy(g.ident_bf[:, :], g.ident[:, :]))
                chain(nc.gpsimd.memset(g.ones[:, :], 1.0))
                chain(nc.gpsimd.affine_select(out=g.before[:, :], in_=g.ones[:, :], compare_op=ALU.is_gt, fill=0.0,
                                              base=0, pattern=[[1, P]], channel_multiplier=-1))
                chain(nc.gpsimd.memset(causal_f[:, :], 0.0))
                chain(nc.gpsimd.affine_select(out=causal_f[:, :], in_=causal_f[:, :], compare_op=ALU.is_ge, fill=NEG,
                                              base=0, pattern=[[-1, P]], channel_multiplier=1))
                chain(nc.gpsimd.tensor_copy(g.causal[:, :], causal_f[:, :]))
                chain(nc.gpsimd.tensor_copy(g.causal_s[0:64, :], causal_f[0:64, 0:64]))
                chain(nc.gpsimd.tensor_copy(g.causal_s[64:P, :], causal_f[64:P, 64:P]))

            @block.tensor
            def _(pe):
                pe.wait_ge(const_ready, 1)
                pe.wait_ge(vec_loaded, 16 * N_VEC)
                nc.tensor.transpose(vec_ps[:, 0:N_VEC * KT], vec_rows[0:N_VEC * KT, :],
                                    g.ident[0:N_VEC * KT, 0:N_VEC * KT]).then_inc(vec_ready, 1)
                for t in range(NT):
                    pe.wait_ge(xs_ready, t + 1)
                    if t >= 2:
                        pe.wait_ge(xT_taken, t - 1)
                    for k in range(KT):
                        last = nc.tensor.transpose(turned[:, t % 2, k, :], tile(t)[:, k * P:(k + 1) * P], g.ident[:, :])
                    last.then_inc(xT_ready, 1)

            @block.vector
            def _(dve):
                chain = Chain(dve, chain_v)
                dve.wait_ge(vec_ready, 1)
                chain(nc.vector.tensor_copy(g.chan[:, :], vec_ps[:, 0:N_VEC * KT]))

                def take(t):
                    dve.wait_ge(xT_ready, t + 1)
                    gain = g.chan[:, V_NORM1 * KT:(V_NORM1 + 1) * KT].unsqueeze(2).to_broadcast([P, KT, P])
                    chain(nc.vector.tensor_tensor(scaled[:, t % 2, :, :], turned[:, t % 2, :, :], gain, ALU.mult), xT_taken)

                def rest(t):
                    dve.wait_ge(xh_ready, t + 1)
                    chain(nc.vector.tensor_tensor(g.xl[:, :, t * P:(t + 1) * P], scaled[:, t % 2, :, :],
                                                  g.xh[:, :, t * P:(t + 1) * P], ALU.subtract))

                for t in range(NT):
                    dve.wait_ge(sq_ready, t + 1)
                    chain(nc.vector.tensor_scalar(rstd[:, t:t + 1], ss[:, t:t + 1], 1.0 / D, EPS, ALU.mult, ALU.add))
                    chain(nc.vector.reciprocal(rstd[:, t:t + 1], rstd[:, t:t + 1]), mean_ready)
                    if t:
                        take(t - 1)
                    dve.wait_ge(rstd_ready, t + 1)
                    chain(nc.vector.tensor_scalar(tile(t), tile(t), rstd[:, t:t + 1], None, ALU.mult), xs_ready)
                    if t >= 2:
                        rest(t - 2)
                take(NT - 1)
                rest(NT - 2)
                rest(NT - 1)


def load_qkv(sp, g, p):
    for n, col in enumerate((COL_Q, COL_K, COL_V)):
        sp.dma_start(g.w_qkv[:, :, n * P:(n + 1) * P], g.w_in_k[:, :, bass.ds(p * P + col, P)]).then_inc(g.w_loaded, 16)


def forget_gates(nc, g):
    with ExitStack() as ctx:
        sb = lambda name, shape, dt=F32: ctx.enter_context(nc.sbuf_tensor(name, shape, dt))
        w_f = sb("w_f", [P, KT, HEADS])
        wf_parts = [sb(f"wf_{part}", [P, KT, HEADS], F32R) for part in ("hi", "lo")]
        past_lf = sb("past_lf", [P, PAST_TILES, HEADS])
        b_f = sb("b_f_all", [P, HEADS])
        z, e, lf, s, s2, acc = (sb(n, [P, NT * HEADS + KT]) for n in ("fz", "fe", "flf", "fs", "fs2", "facc"))
        f_T = sb("f_T", [HEADS, T_PAD])
        ones_row = sb("ones_row", [HEADS, PAST])
        neg_c_p, neg_c_s = sb("neg_c_p", [HEADS, T_PROMPT]), sb("neg_c_s", [HEADS, KV_SAMPLE])
        f_ps = ctx.enter_context(nc.psum_tensor("f_ps", [P, BANK], F32))
        new_ps = ctx.enter_context(nc.psum_tensor("new_ps", [HEADS, 3 * BANK], F32))
        past_ps = ctx.enter_context(nc.psum_tensor("past_ps", [HEADS, PAST], F32))
        sem = g.sem
        f_loaded, f_ready, e_asked, e_ready = sem("f_loaded"), sem("f_ready"), sem("e_asked"), sem("e_ready")
        past_ready, lf_ready, new_ready, chain_v, lf_stored = sem("past_ready"), sem("lf_ready"), sem("new_ready"), sem("f_chain_v"), sem("lf_stored")
        fT_ready, fT_taken = sem("fT_ready"), sem("fT_taken")
        sums_ready, wf_rounded, wf_split = sem("sums_ready"), sem("wf_rounded"), sem("wf_split")
        F = NT * HEADS

        with nc.Block() as block:
            @block.sync
            def _(sp):
                sp.dma_start(w_f[:, :, :], g.w_in_k[:, :, COL_F:COL_F + HEADS]).then_inc(f_loaded, 16)
                sp.dma_start(past_lf[:, :, :], g.cache_logf[0, 0].rearrange("(t p) h -> p t h", p=P)).then_inc(f_loaded, 16)
                sp.dma_start(b_f[:, :], row(g.b_f[0]).to_broadcast([P, HEADS])).then_inc(f_loaded, 16)
                load_qkv(sp, g, 0)
                sp.wait_ge(lf_ready, 1)
                sp.dma_start(g.out_lf_p[0, 0].rearrange("(t p) h -> p t h", p=P),
                             lf[:, 0:PT * HEADS].rearrange("p (t h) -> p t h", h=HEADS)).then_inc(lf_stored, 16)
                sp.dma_start(g.out_lf_s[0, 0], lf[0:T_SAMPLE, PT * HEADS:F]).then_inc(lf_stored, 16)
                sp.wait_ge(sums_ready, 1)
                sp.dma_start(g.neg_c_new[:, 0:T_PROMPT], neg_c_p[:, :]).then_inc(lf_stored, 16)
                sp.dma_start(g.neg_c_new[:, T_PROMPT:T_ALL], neg_c_s[:, PAST:KV_SAMPLE]).then_inc(lf_stored, 16)
                sp.dma_start(g.neg_c_past[:, :], neg_c_s[:, 0:PAST]).then_inc(lf_stored, 16)
                sp.wait_ge(lf_stored, 80)

            @block.gpsimd
            def _(pool):
                pool.wait_ge(g.w_rounded, 1)
                nc.gpsimd.tensor_tensor(g.w_parts[1][:, :, :], g.w_qkv[:, :, :], g.w_parts[0][:, :, :], ALU.subtract)\
                    .then_inc(g.w_split, 1)

            @block.tensor
            def _(pe):
                pe.wait_ge(f_loaded, 48)
                pe.wait_ge(wf_split, 1)
                for c0, n in ((0, BANK), (BANK, BANK), (2 * BANK, P)):
                    for k in range(KT):
                        last = product(nc, new_ps[:, c0:c0 + n], [w[:, k, :] for w in wf_parts],
                                       [x[:, k, c0:c0 + n] for x in (g.xh, g.xl)], k == 0, k == KT - 1)
                last.then_inc(fT_ready, 1)
                for t in range(PAST_TILES):
                    last = nc.tensor.transpose(past_ps[:, t * P:(t + 1) * P], past_lf[:, t, :], g.ident[:, :])
                last.then_inc(past_ready, 1)
                pe.wait_ge(fT_taken, 1)
                for t in range(NT):
                    last = nc.tensor.transpose(f_ps[:, t * HEADS:(t + 1) * HEADS], f_T[:, t * P:(t + 1) * P], g.ident[0:HEADS, 0:HEADS])
                last.then_inc(f_ready, 1)
                pe.wait_ge(lf_ready, 1)
                for t in range(NT):
                    last = nc.tensor.transpose(new_ps[:, t * P:(t + 1) * P], lf[:, t * HEADS:(t + 1) * HEADS], g.ident[:, :])
                last.then_inc(new_ready, 1)

            @block.scalar
            def _(act):
                act.wait_ge(f_loaded, 48)
                nc.scalar.copy(wf_parts[0][:, :, :], w_f[:, :, :]).then_inc(wf_rounded, 1)
                act.wait_ge(fT_ready, 1)
                nc.scalar.copy(f_T[:, :], new_ps[:, 0:T_PAD]).then_inc(fT_taken, 1)
                act.wait_ge(g.w_loaded, 48)
                nc.scalar.copy(g.w_parts[0][:, :, :], g.w_qkv[:, :, :]).then_inc(g.w_rounded, 1)
                act.wait_ge(e_asked, 1)
                nc.scalar.activation(e[:, :], e[:, :], ACT.Exp).then_inc(e_ready, 1)

            @block.vector
            def _(dve):
                v, chain = nc.vector, Chain(dve, chain_v)
                dve.wait_ge(f_loaded, 48)
                dve.wait_ge(wf_rounded, 1)
                chain(v.tensor_tensor(wf_parts[1][:, :, :], w_f[:, :, :], wf_parts[0][:, :, :], ALU.subtract), wf_split)
                chain(v.memset(ones_row[:, :], 1.0))
                chain(v.memset(g.qkT[HD:HD + 1, 0:2, :], 1.0))
                dve.wait_ge(f_ready, 1)
                chain(v.tensor_tensor(z[:, 0:F].rearrange("p (t h) -> p t h", h=HEADS),
                                      f_ps[:, 0:F].rearrange("p (t h) -> p t h", h=HEADS),
                                      b_f[:, :].unsqueeze(1).to_broadcast([P, NT, HEADS]), ALU.add))
                chain(v.tensor_copy(z[:, F:F + KT], g.chan[:, V_LAM * KT:(V_LAM + 1) * KT]))
                chain(v.tensor_scalar(e[:, :], z[:, :], -1.0, None, ALU.mult))
                chain(v.tensor_tensor(e[:, :], e[:, :], z[:, :], ALU.min), e_asked)
                dve.wait_ge(e_ready, 1)
                log1p_steps(nc, chain, lf[:, :], e[:, :], s[:, :], s2[:, :], acc[:, :])
                chain(v.tensor_scalar(z[:, :], z[:, :], 0.0, None, ALU.min))
                chain(v.tensor_tensor(lf[:, :], z[:, :], lf[:, :], ALU.subtract), lf_ready)
                chain(v.tensor_scalar(g.decay[:, :], lf[:, F:F + KT], LRU_C, None, ALU.mult))
                dve.wait_ge(past_ready, 1)
                chain(v.tensor_tensor_scan(neg_c_s[:, 0:PAST], ones_row[:, :], past_ps[:, :], 0.0, ALU.mult, ALU.subtract))
                dve.wait_ge(new_ready, 1)
                chain(v.tensor_tensor_scan(neg_c_p[:, :], ones_row[:, 0:T_PROMPT], new_ps[:, 0:T_PROMPT], 0.0,
                                           ALU.mult, ALU.subtract))
                chain(v.tensor_tensor_scan(neg_c_s[:, PAST:KV_SAMPLE], ones_row[:, 0:T_SAMPLE],
                                           new_ps[:, T_PROMPT:T_ALL], neg_c_s[:, PAST - 1:PAST], ALU.mult, ALU.subtract),
                      sums_ready)


def recurrent(nc, g):
    GATE_UNITS = 2 * len(CHUNKS)
    X_CLEARS, Y_CLEARS = 6, 3
    X_ROWS, Y_ROWS = (SLOTS + CAP) // (KT * X_CLEARS), (SLOTS - EXPERTS * CAP) // (KT * Y_CLEARS)
    assert X_ROWS <= P and Y_ROWS <= P
    assert X_ROWS * X_CLEARS * KT == SLOTS + CAP and Y_ROWS * Y_CLEARS * KT == SLOTS - EXPERTS * CAP
    with ExitStack() as ctx:
        sb = lambda name, shape, dt=F32: ctx.enter_context(nc.sbuf_tensor(name, shape, dt))
        w_x, w_g = sb("r_wx", [P, KT, P]), sb("r_wg", [P, KT, P])
        wx_split, wg_split = ([sb(f"r_{n}_{part}", [P, KT, P], F32R) for part in ("hi", "lo")] for n in ("wx", "wg"))
        bd = sb("r_bd", [P, 2, P])
        y_sb = sb("y_sb", [P, T_WIDE])
        zrows = sb("zrows", [P, D])
        warm = sb("r_warm", [P, 1])
        H = CONV_W - 1
        conv_in = sb("conv_in", [P, H + T_PROMPT + H + T_SAMPLE])
        u_sb, r_sb, i_sb, a_sb, th_sb, v_sb, h_sb = (sb(n, [P, T_ALL]) for n in
                                                     ("u_sb", "r_sb", "i_sb", "a_sb", "th_sb", "v_sb", "h_sb"))
        gel = sb("gel", [P, T_WIDE])
        tails = sb("tails", [P, 2 * H + 2, KT])
        tails_T = sb("tails_T", [P, P])
        ux_ps = ctx.enter_context(nc.psum_tensor("ux_ps", [P, N_THIRDS, BANK], F32))
        ug_ps = ctx.enter_context(nc.psum_tensor("ug_ps", [P, N_THIRDS, BANK], F32))
        gate_ps = ctx.enter_context(nc.psum_tensor("gate_ps", [P, 2, BANK], F32))
        sem = g.sem
        x_loaded, g_loaded, bd_loaded, bd_cleared = sem("rx_loaded"), sem("rg_loaded"), sem("bd_loaded"), sem("bd_cleared")
        x_rounded, g_rounded, x_split, g_split = sem("rx_rounded"), sem("rg_rounded"), sem("rx_split"), sem("rg_split")
        y_stored, y_free, zrows_ready = sem("y_stored"), sem("y_free"), sem("zrows_ready")
        ux_ready, ug_ready, conv_ready = sem("ux_ready"), sem("ug_ready"), sem("conv_in_ready")
        u_ready, gate_ready, gate_taken = sem("u_ready"), sem("gate_ready"), sem("gate_taken")
        ri_ready, at_ready, gel_ready, var_ready, std_ready, step_done = (sem("ri_ready"), sem("at_ready"), sem("gel_ready"),
                                                                          sem("var_ready"), sem("std_ready"), sem("step_done"))
        chain_v, chain_a, chain_e = sem("r_chain_v"), sem("r_chain_a"), sem("r_chain_e")
        tails_ready, tails_turned, tails_kept, tails_stored = sem("tails_ready"), sem("tails_turned"), sem("tails_kept"), sem("tails_stored")
        V_STEPS, A_STEPS = 19, 15

        with nc.Block() as block:
            @block.sync
            def _(sp):
                def load_x(c):
                    sp.dma_start(w_x[:, :, :], g.w_in_k[:, :, bass.ds(c * P + COL_X, P)]).then_inc(x_loaded, 16)

                def load_g(c):
                    sp.dma_start(w_g[:, :, :], g.w_in_k[:, :, bass.ds(c * P + COL_G, P)]).then_inc(g_loaded, 16)

                def load_bd(c):
                    for n, w in enumerate((g.w_a, g.w_x)):
                        for h in range(2):
                            sp.dma_start(bd[h * 64:(h + 1) * 64, n, h * 64:(h + 1) * 64],
                                         w[0, bass.ds(c * 2 + h, 1)].rearrange("o i j -> (o i) j")).then_inc(bd_loaded, 16)

                load_x(0)
                load_g(0)
                sp.wait_ge(bd_cleared, 1)
                load_bd(0)
                with sp.Fori(0, KT - 1) as c:
                    sp.wait_ge(x_split, c + 1)
                    alone(sp, g)
                    load_x(c + 1)
                    sp.wait_ge(g_split, c + 1)
                    alone(sp, g)
                    load_g(c + 1)
                    sp.wait_ge(gate_ready, c * GATE_UNITS + GATE_UNITS)
                    alone(sp, g)
                    load_bd(c + 1)
                sp.wait_ge(tails_kept, 1)
                last_rows = lambda out: out[0, 0].rearrange("j (c p) -> (j c) p", p=P)
                one_row = lambda out: out[0, 0:1].rearrange("o (c p) -> (o c) p", p=P)
                sp.dma_start(last_rows(g.out_conv_p), tails_T[0:H * KT, :]).then_inc(tails_stored, 16)
                sp.dma_start(last_rows(g.out_conv_s), tails_T[H * KT:2 * H * KT, :]).then_inc(tails_stored, 16)
                sp.dma_start(one_row(g.out_h_p), tails_T[2 * H * KT:(2 * H + 1) * KT, :]).then_inc(tails_stored, 16)
                sp.dma_start(one_row(g.out_h_s), tails_T[(2 * H + 1) * KT:(2 * H + 2) * KT, :]).then_inc(tails_stored, 16)
                sp.wait_ge(tails_stored, 64)

            @block.gpsimd
            def _(pool):
                nc.gpsimd.memset(zrows[:, :], 0.0).then_inc(zrows_ready, 1)
                pool.wait_ge(zrows_ready, 1)
                with pool.Fori(0, KT) as c:
                    pool.wait_ge(ux_ready, c + 1)
                    alone(pool, g)
                    for table, start, rows, n in ((g.slot_x, 0, X_ROWS, X_CLEARS), (g.slot_y, EXPERTS * CAP, Y_ROWS, Y_CLEARS)):
                        for j in range(n):
                            pool.dma_start(table[bass.ds(c * (n * rows) + (start + j * rows), rows), :], zrows[0:rows, :])\
                                .then_inc(g.slots_cleared, 16)
                    pool.wait_ge(step_done, c + 2)
                    alone(pool, g)
                    pool.dma_start(g.y_T[bass.ds(c, 1)].rearrange("o p t -> (o p) t"), y_sb[:, :]).then_inc(y_stored, 16)
                    pool.wait_ge(y_stored, c * 16 + 16)
                    pool.sem_inc(y_free, 1)
                pool.wait_ge(g.slots_cleared, 16 * KT * (X_CLEARS + Y_CLEARS))

            @block.tensor
            def _(pe):
                def one_product(out, w):
                    for j in range(N_THIRDS):
                        for k in range(KT):
                            last = product(nc, out[:, j, 0:THIRD], [part[:, k, :] for part in w],
                                           [part[:, k, j * THIRD:(j + 1) * THIRD] for part in (g.xh, g.xl)], k == 0, k == KT - 1)
                    return last

                for free in (conv_ready, gel_ready, gate_taken):
                    pe.sem_inc(free, 1)
                with pe.Fori(0, KT) as c:
                    pe.wait_ge(x_split, c + 1)
                    pe.wait_ge(conv_ready, c + 1)
                    one_product(ux_ps, wx_split).then_inc(ux_ready, 1)
                    pe.wait_ge(g_split, c + 1)
                    pe.wait_ge(gel_ready, c + 1)
                    one_product(ug_ps, wg_split).then_inc(ug_ready, 1)
                    pe.wait_ge(bd_loaded, c * 64 + 64)
                    pe.wait_ge(u_ready, c + 1)
                    for m in range(GATE_UNITS):
                        c0, n = CHUNKS[m % 3]
                        pe.wait_ge(gate_taken, c * GATE_UNITS + max(m - 1, 0) + 1)
                        last = nc.tensor.matmul(gate_ps[:, m % 2, 0:n], bd[:, m // 3, :], u_sb[:, c0:c0 + n],
                                                start=True, stop=True)
                        last.then_inc(gate_ready, 1)
                pe.wait_ge(tails_ready, 1)
                nc.tensor.transpose(ux_ps[0:(2 * H + 2) * KT, 0, 0:P], tails[:, :, :].rearrange("p j c -> p (j c)"),
                                    g.ident[:, :]).then_inc(tails_turned, 1)

            @block.scalar
            def _(act):
                def round_x(c):
                    act.wait_ge(x_loaded, c * 16 + 16)
                    nc.scalar.copy(wx_split[0][:, :, :], w_x[:, :, :]).then_inc(x_rounded, 1)

                def round_g(c):
                    act.wait_ge(g_loaded, c * 16 + 16)
                    nc.scalar.copy(wg_split[0][:, :, :], w_g[:, :, :]).then_inc(g_rounded, 1)

                def step(c, more):
                    chain = Chain(act, chain_a, c * A_STEPS)
                    vec = lambda v: g.chan[:, bass.ds(c + v * KT, 1)]
                    act.wait_ge(ux_ready, c + 1)
                    chain(nc.scalar.copy(conv_in[:, H:H + 2 * THIRD].rearrange("p (j t) -> p j t", t=THIRD), ux_ps[:, 0:2, 0:THIRD]))
                    chain(nc.scalar.copy(conv_in[:, H + 2 * THIRD:H + T_PROMPT], ux_ps[:, 2, 0:T_PROMPT - 2 * THIRD]))
                    chain(nc.scalar.copy(conv_in[:, 2 * H + T_PROMPT:], ux_ps[:, 2, T_PROMPT - 2 * THIRD:T_ALL - 2 * THIRD]))
                    for j in range(H):
                        at = H + T_PROMPT + j
                        chain(nc.scalar.copy(conv_in[:, at:at + 1], vec(V_HIST + j)), conv_ready if j == H - 1 else None)
                    if more:
                        round_x(c + 1)
                    chain(nc.scalar.activation(warm[:, :], g.ident[:, 0:1], ACT.Sigmoid))
                    for m in range(GATE_UNITS):
                        c0, n = CHUNKS[m % 3]
                        act.wait_ge(gate_ready, c * GATE_UNITS + m + 1)
                        if m == 0:
                            act.wait_ge(step_done, c + 1)
                        dst = (r_sb, i_sb)[m // 3]
                        alone(act, g)
                        chain(nc.scalar.activation(dst[:, c0:c0 + n], gate_ps[:, m % 2, 0:n], ACT.Sigmoid,
                                                   bias=vec(V_BA + m // 3)), gate_taken)
                    act.sem_inc(ri_ready, 1)
                    lam = g.decay[:, bass.ds(c, 1)]
                    alone(act, g)
                    nc.scalar.activation(a_sb[:, :], r_sb[:, :], ACT.Exp, scale=lam).then_inc(at_ready, 1)
                    nc.scalar.activation(th_sb[:, :], r_sb[:, :], ACT.Tanh, scale=lam).then_inc(at_ready, 1)
                    act.wait_ge(at_ready, c * 2 + 2)
                    chain(nc.scalar.activation(gel[:, :].rearrange("p (j t) -> p j t", t=THIRD), ug_ps[:, :, 0:THIRD],
                                               ACT.Gelu_apprx_tanh), gel_ready)
                    if more:
                        round_g(c + 1)
                    act.wait_ge(var_ready, c + 1)
                    chain(nc.scalar.activation(v_sb[:, :], v_sb[:, :], ACT.Sqrt, scale=-1.0), std_ready)
                    chain.ended(A_STEPS)

                round_x(0)
                round_g(0)
                with act.Fori(0, KT - 1) as c:
                    step(c, True)
                step(KT - 1, False)

            @block.vector
            def _(dve):
                v = nc.vector
                edge = Chain(dve, chain_e)
                edge(v.memset(bd[:, :, :], 0.0), bd_cleared)
                edge(v.memset(conv_in[:, 0:H], 0.0))
                edge(v.memset(y_sb[:, T_ALL:T_WIDE], 0.0))

                def rest_x(c):
                    dve.wait_ge(x_rounded, c + 1)
                    v.tensor_tensor(wx_split[1][:, :, :], w_x[:, :, :], wx_split[0][:, :, :], ALU.subtract).then_inc(x_split, 1)

                def rest_g(c):
                    dve.wait_ge(g_rounded, c + 1)
                    v.tensor_tensor(wg_split[1][:, :, :], w_g[:, :, :], wg_split[0][:, :, :], ALU.subtract).then_inc(g_split, 1)

                def step(c, more):
                    chain = Chain(dve, chain_v, c * V_STEPS)
                    vec = lambda k: g.chan[:, bass.ds(c + k * KT, 1)]
                    dve.wait_ge(conv_ready, c + 2)
                    parts = ((0, T_PROMPT, 0), (T_PROMPT, T_SAMPLE, H + T_PROMPT))
                    for dst, n, src in parts:
                        chain(v.tensor_scalar(u_sb[:, dst:dst + n], conv_in[:, src + H:src + H + n], vec(V_CONV + H),
                                              vec(V_CONVB), ALU.mult, ALU.add))
                    for j in range(H):
                        for dst, n, src in parts:
                            chain(v.scalar_tensor_tensor(u_sb[:, dst:dst + n], conv_in[:, src + j:src + j + n],
                                                         vec(V_CONV + j), u_sb[:, dst:dst + n], ALU.mult, ALU.add))
                    chain(v.tensor_copy(tails[:, 0:H, bass.ds(c, 1)].rearrange("p j o -> p (j o)"), conv_in[:, T_PROMPT:T_PROMPT + H]))
                    end = H + T_PROMPT + T_SAMPLE
                    chain(v.tensor_copy(tails[:, H:2 * H, bass.ds(c, 1)].rearrange("p j o -> p (j o)"), conv_in[:, end:end + H]), u_ready)
                    if more:
                        rest_x(c + 1)
                    dve.wait_ge(ri_ready, c + 1)
                    chain(v.tensor_tensor(i_sb[:, :], i_sb[:, :], u_sb[:, :], ALU.mult))
                    dve.wait_ge(at_ready, c * 2 + 2)
                    chain(v.tensor_tensor(v_sb[:, :], a_sb[:, :], a_sb[:, :], ALU.mult))
                    chain(v.scalar_tensor_tensor(v_sb[:, :], v_sb[:, :], 1.0, th_sb[:, :], ALU.add, ALU.mult), var_ready)
                    if more:
                        rest_g(c + 1)
                    dve.wait_ge(std_ready, c + 1)
                    chain(v.tensor_tensor(i_sb[:, :], i_sb[:, :], v_sb[:, :], ALU.mult))
                    chain(v.tensor_tensor_scan(h_sb[:, 0:T_PROMPT], a_sb[:, 0:T_PROMPT], i_sb[:, 0:T_PROMPT], 0.0,
                                               ALU.mult, ALU.add))
                    chain(v.tensor_tensor_scan(h_sb[:, T_PROMPT:T_ALL], a_sb[:, T_PROMPT:T_ALL], i_sb[:, T_PROMPT:T_ALL],
                                               vec(V_H0), ALU.mult, ALU.add))
                    for n, at in enumerate((T_PROMPT - 1, T_ALL - 1)):
                        chain(v.tensor_copy(tails[:, 2 * H + n, bass.ds(c, 1)], h_sb[:, at:at + 1]))
                    dve.wait_ge(gel_ready, c + 2)
                    dve.wait_ge(y_free, c + 1)
                    chain(v.tensor_tensor(y_sb[:, 0:T_ALL], gel[:, 0:T_ALL], h_sb[:, :], ALU.mult), step_done)
                    chain.ended(V_STEPS)

                dve.sem_inc(step_done, 1)
                dve.sem_inc(y_free, 1)
                rest_x(0)
                rest_g(0)
                with dve.Fori(0, KT - 1) as c:
                    step(c, True)
                step(KT - 1, False)
                dve.sem_inc(tails_ready, 1)
                dve.wait_ge(tails_turned, 1)
                edge(v.tensor_copy(tails_T[0:(2 * H + 2) * KT, :], ux_ps[0:(2 * H + 2) * KT, 0, 0:P]), tails_kept)


def project(nc, g, sems, call, branch, w_out, gate_col, add, tag):
    with ExitStack() as ctx:
        sb = lambda name, shape, dt=F32: ctx.enter_context(nc.sbuf_tensor(tag + name, shape, dt))
        w_raw = sb("_w", [P, KT, P])
        wg_split, wp_split = ([sb(f"_{n}_{part}", [P, KT, P], F32R) for part in ("hi", "lo")] for n in ("wg", "wp"))
        b_parts = [sb(f"_b_{part}", [P, KT, T_WIDE], F32R) for part in ("hi", "lo")]
        sig = sb("_sig", [P, T_WIDE])
        b_raw = [sb("_b0", [P, T_WIDE]), sig]
        gate_ps = ctx.enter_context(nc.psum_tensor(tag + "_gate_ps", [P, N_THIRDS, BANK], F32))
        proj_ps = ctx.enter_context(nc.psum_tensor(tag + "_proj_ps", [P, N_THIRDS, BANK], F32))
        (g_loaded, p_loaded, b_loaded, g_rounded, p_rounded, b_rounded, g_split, p_split, b_split,
         gate_ready, proj_ready, sig_ready, proj_taken, chain_v) = sems
        before = call * KT
        V_BEFORE = call * KT
        thirds = lambda ap: ap.rearrange("p (j t) -> p j t", t=THIRD)
        w_out_k = w_out[0].rearrange("(k p) n -> p k n", p=P)

        with nc.Block() as block:
            @block.sync
            def _(sp):
                def load_g(c):
                    sp.dma_start(w_raw[:, :, :], g.w_in_k[:, :, bass.ds(c * P + gate_col, P)]).then_inc(g_loaded, 16)

                def load_p(c):
                    sp.dma_start(w_raw[:, :, :], w_out_k[:, :, bass.ds(c * P, P)]).then_inc(p_loaded, 16)

                load_g(0)
                for k in range(KT):
                    if k == 2:
                        sp.wait_ge(g_split, before + 1)
                        load_p(0)
                    if k >= 2:
                        sp.wait_ge(b_split, before + k - 1)
                    sp.dma_start(b_raw[k % 2][:, :], branch[k]).then_inc(b_loaded[k % 2], 16)
                with sp.Fori(0, KT - 1) as c:
                    sp.wait_ge(p_split, before + c + 1)
                    alone(sp, g)
                    load_g(c + 1)
                    sp.wait_ge(g_split, before + c + 2)
                    alone(sp, g)
                    load_p(c + 1)

            @block.tensor
            def _(pe):
                def one_product(out, w, x):
                    for j in range(N_THIRDS):
                        for k in range(KT):
                            last = product(nc, out[:, j, 0:THIRD], [part[:, k, :] for part in w],
                                           [part[:, k, j * THIRD:(j + 1) * THIRD] for part in x], k == 0, k == KT - 1)
                    return last

                if call == 0:
                    pe.sem_inc(sig_ready, 1)
                    pe.sem_inc(proj_taken, 1)
                with pe.Fori(0, KT) as c:
                    pe.wait_ge(g_split, before + c + 1)
                    pe.wait_ge(sig_ready, before + c + 1)
                    one_product(gate_ps, wg_split, (g.xh, g.xl)).then_inc(gate_ready, 1)
                    pe.wait_ge(b_split, before + KT)
                    pe.wait_ge(p_split, before + c + 1)
                    pe.wait_ge(proj_taken, before + c + 1)
                    one_product(proj_ps, wp_split, b_parts).then_inc(proj_ready, 1)

            @block.scalar
            def _(act):
                def round_g(c):
                    act.wait_ge(g_loaded, (before + c) * 16 + 16)
                    nc.scalar.copy(wg_split[0][:, :, :], w_raw[:, :, :]).then_inc(g_rounded, 1)

                def round_p(c):
                    act.wait_ge(p_loaded, (before + c) * 16 + 16)
                    nc.scalar.copy(wp_split[0][:, :, :], w_raw[:, :, :]).then_inc(p_rounded, 1)

                def step(c, more):
                    act.wait_ge(gate_ready, before + c + 1)
                    act.wait_ge(b_split, before + KT)
                    act.wait_ge(proj_taken, before + c + 1)
                    nc.scalar.activation(thirds(sig[:, :]), gate_ps[:, :, 0:THIRD], ACT.Sigmoid).then_inc(sig_ready, 1)
                    if more:
                        round_g(c + 1)
                        act.wait_ge(proj_ready, before + c + 1)
                        round_p(c + 1)

                round_g(0)
                for k in range(KT):
                    if k == 2:
                        round_p(0)
                    act.wait_ge(b_loaded[k % 2], 16 * (before // 2 + k // 2 + 1))
                    nc.scalar.copy(b_parts[0][:, k, :], b_raw[k % 2][:, :]).then_inc(b_rounded, 1)
                with act.Fori(0, KT - 1) as c:
                    step(c, True)
                step(KT - 1, False)

            @block.vector
            def _(dve):
                v = nc.vector

                def rest_g(c):
                    dve.wait_ge(g_rounded, before + c + 1)
                    v.tensor_tensor(wg_split[1][:, :, :], w_raw[:, :, :], wg_split[0][:, :, :], ALU.subtract).then_inc(g_split, 1)

                def rest_p(c):
                    dve.wait_ge(p_rounded, before + c + 1)
                    v.tensor_tensor(wp_split[1][:, :, :], w_raw[:, :, :], wp_split[0][:, :, :], ALU.subtract).then_inc(p_split, 1)

                V_STEPS = 2 if add else 1

                def step(c, more):
                    chain = Chain(dve, chain_v, V_BEFORE + c * V_STEPS)
                    if more:
                        rest_g(c + 1)
                    dve.wait_ge(proj_ready, before + c + 1)
                    dve.wait_ge(sig_ready, before + c + 2)
                    m = g.mT[:, bass.ds(c, 1), 0:T_WIDE].rearrange("p o t -> p (o t)")
                    if add:
                        chain(v.tensor_tensor(thirds(sig[:, :]), thirds(sig[:, :]), proj_ps[:, :, 0:THIRD], ALU.mult))
                        chain(v.tensor_tensor(m, m, sig[:, :], ALU.add), proj_taken)
                    else:
                        chain(v.tensor_tensor(thirds(m), thirds(sig[:, :]), proj_ps[:, :, 0:THIRD], ALU.mult), proj_taken)
                    chain.ended(V_STEPS)
                    if more:
                        rest_p(c + 1)

                rest_g(0)
                for k in range(KT):
                    if k == 2:
                        rest_p(0)
                    dve.wait_ge(b_rounded, before + k + 1)
                    v.tensor_tensor(b_parts[1][:, k, :], b_raw[k % 2][:, :], b_parts[0][:, k, :], ALU.subtract).then_inc(b_split, 1)
                with dve.Fori(0, KT - 1) as c:
                    step(c, True)
                step(KT - 1, False)


def attend(nc, g):
    UNITS = [(n % 2, n // 2) for n in range(2 * PT)] + ["stream"]
    NU = len(UNITS)
    STREAM = NU - 1
    tiles_of = lambda n: PAST_TILES + 1 if n == STREAM else UNITS[n][1] + 1
    groups_of = lambda n: [list(range(j, min(j + 4, tiles_of(n)))) for j in range(0, tiles_of(n), 4)]
    NG = sum(len(groups_of(n)) for n in range(NU))
    first_group = lambda n: sum(len(groups_of(m)) for m in range(n))
    end_group = lambda n: first_group(n) + len(groups_of(n))
    owner = [(n, js) for n in range(NU) for js in groups_of(n)]
    PAST_TURNS = 2 * PAST_TILES // 4
    HALVES_AT = (0, 0, 1, 1, 2, 2, 3, 4, 5, 6, 7, 8, 9, 10, 11, 12, 13, 14)
    PROJECTED_AT = HALVES_AT[1::2]
    PAST_AT = (5, 7, 8, 9, 11, 12, 13, 14)
    assert len(HALVES_AT) == 2 * NT and len(PAST_AT) == PAST_TURNS
    O_TURNS = PT // 4 + 1
    NORM_PARTS = 3
    FIRST_O = 2 * PT // 2 + 2
    TAKE_QK_ACT = 3

    def turns_of(ahead):
        order = []
        for n in range(STREAM):
            if n in PAST_AT:
                order.append(("past", PAST_AT.index(n)))
            if n == FIRST_O:
                order.append(("o", 0))
            order += [("p", q) for q in range(first_group(n), end_group(n))]
        if ahead:
            order += [("qk", t) for t in range(NT)]
        order += [("p", first_group(STREAM)), ("o", 1)]
        order += [("p", q) for q in range(first_group(STREAM) + 1, NG)] + [("o", 2)]
        return {use: m for m, use in enumerate(order)}

    TURNS, TURNS_LAST = turns_of(True), turns_of(False)
    USES = len(TURNS)
    in_bank = lambda m, b: (m + 1 - b) // 2

    with ExitStack() as ctx:
        sb = lambda name, shape, dt=F32: ctx.enter_context(nc.sbuf_tensor(name, shape, dt))
        w_qkv, w_parts = g.w_qkv, g.w_parts
        out_T = sb("out_T", [P, T_WIDE])
        gain = sb("qk_gain", [P, 4, HD])
        qk_sb = sb("qk_sb", [P, NT, 4, HD])
        v_next, v_new = sb("v_next", [P, NT, P]), sb("v_new", [P, NT, P])
        squares = sb("qk_squares", [P, 2, 4, HD])
        rstd = sb("qk_rstd", [P, NT, 4])
        qkT, spare = g.qkT, g.mT[:, :, :].rearrange("p k t -> p (k t)")
        kT_past = spare[0:HD + 1, 0:2 * PAST].rearrange("p (h t) -> p h t", h=2)
        k_past, v_past = (spare[:, 2 * PAST + n * PAST:3 * PAST + n * PAST].rearrange("p (t d) -> p t d", d=P) for n in range(2))
        o_sb = spare[:, 4 * PAST:4 * PAST + PT * P].rearrange("p (t d) -> p t d", d=P)
        probs_s = sb("probs_s", [P, KV_SAMPLE])
        probs = [probs_s[:, b * T_PROMPT:(b + 1) * T_PROMPT] for b in range(2)]
        probsT = [sb(f"probsT{b}", [P, BANK]) for b in range(2)]
        warm = sb("warm", [P, 1])
        neg_max, total = sb("neg_max", [P, NU + 2]), sb("exp_total", [P, NU + 1])
        o_s = sb("o_s", [P, P])
        scores = ctx.enter_context(nc.psum_tensor("scores", [P, 4 * BANK], F32))
        turn_ps = ctx.enter_context(nc.psum_tensor("turn_ps", [P, 2, BANK], F32))
        out_ps = ctx.enter_context(nc.psum_tensor("out_ps", [P, BANK], F32))
        proj_ps = ctx.enter_context(nc.psum_tensor("proj_ps", [P, BANK], F32))
        tail = proj_ps[:, 0:T_SAMPLE]
        half = lambda n: scores[:, (n % 2) * 2 * BANK:(n % 2 + 1) * 2 * BANK]

        sem = lambda name: g.sem("a_" + name)
        gain_loaded, past_k_loaded, past_v_loaded, c_loaded = sem("gain_loaded"), sem("k_loaded"), sem("v_loaded"), sem("c_loaded")
        kv_ready, kv_stored, v_copied = sem("kv_ready"), sem("kv_stored"), sem("v_copied")
        w_loaded, w_rounded, w_split = g.w_loaded, g.w_rounded, g.w_split
        pair_done, pair_stored = sem("pair_done"), sem("pair_stored")
        qkv_ready, tile_taken, sq_summed = sem("qkv_ready"), sem("tile_taken"), sem("sq_summed")
        mean_ready, rstd_ready = sem("mean_ready"), sem("rstd_ready")
        turned = sem("turned")
        turn_taken = [sem(f"turn_taken{b}") for b in range(2)]
        scores_ready, max_ready, exp_ready = sem("scores_ready"), sem("max_ready"), sem("exp_ready")
        half_ready = sem("half_ready")
        pv_done, out_taken = sem("pv_done"), sem("out_taken")
        chain_v, chain_a, chain_g = sem("chain_v"), sem("chain_a"), sem("chain_g")
        turned_count = lambda i, m: NT + i * USES + m + 1
        taken_before = lambda i, m: in_bank(NT, m % 2) + i * in_bank(USES, m % 2) + m // 2

        with nc.Block() as block:
            @block.sync
            def _(sp):
                for n, vec in enumerate((g.q_norm_g, g.q_norm_g, g.k_norm_g, g.k_norm_g)):
                    sp.dma_start(gain[:, n, :], row(vec[0]).to_broadcast([P, HD])).then_inc(gain_loaded, 16)
                heads = lambda ap, p: ap.rearrange("(t p) h d -> p t (h d)", p=P)[:, :, bass.ds(p * P, P)]

                def load_past_k(p):
                    sp.dma_start(k_past[:, :, :], heads(g.cache_k[0, 0], p)).then_inc(past_k_loaded, 16)

                def store_kv(p):
                    sp.wait_ge(kv_ready, p + 1)
                    sp.dma_start(heads(g.out_k_p[0, 0], p), qk_sb[:, 0:PT, 2:4, :].rearrange("p t h d -> p t (h d)")).then_inc(kv_stored, 16)
                    sp.dma_start(heads(g.out_v_p[0, 0], p), v_next[:, 0:PT, :]).then_inc(kv_stored, 16)
                    stream = lambda ap: ap.rearrange("t h d -> t (h d)")[:, bass.ds(p * P, P)]
                    sp.dma_start(stream(g.out_k_s[0, 0]), qk_sb[0:T_SAMPLE, PT, 2:4, :].rearrange("p h d -> p (h d)")).then_inc(kv_stored, 16)
                    sp.dma_start(stream(g.out_v_s[0, 0]), v_next[0:T_SAMPLE, PT, :]).then_inc(kv_stored, 16)

                def past_turned(i):
                    sp.wait_ge(turned, turned_count(i, TURNS["past", PAST_TURNS - 1]))

                def store_out(i):
                    sp.wait_ge(pair_done, i + 1)
                    alone(sp, g)
                    sp.dma_start(g.attn_T[bass.ds(i, 1)].rearrange("o p t -> (o p) t"), out_T[:, :]).then_inc(pair_stored, 16)

                load_qkv(sp, g, 1)
                load_past_k(0)
                store_kv(0)
                with sp.Fori(0, PAIRS - 2) as i:
                    sp.wait_ge(w_split, i + 2)
                    alone(sp, g)
                    load_qkv(sp, g, i + 2)
                    store_kv(i + 1)
                    past_turned(i)
                    load_past_k(i + 1)
                    store_out(i)
                store_kv(PAIRS - 1)
                past_turned(PAIRS - 2)
                load_past_k(PAIRS - 1)
                store_out(PAIRS - 2)
                store_out(PAIRS - 1)
                sp.wait_ge(kv_stored, PAIRS * 64)
                sp.wait_ge(pair_stored, PAIRS * 16 + 16)

            @block.gpsimd
            def _(pool):
                def load_c(p):
                    pool.dma_start(qkT[HD:HD + 1, 2:4, 0:T_ALL], g.neg_c_new[bass.ds(p * 2, 2), :].unsqueeze(0)).then_inc(c_loaded, 16)
                    pool.dma_start(kT_past[HD:HD + 1, :, :], g.neg_c_past[bass.ds(p * 2, 2), :].unsqueeze(0)).then_inc(c_loaded, 16)

                def take_v(p):
                    pool.wait_ge(kv_ready, p + 1)
                    alone(pool, g)
                    nc.gpsimd.tensor_copy(v_new[:, :, :], v_next[:, :, :]).then_inc(v_copied, 1)

                def load_past_v(p):
                    pool.dma_start(v_past[:, :, :], g.cache_v[0, 0].rearrange("(t p) h d -> p t (h d)", p=P)[:, :, bass.ds(p * P, P)])\
                        .then_inc(past_v_loaded, 16)

                def rest_w(p):
                    pool.wait_ge(w_rounded, p + 1)
                    alone(pool, g)
                    nc.gpsimd.tensor_tensor(w_parts[1][:, :, :], w_qkv[:, :, :], w_parts[0][:, :, :], ALU.subtract).then_inc(w_split, 1)

                load_c(0)
                load_past_v(0)
                rest_w(1)
                take_v(0)

                def step(i, more):
                    if more:
                        rest_w(i + 2)
                    pool.wait_ge(scores_ready, (i + 1) * NU)
                    load_c(i + 1)
                    pool.wait_ge(pv_done, (i + 1) * NG)
                    take_v(i + 1)
                    load_past_v(i + 1)

                with pool.Fori(0, PAIRS - 2) as i:
                    step(i, True)
                step(PAIRS - 2, False)

            @block.tensor
            def _(pe):
                te = nc.tensor

                def project_half(t, part, acc):
                    for k in range(part * KT // 2, (part + 1) * KT // 2):
                        last = product(nc, acc[:, 0:QKV], [x[:, k, t * P:(t + 1) * P] for x in (g.xh, g.xl)],
                                       [w[:, k, :] for w in w_parts], k == 0, k == KT - 1)
                    if part:
                        last.then_inc(qkv_ready, 1)

                def turn_qk(t, bank):
                    for n in range(4):
                        last = te.transpose(turn_ps[0:HD, bank, n * P:(n + 1) * P], qk_sb[:, t, n, :], g.ident[:, :])
                    last.then_inc(turned, 1)

                pe.wait_ge(w_split, 1)
                for t in range(NT):
                    if t >= 2:
                        pe.wait_ge(tile_taken, 3 * (t - 1))
                    for part in range(2):
                        project_half(t, part, (proj_ps, out_ps)[t % 2])
                pe.wait_ge(kv_ready, 1)
                for t in range(NT):
                    if t >= 2:
                        pe.wait_ge(turn_taken[t % 2], t // 2)
                    turn_qk(t, t % 2)

                def step(i, ahead):
                    use = TURNS if ahead else TURNS_LAST

                    def bank_of(*which):
                        m = use[which]
                        pe.wait_ge(turn_taken[m % 2], taken_before(i, m))
                        return m % 2

                    def score(n):
                        if n == STREAM:
                            pe.wait_ge(exp_ready, i * NU + n)
                            b = use["past", PAST_TURNS - 1]
                            for m in (b - 1, b):
                                pe.wait_ge(turn_taken[m % 2], taken_before(i, m) + 1)
                            for c in range(PAST // BANK):
                                if c == PAST // BANK // 2:
                                    last.then_inc(half_ready, 1)
                                for h in range(2):
                                    last = te.matmul(scores[h * 64:(h + 1) * 64, c * BANK:(c + 1) * BANK],
                                              qkT[:, h, T_PROMPT:T_ALL], kT_past[:, h, c * BANK:(c + 1) * BANK],
                                              start=True, stop=True)
                            for h in range(2):
                                te.matmul(tail[h * 64:(h + 1) * 64, :], qkT[:, h, T_PROMPT:T_ALL],
                                          qkT[:, 2 + h, T_PROMPT:T_ALL], start=True, stop=False, skip_group_check=True)
                            te.matmul(tail, g.ident_bf[:, :], g.causal_s[:, :], start=False, stop=True,
                                      skip_group_check=True).then_inc(scores_ready, 1)
                            return
                        h, t = UNITS[n]
                        if n >= 2:
                            pe.wait_ge(exp_ready, i * NU + n - 1)
                        for c0 in range(0, (t + 1) * P, BANK):
                            w = min(BANK, (t + 1) * P - c0)
                            diagonal = c0 + w == (t + 1) * P
                            te.matmul(half(n)[:, c0:c0 + w], qkT[:, h, t * P:(t + 1) * P], qkT[:, 2 + h, c0:c0 + w],
                                      start=True, stop=not diagonal)
                        te.matmul(half(n)[:, t * P:(t + 1) * P], g.ident_bf[:, :], g.causal[:, :],
                                  start=False, stop=True).then_inc(scores_ready, 1)

                    def turn_past(s):
                        h, c = s // (PAST_TILES // 4), s % (PAST_TILES // 4)
                        if s == 0:
                            pe.wait_ge(past_k_loaded, i * 16 + 16)
                        bank = bank_of("past", s)
                        alone(pe, g)
                        for n in range(4):
                            last = te.transpose(turn_ps[0:HD, bank, n * P:(n + 1) * P],
                                                k_past[:, c * 4 + n, h * HD:(h + 1) * HD], g.ident[:, :])
                        last.then_inc(turned, 1)

                    def turn_group(q):
                        n, js = owner[q]
                        bank = bank_of("p", q)
                        if js[0] == PAST_TILES:
                            alone(pe, g)
                        src = probs_s if n == STREAM else probs[n % 2]
                        for s, j in enumerate(js):
                            w = T_SAMPLE if j == PAST_TILES else P
                            last = te.transpose(turn_ps[0:w, bank, s * P:(s + 1) * P], src[:, j * P:j * P + w], g.ident[:, :])
                        last.then_inc(turned, 1)

                    def weigh_group(q):
                        n, js = owner[q]
                        m = use["p", q]
                        pe.wait_ge(turn_taken[m % 2], taken_before(i, m) + 1)
                        if q == 0:
                            pe.wait_ge(v_copied, i + 1)
                        elif js[0] == 0:
                            pe.wait_ge(out_taken, i * NU + n)
                        for s, j in enumerate(js):
                            flags = dict(start=(j == 0), stop=(j == tiles_of(n) - 1))
                            pt = probsT[q % 2][:, s * P:(s + 1) * P]
                            if n == STREAM and j == PAST_TILES:
                                last = te.matmul(out_ps[:, 0:P], pt[0:T_SAMPLE, :], v_new[0:T_SAMPLE, PT, :], **flags)
                            elif n == STREAM:
                                last = te.matmul(out_ps[:, 0:P], pt, v_past[:, j, :], **flags)
                            else:
                                h = UNITS[n][0]
                                last = te.matmul(out_ps[:, 0:HD], pt, v_new[:, j, h * HD:(h + 1) * HD], **flags)
                        last.then_inc(pv_done, 1)

                    def turn_out(s):
                        pe.wait_ge(out_taken, i * NU + (s + 1) * 8)
                        bank = bank_of("o", s)
                        for n in range(4):
                            last = te.transpose(turn_ps[:, bank, n * P:(n + 1) * P], o_sb[:, s * 4 + n, :], g.ident[:, :])
                        last.then_inc(turned, 1)

                    pe.wait_ge(c_loaded, i * 32 + 32)
                    for b in range(2):
                        pe.wait_ge(turn_taken[b], taken_before(i, b))
                    score(0)
                    for n in range(STREAM):
                        if n + 1 < STREAM:
                            score(n + 1)
                        if n:
                            weigh_group(first_group(n) - 1)
                        for x, at in enumerate(HALVES_AT):
                            if not ahead or at != n:
                                continue
                            if x == 0:
                                pe.wait_ge(w_split, i + 2)
                            elif x % 2 == 0:
                                pe.wait_ge(tile_taken, 3 * ((i + 1) * NT + x // 2))
                            project_half(x // 2, x % 2, proj_ps)
                        if n in PAST_AT:
                            turn_past(PAST_AT.index(n))
                        if n == FIRST_O:
                            turn_out(0)
                        pe.wait_ge(exp_ready, i * NU + n + 1)
                        for q in range(first_group(n), end_group(n)):
                            turn_group(q)
                            if q > first_group(n):
                                weigh_group(q - 1)
                    score(STREAM)
                    weigh_group(first_group(STREAM) - 1)
                    if ahead:
                        pe.wait_ge(kv_ready, i + 2)
                        for t in range(NT):
                            bank = bank_of("qk", t)
                            alone(pe, g)
                            turn_qk(t, bank)
                    pe.wait_ge(exp_ready, (i + 1) * NU)
                    pe.wait_ge(past_v_loaded, i * 16 + 16)
                    for q in range(first_group(STREAM), NG):
                        turn_group(q)
                        if q > first_group(STREAM):
                            weigh_group(q - 1)
                        else:
                            turn_out(1)
                    weigh_group(NG - 1)
                    pe.wait_ge(out_taken, (i + 1) * NU)
                    te.transpose(turn_ps[:, bank_of("o", 2), 0:P], o_s[:, :], g.ident[:, :]).then_inc(turned, 1)

                with pe.Fori(0, PAIRS - 1) as i:
                    step(i, True)
                step(PAIRS - 1, False)

            @block.scalar
            def _(act):
                sc = nc.scalar

                def take_tile(p, t, acc, first=False):
                    act.wait_ge(qkv_ready, p * NT + t + 1)
                    sc.copy(v_next[:, t, :], acc[:, 2 * P:QKV]).then_inc(tile_taken, 1)
                    q_and_k = acc[:, 0:2 * P].rearrange("p (n d) -> p n d", n=4)
                    sc.copy(qk_sb[:, t, :, :], q_and_k).then_inc(tile_taken, 1)
                    if not first or t >= 2:
                        act.wait_ge(sq_summed, p * NT + max(t - 1, 0))
                    sc.activation(squares[:, t % 2, :, :], q_and_k, ACT.Square).then_inc(tile_taken, 1)

                def round_w(p):
                    act.wait_ge(w_loaded, p * 48 + 48)
                    sc.copy(w_parts[0][:, :, :], w_qkv[:, :, :]).then_inc(w_rounded, 1)

                def root(p):
                    act.wait_ge(mean_ready, p + 1)
                    sc.activation(rstd[:, :, :], rstd[:, :, :], ACT.Sqrt).then_inc(rstd_ready, 1)

                def take_qk(chain, t, bank):
                    chain(sc.copy(qkT[0:HD, :, t * P:(t + 1) * P],
                                  turn_ps[0:HD, bank, :].rearrange("p (n c) -> p n c", n=4)), turn_taken[bank])

                A_FIRST = NT
                A_STEPS = TAKE_QK_ACT + PAST_TURNS + NU + 2
                chain = Chain(act, chain_a)
                for t in range(NT):
                    take_tile(0, t, (proj_ps, out_ps)[t % 2], first=True)
                root(0)
                round_w(1)
                for t in range(NT):
                    act.wait_ge(turned, t + 1)
                    take_qk(chain, t, t % 2)
                chain.ended(A_FIRST)

                def step(i, ahead, more):
                    use = TURNS if ahead else TURNS_LAST
                    chain = Chain(act, chain_a, i * A_STEPS + A_FIRST)

                    def exp(n):
                        act.wait_ge(max_ready, i * NU + n + 1)
                        if n >= 2:
                            act.wait_ge(turned, turned_count(i, use["p", end_group(n - 1 if n == STREAM else n - 2) - 1]))
                        if n < STREAM:
                            w = (UNITS[n][1] + 1) * P
                            chain(sc.activation(probs[n % 2][:, 0:w], half(n)[:, 0:w], ACT.Exp, bias=neg_max[:, n:n + 1],
                                                accum_out=total[:, n:n + 1]), exp_ready)
                        else:
                            chain(sc.activation(probs_s[:, 0:PAST], scores[:, :], ACT.Exp, bias=neg_max[:, n:n + 1],
                                                accum_out=total[:, n:n + 1]))
                            chain(sc.activation(probs_s[:, PAST:], tail, ACT.Exp, bias=neg_max[:, n:n + 1],
                                                accum_out=total[:, n + 1:n + 2]), exp_ready)

                    exp(0)
                    for n in range(STREAM):
                        if n + 1 < STREAM:
                            exp(n + 1)
                        if ahead and n == 0:
                            act.wait_ge(kv_stored, i * 64 + 64)
                            act.wait_ge(v_copied, i + 1)
                        if ahead and n in PROJECTED_AT:
                            take_tile(i + 1, PROJECTED_AT.index(n), proj_ps)
                        if n in PAST_AT:
                            s = PAST_AT.index(n)
                            m = use["past", s]
                            h, c = s // (PAST_TILES // 4), s % (PAST_TILES // 4)
                            act.wait_ge(turned, turned_count(i, m))
                            chain(sc.copy(kT_past[0:HD, h, c * BANK:(c + 1) * BANK], turn_ps[0:HD, m % 2, :]), turn_taken[m % 2])
                    if ahead:
                        root(i + 1)
                        if more:
                            round_w(i + 2)
                        chain(sc.activation(warm[:, :], g.ident[:, 0:1], ACT.Exp))
                        for t in range(TAKE_QK_ACT):
                            m = use["qk", t]
                            act.wait_ge(turned, turned_count(i, m))
                            take_qk(chain, t, m % 2)
                    exp(STREAM)
                    if ahead:
                        chain.ended(A_STEPS)

                with act.Fori(0, PAIRS - 2) as i:
                    step(i, True, True)
                step(PAIRS - 2, True, False)
                step(PAIRS - 1, False, False)

            @block.vector
            def _(dve):
                v = nc.vector
                edge = Chain(dve, chain_g)
                edge(v.memset(out_T[:, T_ALL:T_WIDE], 0.0))
                dve.sem_inc(pair_stored, 16)
                dve.wait_ge(gain_loaded, 64)
                edge(v.tensor_scalar(gain[:, 0:2, :], gain[:, 0:2, :], HD ** -0.5, None, ALU.mult))

                def sum_squares(chain, p, t):
                    dve.wait_ge(tile_taken, 3 * (p * NT + t + 1))
                    chain(v.reduce_sum(rstd[:, t, :], squares[:, t % 2, :, :], axis=X_AXIS), sq_summed)

                def mean(chain):
                    chain(v.tensor_scalar(rstd[:, :, :], rstd[:, :, :], 1.0 / HD, EPS, ALU.mult, ALU.add))
                    chain(v.reciprocal(rstd[:, :, :], rstd[:, :, :]), mean_ready)

                def norm_part(chain, p, s):
                    if s == 0:
                        dve.wait_ge(rstd_ready, p + 1)
                    n = NT // NORM_PARTS
                    part = qk_sb[:, s * n:(s + 1) * n, :, :]
                    chain(v.tensor_tensor(part, part, rstd[:, s * n:(s + 1) * n, :].unsqueeze(3).to_broadcast([P, n, 4, HD]), ALU.mult))
                    chain(v.tensor_tensor(part, part, gain[:, :, :].unsqueeze(1).to_broadcast([P, n, 4, HD]), ALU.mult),
                          kv_ready if s == NORM_PARTS - 1 else None)

                V_FIRST = NT + 2 + 2 * NORM_PARTS
                V_STEPS = V_FIRST + NT - TAKE_QK_ACT + (NU + 3) + NG + 2 * NU + 1 + PT // 4 + 2
                chain = Chain(dve, chain_v)
                for t in range(NT):
                    sum_squares(chain, 0, t)
                mean(chain)
                for s in range(NORM_PARTS):
                    norm_part(chain, 0, s)
                chain.ended(V_FIRST)

                def step(i, ahead):
                    use = TURNS if ahead else TURNS_LAST
                    chain = Chain(dve, chain_v, i * V_STEPS + V_FIRST)

                    def maximum(n):
                        dve.wait_ge(scores_ready, i * NU + n + 1)
                        if n < STREAM:
                            chain(v.tensor_reduce(neg_max[:, n:n + 1], half(n)[:, 0:(UNITS[n][1] + 1) * P], X_AXIS, ALU.max,
                                                  negate=True), max_ready)
                        else:
                            chain(v.tensor_reduce(neg_max[:, n:n + 1], half(1), X_AXIS, ALU.max, negate=True))
                            chain(v.tensor_reduce(neg_max[:, n + 1:n + 2], tail, X_AXIS, ALU.max, negate=True))
                            chain(v.tensor_reduce(neg_max[:, n:n + 1], neg_max[:, n:n + 3], X_AXIS, ALU.min), max_ready)

                    def take_group(q):
                        n, js = owner[q]
                        m = use["p", q]
                        dve.wait_ge(turned, turned_count(i, m))
                        if q >= 2:
                            dve.wait_ge(pv_done, i * NG + q - 1)
                        rows = T_SAMPLE if js[0] == PAST_TILES else P
                        chain(v.tensor_copy(probsT[q % 2][0:rows, 0:len(js) * P], turn_ps[0:rows, m % 2, 0:len(js) * P]),
                              turn_taken[m % 2])

                    def take_out(n):
                        if n == STREAM:
                            chain(v.tensor_tensor(total[:, n:n + 1], total[:, n:n + 1], total[:, n + 1:n + 2], ALU.add))
                        chain(v.reciprocal(total[:, n:n + 1], total[:, n:n + 1]))
                        dve.wait_ge(pv_done, i * NG + end_group(n))
                        if n == STREAM:
                            chain(v.tensor_scalar(o_s[:, :], out_ps[:, 0:P], total[:, n:n + 1], None, ALU.mult), out_taken)
                        else:
                            h, t = UNITS[n]
                            chain(v.tensor_scalar(o_sb[:, t, h * HD:(h + 1) * HD], out_ps[:, 0:HD], total[:, n:n + 1],
                                                  None, ALU.mult), out_taken)

                    def take_turned_out(s):
                        m = use["o", s]
                        dve.wait_ge(turned, turned_count(i, m))
                        if s == 0:
                            dve.wait_ge(pair_stored, i * 16 + 16)
                        chain(v.tensor_copy(out_T[:, s * BANK:(s + 1) * BANK], turn_ps[:, m % 2, :]), turn_taken[m % 2])

                    maximum(0)
                    for n in range(STREAM):
                        if n + 1 < STREAM:
                            maximum(n + 1)
                        if n:
                            take_out(n - 1)
                        if n == FIRST_O:
                            take_turned_out(0)
                        take_group(first_group(n))
                        if ahead and n in PROJECTED_AT:
                            sum_squares(chain, i + 1, PROJECTED_AT.index(n))
                            if n == PROJECTED_AT[-1]:
                                mean(chain)
                        for q in range(first_group(n) + 1, end_group(n)):
                            take_group(q)
                    if ahead:
                        norm_part(chain, i + 1, 0)
                        norm_part(chain, i + 1, 1)
                    dve.wait_ge(half_ready, i + 1)
                    chain(v.tensor_reduce(neg_max[:, STREAM + 2:STREAM + 3], half(0), X_AXIS, ALU.max, negate=True))
                    if ahead:
                        norm_part(chain, i + 1, 2)
                    maximum(STREAM)
                    take_out(STREAM - 1)
                    if ahead:
                        for t in range(TAKE_QK_ACT, NT):
                            m = use["qk", t]
                            dve.wait_ge(turned, turned_count(i, m))
                            chain(v.tensor_copy(qkT[0:HD, :, t * P:(t + 1) * P],
                                                turn_ps[0:HD, m % 2, :].rearrange("p (n c) -> p n c", n=4)), turn_taken[m % 2])
                    for q in range(first_group(STREAM), NG):
                        take_group(q)
                        if q == first_group(STREAM):
                            take_turned_out(1)
                    take_out(STREAM)
                    m = use["o", 2]
                    dve.wait_ge(turned, turned_count(i, m))
                    for h in range(2):
                        rows = slice(h * HD, (h + 1) * HD)
                        chain(v.tensor_copy(out_T[rows, T_PROMPT:T_ALL], turn_ps[rows, m % 2, rows]),
                              turn_taken[m % 2] if h else None)
                    dve.sem_inc(pair_done, 1)
                    if ahead:
                        chain.ended(V_STEPS)

                with dve.Fori(0, PAIRS - 1) as i:
                    step(i, True)
                step(PAIRS - 1, False)


def merge(nc, g, w, x1, xn2, logits):
    R = GROUPS + EXPERTS
    with ExitStack() as ctx:
        sb = lambda name, shape, dt=F32: ctx.enter_context(nc.sbuf_tensor("m_" + name, shape, dt))
        w_o = sb("w_o", [P, KT, D])
        w_r = sb("w_r", [P, KT, R])
        gain = sb("gain", [P, D])
        ss = sb("ss", [P, NT])
        turned_sb = [sb(f"turned{b}", [P, KT, P]) for b in range(2)]
        prod = ctx.enter_context(nc.psum_tensor("m_prod", [P, 2, D], F32))
        turn_ps = ctx.enter_context(nc.psum_tensor("m_turn", [P, KT, P], F32))
        logit_ps = ctx.enter_context(nc.psum_tensor("m_logits", [P, NT, R], F32))
        sem = lambda name: g.sem("m_" + name)
        w_loaded, r_loaded, x_loaded, prod_ready, x1_ready, sq_ready, mean_ready, rstd_ready, xn2_ready = (
            [sem(f"w_loaded{c}") for c in range(2)], sem("r_loaded"), sem("x_loaded"), sem("prod_ready"), sem("x1_ready"), sem("sq_ready"),
            sem("mean_ready"), sem("rstd_ready"), sem("xn2_ready"))
        turned, turn_taken, logits_ready, chain_v, chain_a, tail_clear = (sem("turned"), sem("turn_taken"), sem("logits_ready"),
                                                                          sem("chain_v"), sem("chain_a"), sem("tail_clear"))
        rows = lambda t: T_SAMPLE if t == PT else P

        with nc.Block() as block:
            @block.sync
            def _(sp):
                for c in range(D // BANK):
                    sp.dma_start(w_o[:, :, c * BANK:(c + 1) * BANK],
                                 g.w_o[0].rearrange("(k p) n -> p k n", p=P)[:, :, c * BANK:(c + 1) * BANK]).then_inc(w_loaded[c], 16)
                sp.dma_start(x1[:, 0:PT, :], g.x_prompt[0].rearrange("(t p) n -> p t n", p=P)).then_inc(x_loaded, 16)
                sp.dma_start(x1[0:T_SAMPLE, PT, :], g.x_sample[0]).then_inc(x_loaded, 16)
                sp.dma_start(gain[:, :], row(g.norm2_g[0]).to_broadcast([P, D])).then_inc(r_loaded, 16)
                sp.dma_start(w_r[:, :, 0:GROUPS], g.w_route_group[0].rearrange("(k p) n -> p k n", p=P)).then_inc(r_loaded, 16)
                sp.dma_start(w_r[:, :, GROUPS:], g.w_route_expert[0].rearrange("(k p) n -> p k n", p=P)).then_inc(r_loaded, 16)
                w.load_in(sp, g, 0, 0)
                w.load_down(sp, g, 0, 0)

            @block.gpsimd
            def _(pool):
                nc.gpsimd.memset(x1[T_SAMPLE:P, PT, :], 0.0).then_inc(tail_clear, 1)

            @block.tensor
            def _(pe):
                te = nc.tensor

                def route_tile(t):
                    pe.wait_ge(xn2_ready, t + 1)
                    if t:
                        pe.wait_ge(turn_taken, t)
                    for k in range(KT):
                        last = te.transpose(turn_ps[:, k, :], xn2[:, t, k * P:(k + 1) * P], g.ident[:, :])
                    last.then_inc(turned, 1)

                def logit_tile(t):
                    pe.wait_ge(turn_taken, t + 1)
                    pe.wait_ge(r_loaded, 48)
                    for k in range(KT):
                        last = te.matmul(logit_ps[:, t, :], turned_sb[t % 2][:, k, :], w_r[:, k, :], start=(k == 0),
                                         stop=(k == KT - 1))
                    last.then_inc(logits_ready, 1)

                for t in range(NT + 2):
                    if t < NT:
                        if t >= 2:
                            pe.wait_ge(x1_ready, t - 1)
                        for c in range(D // BANK):
                            for k in range(KT):
                                if t == 0 and k == 0:
                                    pe.wait_ge(w_loaded[c], 16)
                                last = te.matmul(prod[0:rows(t), t % 2, c * BANK:(c + 1) * BANK], g.mT[:, k, t * P:t * P + rows(t)],
                                                 w_o[:, k, c * BANK:(c + 1) * BANK], start=(k == 0), stop=(k == KT - 1))
                        last.then_inc(prod_ready, 1)
                    if t >= 2:
                        logit_tile(t - 2)
                    if 1 <= t <= NT:
                        route_tile(t - 1)

            @block.scalar
            def _(act):
                sc = nc.scalar
                chain = Chain(act, chain_a)

                def take(t):
                    act.wait_ge(turned, t + 1)
                    if t >= 2:
                        act.wait_ge(logits_ready, t - 1)
                    chain(sc.copy(turned_sb[t % 2][:, :, :], turn_ps[:, :, :]), turn_taken)

                for t in range(NT):
                    act.wait_ge(x1_ready, t + 1)
                    if t == PT:
                        act.wait_ge(tail_clear, 1)
                    chain(sc.activation(xn2[:, t, :], x1[:, t, :], ACT.Square, accum_out=ss[:, t:t + 1]), sq_ready)
                    act.wait_ge(mean_ready, t + 1)
                    chain(sc.activation(ss[:, t:t + 1], ss[:, t:t + 1], ACT.Sqrt), rstd_ready)
                    if t:
                        take(t - 1)
                take(NT - 1)

            @block.vector
            def _(dve):
                v, chain = nc.vector, Chain(dve, chain_v)
                dve.wait_ge(x_loaded, 32)
                dve.wait_ge(tail_clear, 1)
                dve.wait_ge(r_loaded, 48)
                for t in range(NT):
                    dve.wait_ge(prod_ready, t + 1)
                    n = rows(t)
                    chain(v.tensor_tensor(x1[0:n, t, :], x1[0:n, t, :], prod[0:n, t % 2, :], ALU.add), x1_ready)
                    dve.wait_ge(sq_ready, t + 1)
                    chain(v.tensor_scalar(ss[:, t:t + 1], ss[:, t:t + 1], 1.0 / D, EPS, ALU.mult, ALU.add))
                    chain(v.reciprocal(ss[:, t:t + 1], ss[:, t:t + 1]), mean_ready)
                    dve.wait_ge(rstd_ready, t + 1)
                    chain(v.scalar_tensor_tensor(xn2[:, t, :], x1[:, t, :], ss[:, t:t + 1], gain[:, :], ALU.mult, ALU.mult),
                          xn2_ready)
                dve.wait_ge(logits_ready, NT)
                chain(v.tensor_copy(logits[:, :, :], logit_ps[:, :, :]))


def route(nc, g, w, xn2, logits, gates, slots, passes, expert_of):
    OVER = BLOCKS_MAX - EXPERTS
    with ExitStack() as ctx:
        sb = lambda name, shape, dt=F32: ctx.enter_context(nc.sbuf_tensor("q_" + name, shape, dt))
        bias = sb("bias", [P, GROUPS + EXPERTS])
        counting = sb("counting_i", [P, 64], I32)
        ramp = sb("ramp", [P, 64])
        down4, down8 = sb("down4", [P, GROUPS]), sb("down8", [P, PER_GROUP])
        steps = sb("steps", [P, OVER])
        s1, s2, s3, s4 = sb("s1", [P, NT]), sb("s2", [P, NT]), sb("s3", [P, NT]), sb("s4", [P, NT])
        grp, wide4 = sb("grp", [P, NT, GROUPS]), sb("wide4", [P, NT, GROUPS])
        spread = sb("spread", [P, NT, PER_GROUP, GROUPS])
        inner, wide8 = sb("inner", [P, NT, PER_GROUP]), sb("wide8", [P, NT, PER_GROUP])
        pick = [sb(f"pick{n}", [P, NT, PER_GROUP]) for n in range(TOP_K)]
        chosen = [sb(f"chosen{n}", [P, NT, GROUPS, PER_GROUP]) for n in range(TOP_K)]
        both = sb("both", [P, NT, EXPERTS])
        run = sb("run", [P, NT + 1, EXPERTS])
        weighed = sb("weighed", [P, NT, EXPERTS])
        over, over_end, over_start = sb("over", [P, EXPERTS]), sb("over_end", [P, EXPERTS]), sb("over_start", [P, EXPERTS])
        ones_e = sb("ones_e", [P, EXPERTS])
        compared = sb("compared", [P, EXPERTS, OVER])
        rank, expert, start, times, block_of, slot_f = (sb(n, [P, TOP_K, NT]) for n in
                                                        ("rank", "expert", "start", "times", "block_of", "slot_f"))
        ge = sb("ge", [P, TOP_K * NT, OVER])
        pass_cmp, pass_sum = sb("pass_cmp", [1, OVER // 2]), sb("pass_sum", [1, 1])
        table_f = sb("table_f", [1, BLOCKS_MAX])
        counts_ps = ctx.enter_context(nc.psum_tensor("q_counts", [P, 2, BANK], F32))
        sem = lambda name: g.sem("q_" + name)
        bias_loaded, ramps_ready, exp_asked, exp_ready, both_ready, counts_ready, slots_ready, chain_v, chain_p, sent = (
            sem("bias_loaded"), sem("ramps_ready"), sem("exp_asked"), sem("exp_ready"), sem("both_ready"), sem("counts_ready"),
            sem("slots_ready"), sem("chain_v"), sem("chain_p"), sem("sent"))
        W = NT * EXPERTS

        with nc.Block() as block:
            @block.sync
            def _(sp):
                sp.dma_start(bias[:, 0:GROUPS], row(g.b_route_group[0]).to_broadcast([P, GROUPS])).then_inc(bias_loaded, 16)
                sp.dma_start(bias[:, GROUPS:], row(g.b_route_expert[0]).to_broadcast([P, EXPERTS])).then_inc(bias_loaded, 16)
                w.load_in(sp, g, 1, 1)
                w.load_down(sp, g, 1, 1)

            @block.gpsimd
            def _(pool):
                chain = Chain(pool, chain_p)
                chain(nc.gpsimd.iota(counting[:, :], pattern=[[1, 64]], base=0, channel_multiplier=0))
                chain(nc.gpsimd.tensor_copy(ramp[:, :], counting[:, :]), ramps_ready)
                pool.wait_ge(slots_ready, 1)
                for t in range(NT):
                    n = T_SAMPLE if t == PT else P
                    for s in range(TOP_K):
                        pool.indirect_dma_start(out=g.slot_x[:, :],
                                                out_offset=bass.IndirectOffsetOnAxis(ap=slots[0:n, s, t:t + 1], axis=0),
                                                in_=xn2[0:n, t, :], in_offset=None).then_inc(sent, 16)
                pool.wait_ge(sent, 16 * NT * TOP_K)

            @block.scalar
            def _(act):
                act.wait_ge(exp_asked, 1)
                nc.scalar.activation(wide4[:, :, :], wide4[:, :, :], ACT.Exp).then_inc(exp_ready, 1)
                act.wait_ge(exp_asked, 2)
                nc.scalar.activation(s3[:, :], s3[:, :], ACT.Exp).then_inc(exp_ready, 1)

            @block.tensor
            def _(pe):
                pe.wait_ge(both_ready, 1)
                flat = both[:, :, :].rearrange("p t e -> p (t e)")
                nc.tensor.matmul(counts_ps[:, 0, 0:W], g.before[:, :], flat, start=True, stop=True)
                nc.tensor.matmul(counts_ps[:, 1, 0:W], g.ones[:, :], flat, start=True, stop=True).then_inc(counts_ready, 1)

            @block.vector
            def _(dve):
                v, chain = nc.vector, Chain(dve, chain_v)
                tt, ts = v.tensor_tensor, v.tensor_scalar
                dve.wait_ge(ramps_ready, 1)
                chain(ts(down4[:, :], ramp[:, 0:GROUPS], -1.0, float(GROUPS), ALU.mult, ALU.add))
                chain(ts(down8[:, :], ramp[:, 0:PER_GROUP], -1.0, float(PER_GROUP), ALU.mult, ALU.add))
                chain(ts(steps[:, :], ramp[:, 1:OVER + 1], float(CAP), None, ALU.mult))
                chain(v.memset(ones_e[:, :], 1.0))
                dve.wait_ge(bias_loaded, 32)
                chain(tt(logits[:, :, :], logits[:, :, :], bias[:, :].unsqueeze(1).to_broadcast([P, NT, GROUPS + EXPERTS]), ALU.add))

                def first_of(out, values, top, down, n, scratch):
                    chain(tt(out, values, top.unsqueeze(2).to_broadcast([P, NT, n]), ALU.is_equal))
                    chain(tt(out, out, down.unsqueeze(1).to_broadcast([P, NT, n]), ALU.mult))
                    chain(v.tensor_reduce(scratch, out, X_AXIS, ALU.max))
                    chain(tt(out, out, scratch.unsqueeze(2).to_broadcast([P, NT, n]), ALU.is_equal))

                by_group = logits[:, :, 0:GROUPS]
                chain(v.tensor_reduce(s1[:, :], by_group, X_AXIS, ALU.max))
                chain(tt(wide4[:, :, :], by_group, s1[:, :].unsqueeze(2).to_broadcast([P, NT, GROUPS]), ALU.subtract), exp_asked)
                first_of(grp[:, :, :], by_group, s1[:, :], down4[:, :], GROUPS, s2[:, :])
                dve.wait_ge(exp_ready, 1)
                chain(v.reduce_sum(s4[:, :], wide4[:, :, :], axis=X_AXIS))
                chain(v.reciprocal(s4[:, :], s4[:, :]))

                per_expert = logits[:, :, GROUPS:].rearrange("p t (g e) -> p t e g", g=GROUPS)
                chain(tt(spread[:, :, :, :], per_expert, grp[:, :, :].unsqueeze(2).to_broadcast([P, NT, PER_GROUP, GROUPS]), ALU.mult))
                chain(v.reduce_sum(inner[:, :, :], spread[:, :, :, :], axis=X_AXIS))
                chain(v.tensor_reduce(s1[:, :], inner[:, :, :], X_AXIS, ALU.max))
                first_of(pick[0][:, :, :], inner[:, :, :], s1[:, :], down8[:, :], PER_GROUP, s2[:, :])
                chain(v.scalar_tensor_tensor(wide8[:, :, :], pick[0][:, :, :], NEG, inner[:, :, :], ALU.mult, ALU.add))
                chain(v.tensor_reduce(s3[:, :], wide8[:, :, :], X_AXIS, ALU.max))
                first_of(pick[1][:, :, :], wide8[:, :, :], s3[:, :], down8[:, :], PER_GROUP, s2[:, :])
                chain(tt(s3[:, :], s3[:, :], s1[:, :], ALU.subtract), exp_asked)
                dve.wait_ge(exp_ready, 2)
                chain(ts(s1[:, :], s3[:, :], 1.0, None, ALU.add))
                chain(v.reciprocal(s1[:, :], s1[:, :]))
                chain(tt(gates[:, 0, :], s1[:, :], s4[:, :], ALU.mult))
                chain(tt(gates[:, 1, :], gates[:, 0, :], s3[:, :], ALU.mult))

                for n in range(TOP_K):
                    for k in range(GROUPS):
                        chain(tt(chosen[n][:, :, k, :], pick[n][:, :, :],
                                 grp[:, :, k:k + 1].to_broadcast([P, NT, PER_GROUP]), ALU.mult))
                flat = [c[:, :, :, :].rearrange("p t g e -> p t (g e)") for c in chosen]
                chain(tt(both[:, :, :], flat[0], flat[1], ALU.add))
                chain(v.memset(both[T_SAMPLE:P, PT, :], 0.0), both_ready)

                dve.wait_ge(counts_ready, 1)
                local = counts_ps[:, 0, 0:W].rearrange("p (t e) -> p t e", t=NT)
                whole = counts_ps[:, 1, 0:W].rearrange("p (t e) -> p t e", t=NT)
                chain(v.memset(run[:, 0, :], 0.0))
                for t in range(NT):
                    chain(tt(run[:, t + 1, :], run[:, t, :], whole[:, t, :], ALU.add))
                chain(tt(compared[:, :, :], run[:, NT, :].unsqueeze(2).to_broadcast([P, EXPERTS, OVER]),
                         steps[:, :].unsqueeze(1).to_broadcast([P, EXPERTS, OVER]), ALU.is_gt))
                chain(v.reduce_sum(over[:, :], compared[:, :, :], axis=X_AXIS))
                chain(v.tensor_tensor_scan(over_end[:, :], ones_e[:, :], over[:, :], 0.0, ALU.mult, ALU.add))
                chain(tt(over_start[:, :], over_end[:, :], over[:, :], ALU.subtract))
                chain(tt(both[:, :, :], local, run[:, 0:NT, :], ALU.add))
                wide = lambda ap: ap.unsqueeze(1).to_broadcast([P, NT, EXPERTS])
                for n in range(TOP_K):
                    for out, of in ((rank, both[:, :, :]), (expert, wide(ramp[:, 0:EXPERTS])), (start, wide(over_start[:, :]))):
                        chain(tt(weighed[:, :, :], flat[n], of, ALU.mult))
                        chain(v.reduce_sum(out[:, n, :], weighed[:, :, :], axis=X_AXIS))
                two = lambda a: a[:, :, :].rearrange("p s t -> p (s t)")
                chain(tt(ge[:, :, :], two(rank).unsqueeze(2).to_broadcast([P, TOP_K * NT, OVER]),
                         steps[:, :].unsqueeze(1).to_broadcast([P, TOP_K * NT, OVER]), ALU.is_ge))
                chain(v.reduce_sum(two(times), ge[:, :, :], axis=X_AXIS))
                chain(tt(two(block_of), two(start), two(times), ALU.add))
                chain(tt(two(block_of), two(block_of), two(expert), ALU.subtract))
                chain(ts(two(block_of), two(block_of), float(EXPERTS - 1), None, ALU.add))
                chain(ts(two(slot_f), two(times), 1.0, None, ALU.min))
                chain(tt(two(block_of), two(block_of), two(slot_f), ALU.mult))
                chain(tt(two(block_of), two(block_of), two(expert), ALU.add))
                chain(tt(two(slot_f), two(block_of), two(times), ALU.subtract))
                chain(v.scalar_tensor_tensor(two(slot_f), two(slot_f), float(CAP), two(rank), ALU.mult, ALU.add))
                chain(v.tensor_copy(slots[:, :, :], slot_f[:, :, :]), slots_ready)

                chain(ts(pass_cmp[:, :], ramp[0:1, 0:OVER // 2], 2.0, None, ALU.mult))
                chain(tt(pass_cmp[:, :], over_end[0:1, EXPERTS - 1:EXPERTS].to_broadcast([1, OVER // 2]), pass_cmp[:, :], ALU.is_gt))
                chain(v.reduce_sum(pass_sum[:, :], pass_cmp[:, :], axis=X_AXIS))
                chain(ts(passes[:, :], pass_sum[:, :], float(EXPERTS // 2), None, ALU.add))
                chain(v.tensor_copy(table_f[:, 0:EXPERTS], ramp[0:1, 0:EXPERTS]))
                by_block = compared[0:1, :, :].rearrange("p e o -> p (e o)").rearrange("p (o e) -> p o e", e=EXPERTS)
                chain(tt(by_block, over_end[0:1, :].unsqueeze(1).to_broadcast([1, OVER, EXPERTS]),
                         ramp[0:1, 0:OVER].unsqueeze(2).to_broadcast([1, OVER, EXPERTS]), ALU.is_le))
                chain(v.reduce_sum(table_f[:, EXPERTS:], by_block, axis=X_AXIS))
                chain(ts(table_f[:, :], table_f[:, :], float(EXPERTS - 1), None, ALU.min))
                chain(v.tensor_copy(expert_of[:, :], table_f[:, :]))


class ExpertWeights:

    def __init__(self, nc, g, ctx):
        sb = lambda name, shape: ctx.enter_context(nc.sbuf_tensor("e_" + name, shape, F32))
        self.gate = [sb("gate0", [P, KT, F_EXP])]
        self.up = [sb("up0", [P, KT, F_EXP])]
        self.down = [sb("down0", [P, FT, D])]
        self.gate_loaded, self.up_loaded, self.down_loaded = ([g.sem(f"e_{n}_loaded{u}") for u in range(2)]
                                                              for n in ("gate", "up", "down"))

    def second(self, nc, ctx):
        sb = lambda name, shape: ctx.enter_context(nc.sbuf_tensor("e_" + name, shape, F32, side="right"))
        self.gate.append(sb("gate1", [P, KT, F_EXP]))
        self.up.append(sb("up1", [P, KT, F_EXP]))
        self.down.append(sb("down1", [P, FT, D]))

    def load_in(self, sp, g, u, e):
        into = lambda w: w[0, bass.ds(e, 1)].rearrange("o (k p) n -> p (o k) n", p=P)
        sp.dma_start(self.gate[u][:, :, :], into(g.w_gate_e)).then_inc(self.gate_loaded[u], 16)
        sp.dma_start(self.up[u][:, :, :], into(g.w_up_e)).then_inc(self.up_loaded[u], 16)

    def load_down(self, sp, g, u, e):
        sp.dma_start(self.down[u][:, :, :], g.w_down_e[0, bass.ds(e, 1)].rearrange("o (k p) n -> p (o k) n", p=P))\
            .then_inc(self.down_loaded[u], 16)


def experts(nc, g, w, passes, expert_of):
    with ExitStack() as ctx:
        sb = lambda name, shape, dt=F32: ctx.enter_context(nc.sbuf_tensor("e_" + name, shape, dt))
        xb = [sb(f"x{u}", [CAP, D]) for u in range(2)]
        xT = sb("xT", [P, KT, CAP])
        act_sb = sb("act", [P, FT * CAP])
        hT = sb("hT", [P, FT * CAP])
        y_sb = [sb(f"y{u}", [CAP, D]) for u in range(2)]
        xT_ps = ctx.enter_context(nc.psum_tensor("e_xT_ps", [P, 2, BANK], F32))
        gate_ps = ctx.enter_context(nc.psum_tensor("e_gate_ps", [P, BANK], F32))
        up_ps = ctx.enter_context(nc.psum_tensor("e_up_ps", [P, BANK], F32))
        y_ps = ctx.enter_context(nc.psum_tensor("e_y_ps", [CAP, D], F32))
        sem = lambda name: g.sem("e_" + name)
        x_loaded = [sem(f"x_loaded{u}") for u in range(2)]
        x_turned, xT_ready, gate_ready, up_ready, act_ready, h_ready, y_ready, y_kept = (
            sem("x_turned"), sem("xT_ready"), sem("gate_ready"), sem("up_ready"), sem("act_ready"), sem("h_ready"),
            sem("y_ready"), sem("y_kept"))
        y_stored = [sem(f"y_stored{u}") for u in range(2)]
        limits = dict(min_val=EXPERTS // 2, max_val=BLOCKS_MAX // 2)

        with nc.Block() as block:
            @block.sync
            def _(sp):
                n = sp.value_load(passes[0:1, 0:1], **limits)

                def load_x(b, u):
                    sp.dma_start(xb[u][:, :], g.slot_x[bass.ds(b * CAP, CAP), :]).then_inc(x_loaded[u], 16)

                load_x(0, 0)
                load_x(1, 1)
                with sp.Fori(0, n - 1) as i:
                    for u in range(2):
                        b = i * 2 + u
                        e = sp.value_load(expert_of[0:1, bass.ds(b + 2, 1)], min_val=0, max_val=EXPERTS - 1)
                        sp.wait_ge(x_turned, b + 2)
                        load_x(b + 2, u)
                        sp.wait_ge(up_ready, b + 1)
                        w.load_in(sp, g, u, e)
                        sp.wait_ge(y_ready, b + 1)
                        w.load_down(sp, g, u, e)
                sp.wait_ge(x_turned, n * 2)
                load_x(n * 2, 0)

            @block.tensor
            def _(pe):
                te = nc.tensor

                def turn_x(u):
                    for k in range(KT):
                        last = te.transpose(xT_ps[:, k // 4, (k % 4) * CAP:(k % 4 + 1) * CAP], xb[u][:, k * P:(k + 1) * P],
                                            g.ident[0:CAP, 0:CAP])
                    last.then_inc(x_turned, 1)

                n = pe.value_load(passes[0:1, 0:1], **limits)
                pe.sem_inc(y_kept, 1)
                pe.sem_inc(x_turned, 1)
                pe.wait_ge(x_loaded[0], 16)
                turn_x(0)
                with pe.Fori(0, n) as i:
                    for u in range(2):
                        b = i * 2 + u
                        pe.wait_ge(xT_ready, b + 1)
                        for weights, loaded, out, ready in ((w.gate, w.gate_loaded, gate_ps, gate_ready),
                                                            (w.up, w.up_loaded, up_ps, up_ready)):
                            pe.wait_ge(loaded[u], i * 16 + 16)
                            for f in range(FT):
                                for k in range(KT):
                                    last = te.matmul(out[:, f * CAP:(f + 1) * CAP], weights[u][:, k, f * P:(f + 1) * P], xT[:, k, :],
                                                     start=(k == 0), stop=(k == KT - 1))
                            last.then_inc(ready, 1)
                        pe.wait_ge(x_loaded[1 - u], i * 16 + 16 + 16 * u)
                        alone(pe, g)
                        turn_x(1 - u)
                        pe.wait_ge(h_ready, b + 1)
                        pe.wait_ge(w.down_loaded[u], i * 16 + 16)
                        pe.wait_ge(y_kept, b + 1)
                        for c in range(D // BANK):
                            for f in range(FT):
                                last = te.matmul(y_ps[:, c * BANK:(c + 1) * BANK], hT[:, f * CAP:(f + 1) * CAP],
                                                 w.down[u][:, f, c * BANK:(c + 1) * BANK], start=(f == 0), stop=(f == FT - 1))
                        last.then_inc(y_ready, 1)

            @block.scalar
            def _(act):
                n = act.value_load(passes[0:1, 0:1], **limits)
                for u in range(2):
                    act.sem_inc(y_stored[u], 16)
                with act.Fori(0, n) as i:
                    for u in range(2):
                        b = i * 2 + u
                        act.wait_ge(gate_ready, b + 1)
                        nc.scalar.activation(act_sb[:, :], gate_ps[:, 0:FT * CAP], ACT.Silu).then_inc(act_ready, 1)
                        act.wait_ge(y_ready, b + 1)
                        act.wait_ge(y_stored[u], i * 16 + 16)
                        nc.scalar.copy(y_sb[u][:, :], y_ps[:, :]).then_inc(y_kept, 1)
                        act.wait_ge(y_kept, b + 2)
                        act.dma_start(g.slot_y[bass.ds(b * CAP, CAP), :], y_sb[u][:, :]).then_inc(y_stored[u], 16)
                for u in range(2):
                    act.wait_ge(y_stored[u], n * 16 + 16)
                alone(act, g)

            @block.vector
            def _(dve):
                def take_x():
                    nc.vector.tensor_copy(xT[:, :, :].rearrange("p (a k) c -> p a (k c)", a=2), xT_ps[:, :, 0:4 * CAP])\
                        .then_inc(xT_ready, 1)

                n = dve.value_load(passes[0:1, 0:1], **limits)
                dve.wait_ge(x_turned, 2)
                take_x()
                with dve.Fori(0, n) as i:
                    for u in range(2):
                        b = i * 2 + u
                        dve.wait_ge(up_ready, b + 1)
                        dve.wait_ge(act_ready, b + 1)
                        nc.vector.tensor_tensor(hT[:, :], act_sb[:, :], up_ps[:, 0:FT * CAP], ALU.mult).then_inc(h_ready, 1)
                        dve.wait_ge(x_turned, b + 3)
                        take_x()


def combine(nc, g, x1, gates, slots):
    BUFS = 3
    with ExitStack() as ctx:
        got = [[ctx.enter_context(nc.sbuf_tensor(f"c_got{s}_{b}", [P, D], F32)) for b in range(BUFS)] for s in range(TOP_K)]
        sem = lambda name: g.sem("c_" + name)
        gathered = [sem(f"gathered{b}") for b in range(BUFS)]
        summed, chain_v, y_stored = sem("summed"), sem("chain_v"), sem("y_stored")
        rows = lambda t: T_SAMPLE if t == PT else P

        with nc.Block() as block:
            @block.gpsimd
            def _(pool):
                for t in range(NT):
                    if t >= BUFS:
                        pool.wait_ge(summed, t - BUFS + 1)
                    for s in range(TOP_K):
                        pool.indirect_dma_start(out=got[s][t % BUFS][0:rows(t), :], out_offset=None, in_=g.slot_y[:, :],
                                                in_offset=bass.IndirectOffsetOnAxis(ap=slots[0:rows(t), s, t:t + 1], axis=0))\
                            .then_inc(gathered[t % BUFS], 16)

            @block.vector
            def _(dve):
                chain = Chain(dve, chain_v)
                for t in range(NT):
                    n = rows(t)
                    dve.wait_ge(gathered[t % BUFS], 16 * TOP_K * (t // BUFS + 1))
                    for s in range(TOP_K):
                        chain(nc.vector.scalar_tensor_tensor(x1[0:n, t, :], got[s][t % BUFS][0:n, :], gates[0:n, s, t:t + 1],
                                                             x1[0:n, t, :], ALU.mult, ALU.add), summed if s else None)

            @block.sync
            def _(sp):
                for t in range(NT):
                    sp.wait_ge(summed, t + 1)
                    out = g.out_y_s[0] if t == PT else g.out_y_p[0, t * P:(t + 1) * P, :]
                    sp.dma_start(out, x1[0:rows(t), t, :]).then_inc(y_stored, 16)
                sp.wait_ge(y_stored, 16 * NT)


def back(nc, g, mixed):
    with ExitStack() as ctx:
        sb = lambda name, shape, dt=F32: ctx.enter_context(nc.sbuf_tensor(name, shape, dt))
        x1 = sb("x1", [P, NT, D])
        gates, slots = sb("gates", [P, TOP_K, NT]), sb("slots", [P, TOP_K, NT], U32)
        passes, expert_of = sb("passes", [1, 1], I32), sb("expert_of", [1, BLOCKS_MAX], I32)
        with ExitStack() as weights:
            w = ExpertWeights(nc, g, weights)
            with nc.sbuf_tensor("xn2", [P, NT, D], F32) as xn2, nc.sbuf_tensor("logits", [P, NT, GROUPS + EXPERTS], F32) as logits:
                merge(nc, g, w, x1, xn2, logits)
                mixed.close()
                w.second(nc, g.right)
                route(nc, g, w, xn2, logits, gates, slots, passes, expert_of)
            experts(nc, g, w, passes, expert_of)
        combine(nc, g, x1, gates, slots)


_INS = ["x_prompt", "x_sample", "cache_k", "cache_v", "cache_logf", "state_conv", "state_rglru", "norm1_g", "w_in",
        "conv_w", "conv_b", "w_a", "b_a", "w_x", "b_x", "lru_lambda", "b_f", "q_norm_g", "k_norm_g", "w_rnn_out",
        "w_attn_out", "w_o", "norm2_g", "w_route_group", "b_route_group", "w_route_expert", "b_route_expert",
        "w_gate_e", "w_up_e", "w_down_e"]
_OUTS = [("out_y_p", (1, T_PROMPT, D)), ("out_y_s", (1, T_SAMPLE, D)),
         ("out_k_p", (1, 1, T_PROMPT, HEADS, HD)), ("out_v_p", (1, 1, T_PROMPT, HEADS, HD)),
         ("out_lf_p", (1, 1, T_PROMPT, HEADS)), ("out_conv_p", (1, 1, CONV_W - 1, D)), ("out_h_p", (1, 1, D)),
         ("out_k_s", (1, 1, T_SAMPLE, HEADS, HD)), ("out_v_s", (1, 1, T_SAMPLE, HEADS, HD)),
         ("out_lf_s", (1, 1, T_SAMPLE, HEADS)), ("out_conv_s", (1, 1, CONV_W - 1, D)), ("out_h_s", (1, 1, D))]


class Shared:
    pass


def layer(nc, ctx, a):
    g = Shared()
    (g.x_prompt, g.x_sample, g.cache_k, g.cache_v, g.cache_logf, g.state_conv, g.state_rglru, g.norm1_g, g.w_in,
     g.conv_w, g.conv_b, g.w_a, g.b_a, g.w_x, g.b_x, g.lru_lambda, g.b_f, g.q_norm_g, g.k_norm_g, g.w_rnn_out,
     g.w_attn_out, g.w_o, g.norm2_g, g.w_route_group, g.b_route_group, g.w_route_expert, g.b_route_expert,
     g.w_gate_e, g.w_up_e, g.w_down_e) = (a[name] for name in _INS)
    (g.out_y_p, g.out_y_s, g.out_k_p, g.out_v_p, g.out_lf_p, g.out_conv_p, g.out_h_p, g.out_k_s, g.out_v_s,
     g.out_lf_s, g.out_conv_s, g.out_h_s) = (a[name] for name, _ in _OUTS)
    sb = lambda name, shape, dt=F32: ctx.enter_context(nc.sbuf_tensor(name, shape, dt))
    g.sem = lambda name: ctx.enter_context(nc.semaphore(name))
    g.slots_cleared = g.sem("slots_cleared")
    g.apart = g.sem("apart")
    g.w_in_k = g.w_in[0].rearrange("(k p) n -> p k n", p=P)
    g.slot_x = nc.dram_tensor("slot_x", [SLOTS + CAP, D], F32, kind="Internal").ap()
    g.slot_y = nc.dram_tensor("slot_y", [SLOTS, D], F32, kind="Internal").ap()
    g.neg_c_new = nc.dram_tensor("neg_c_new", [HEADS, T_ALL], F32, kind="Internal").ap()
    g.neg_c_past = nc.dram_tensor("neg_c_past", [HEADS, PAST], F32, kind="Internal").ap()
    g.ident, g.ones, g.before = sb("ident", [P, P]), sb("ones", [P, P]), sb("before", [P, P])
    g.ident_bf, g.causal = sb("ident_bf", [P, P], BF16), sb("causal", [P, P], BF16)
    g.causal_s = sb("causal_s", [P, T_SAMPLE], BF16)
    g.chan = sb("chan", [P, N_VEC * KT])
    g.decay = sb("decay", [P, KT])
    g.right, mixed = ExitStack(), ExitStack()
    g.mT = mixed.enter_context(nc.sbuf_tensor("mT", [P, KT, T_PAD], F32, side="right"))
    g.y_T = nc.dram_tensor("y_T", [KT, P, T_WIDE], F32, kind="Internal").ap()
    g.attn_T = nc.dram_tensor("attn_T", [KT, P, T_WIDE], F32, kind="Internal").ap()
    with ExitStack() as front:
        g.xh, g.xl = (front.enter_context(nc.sbuf_tensor(name, [P, KT, T_PAD], F32R)) for name in ("xh", "xl"))
        normalize(nc, g)
        with nc.sbuf_tensor("qkT", [HD + 1, 4, T_PAD], F32) as g.qkT, nc.sbuf_tensor("w_qkv", [P, KT, QKV], F32) as g.w_qkv, \
                nc.sbuf_tensor("w_qkv_hi", [P, KT, QKV], F32R) as hi, nc.sbuf_tensor("w_qkv_lo", [P, KT, QKV], F32R) as lo:
            g.w_parts = [hi, lo]
            g.w_loaded, g.w_rounded, g.w_split = g.sem("w_loaded"), g.sem("w_rounded"), g.sem("w_split")
            forget_gates(nc, g)
            attend(nc, g)
        sem = lambda name: g.sem("p_" + name)
        sems = (sem("g_loaded"), sem("p_loaded"), [sem(f"b_loaded{u}") for u in range(2)], sem("g_rounded"), sem("p_rounded"),
                sem("b_rounded"), sem("g_split"), sem("p_split"), sem("b_split"), sem("gate_ready"), sem("proj_ready"),
                sem("sig_ready"), sem("proj_taken"), sem("chain_v"))
        project(nc, g, sems, 0, g.attn_T, g.w_attn_out, COL_GATE_ATTN, False, "pa")
        recurrent(nc, g)
        project(nc, g, sems, 1, g.y_T, g.w_rnn_out, COL_GATE_RNN, True, "pr")
    with g.right:
        back(nc, g, mixed)


def kernel(**inputs):
    import numpy as np
    import concourse.bacc as bacc
    from concourse.bass_utils import run_bass_kernel_spmd

    nc = bacc.Bacc("TRN2", target_bir_lowering=False, num_devices=1)
    arrays, aps = {}, {}
    for name in _INS:
        arrays[name] = np.ascontiguousarray(inputs[name])
        aps[name] = nc.dram_tensor(name, arrays[name].shape, F32, kind="ExternalInput").ap()
    for name, shape in _OUTS:
        aps[name] = nc.dram_tensor(name, shape, F32, kind="ExternalOutput").ap()
    with ExitStack() as ctx:
        layer(nc, ctx, aps)
    r = run_bass_kernel_spmd(nc, [arrays], core_ids=[0])
    return tuple(r.results[0][name] for name, _ in _OUTS)
```
